# Optimizing a Trainium2 kernel written in Bass

```python
import jax, jax.numpy as jnp
from jax import lax
import numpy as np

D_MODEL = 1024
BATCH = 1
SEQ = 256
DEPTH = 2

HEAD_DIM = D_MODEL // 8
DILATED_CONFIGS = ((128, 1), (512, 4), (2048, 16))
N_GROUPS = len(DILATED_CONFIGS)
N_SLOT_HEADS = 4
N_ATTN_HEADS = N_GROUPS * N_SLOT_HEADS
QKV_WIDTH = 3 * N_ATTN_HEADS * HEAD_DIM
ATTN_WIDTH = N_SLOT_HEADS * HEAD_DIM
N_MEM = 256
N_MEM_HEADS = 4
MEM_WIDTH = N_MEM_HEADS * HEAD_DIM
N_FOURIER_GROUPS = 4
FOURIER_GROUP_DIM = HEAD_DIM
FOURIER_WIDTH = N_FOURIER_GROUPS * FOURIER_GROUP_DIM
MIX_WIDTH = ATTN_WIDTH + MEM_WIDTH
D_FF = ((8 * D_MODEL // 3 + 255) // 256) * 256
N_EXPERTS = 8
TOP_K = 2
D_FF_EXPERT = 7 * D_MODEL // 2
ALPHA = (2.0 * DEPTH) ** 0.25
BETA = (8.0 * DEPTH) ** -0.25
LN_EPS = 1e-5
NEG_INF = -1e30
N_EVEN = (DEPTH + 1) // 2
N_ODD = DEPTH // 2

kernel_name = "hybrid_dilated_fourier_memory_moe_encoder"

def _layer_norm(x, g, b=None):
    xf = x.astype(jnp.float32)
    xc = xf - jnp.mean(xf, axis=-1, keepdims=True)
    var = jnp.mean(xc * xc, axis=-1, keepdims=True)
    y = xc * lax.rsqrt(var + LN_EPS) * g
    if b is not None:
        y = y + b
    return y.astype(x.dtype)

def _alibi_slopes():
    exps = np.arange(1, N_ATTN_HEADS + 1, dtype=np.float32) * np.float32(8.0 / N_ATTN_HEADS)
    return jnp.asarray(np.exp2(-exps).astype(np.float32))

def _dilated_group_attention(q, k, v, dilation, n_side, slopes):
    B, H, S, hd = q.shape
    L = S // dilation
    nb = -(-L // n_side)
    Lp = nb * n_side

    def classes(t):
        return t.reshape(B, H, L, dilation, hd).transpose(0, 1, 3, 2, 4)

    pad4 = ((0, 0), (0, 0), (0, 0))
    qb = jnp.pad(classes(q), pad4 + ((0, Lp - L), (0, 0))).reshape(B, H, dilation, nb, n_side, hd)

    def windows(t):
        tp = jnp.pad(classes(t), pad4 + ((n_side, Lp - L + n_side), (0, 0)))
        tp = tp.reshape(B, H, dilation, nb + 2, n_side, hd)
        return jnp.concatenate([tp[:, :, :, :-2], tp[:, :, :, 1:-1], tp[:, :, :, 2:]], axis=4)

    kw, vw = windows(k), windows(v)
    qi = jnp.arange(n_side)
    kj = jnp.arange(3 * n_side)
    blk = jnp.arange(nb)
    delta = kj[None, :] - n_side - qi[:, None]
    key_idx = blk[:, None] * n_side - n_side + kj[None, :]
    valid = (jnp.abs(delta) <= n_side)[None] & ((key_idx >= 0) & (key_idx < L))[:, None, :]
    dist = (jnp.abs(delta) * dilation).astype(jnp.float32)
    bias = -slopes.astype(jnp.float32)[:, None, None] * dist

    s = jnp.einsum('bhrnqd,bhrnkd->bhrnqk', qb, kw).astype(jnp.float32) * (hd ** -0.5)
    s = s + bias[None, :, None, None]
    s = jnp.where(valid[None, None, None], s, NEG_INF)
    m = jnp.max(s, axis=-1, keepdims=True)
    p = jnp.exp(s - m)
    l = jnp.sum(p, axis=-1, keepdims=True)
    o = jnp.einsum('bhrnqk,bhrnkd->bhrnqd', p, vw.astype(jnp.float32)) / l
    lse = (m + jnp.log(l))[..., 0]
    o = o.reshape(B, H, dilation, Lp, hd)[:, :, :, :L].transpose(0, 1, 3, 2, 4).reshape(B, H, S, hd)
    lse = lse.reshape(B, H, dilation, Lp)[..., :L].transpose(0, 1, 3, 2).reshape(B, H, S)
    return o, lse

def _memory_attention(q_flat, mem, w_mem_kv):
    B, S, _ = q_flat.shape
    n_mem = mem.shape[1]
    q = q_flat.reshape(B, S, N_MEM_HEADS, HEAD_DIM)
    kv = (mem @ w_mem_kv).reshape(B, n_mem, 2, N_MEM_HEADS, HEAD_DIM)
    s = jnp.einsum('bshd,bmhd->bhsm', q, kv[:, :, 0]).astype(jnp.float32) * (HEAD_DIM ** -0.5)
    p = jax.nn.softmax(s, axis=-1)
    o = jnp.einsum('bhsm,bmhd->bshd', p, kv[:, :, 1].astype(jnp.float32))
    return o.reshape(B, S, MEM_WIDTH).astype(q_flat.dtype)

def _dilated_mixer(x, mem, w_in, w_mem_kv, w_out):
    B, S, _ = x.shape
    proj = x @ w_in
    qkv = proj[..., :QKV_WIDTH].reshape(B, S, 3, N_GROUPS, N_SLOT_HEADS, HEAD_DIM)
    qkv = qkv.transpose(2, 3, 0, 4, 1, 5)
    q_mem = proj[..., QKV_WIDTH:]
    slopes = _alibi_slopes().reshape(N_GROUPS, N_SLOT_HEADS)
    outs, lses = [], []
    for g, (window, dilation) in enumerate(DILATED_CONFIGS):
        o, lse = _dilated_group_attention(qkv[0, g], qkv[1, g], qkv[2, g], dilation,
                                          window // (2 * dilation), slopes[g])
        outs.append(o)
        lses.append(lse)
    weights = jax.nn.softmax(jnp.stack(lses), axis=0)
    attn = jnp.einsum('gbhs,gbhsd->bshd', weights, jnp.stack(outs))
    attn = attn.reshape(B, S, ATTN_WIDTH).astype(x.dtype)
    mix = jnp.concatenate([attn, _memory_attention(q_mem, mem, w_mem_kv)], axis=-1)
    return mix @ w_out

def _fourier_mixer(x, mem, w_in, fourier_g, w_mem_kv, w_out):
    B, S, _ = x.shape
    proj = x @ w_in
    u = proj[..., :FOURIER_WIDTH].reshape(B, S, N_FOURIER_GROUPS, FOURIER_GROUP_DIM)
    u = _layer_norm(u, fourier_g)
    f = jnp.fft.fft2(u.astype(jnp.float32), axes=(1, 3), norm='ortho').real
    f = f.reshape(B, S, FOURIER_WIDTH).astype(x.dtype)
    q_mem = proj[..., FOURIER_WIDTH:]
    mix = jnp.concatenate([f, _memory_attention(q_mem, mem, w_mem_kv)], axis=-1)
    return mix @ w_out

def _swiglu(h, w_gate, w_up, w_down):
    return (jax.nn.silu(h @ w_gate) * (h @ w_up)) @ w_down

def _moe_swiglu(h, router_w, router_b, w_gate, w_up, w_down):
    B, S, D = h.shape
    t = h.reshape(B * S, D)
    logits = (t @ router_w).astype(jnp.float32) + router_b.astype(jnp.float32)
    top_logits, top_idx = lax.top_k(logits, TOP_K)
    gates = jax.nn.softmax(top_logits, axis=-1)
    combine = jnp.einsum('tk,tke->te', gates,
                         jax.nn.one_hot(top_idx, N_EXPERTS, dtype=jnp.float32)).astype(h.dtype)
    y = jnp.zeros_like(t)
    for e in range(N_EXPERTS):
        y = y + combine[:, e:e + 1] * _swiglu(t, w_gate[e], w_up[e], w_down[e])
    return y.reshape(B, S, D)

def _normal(key, shape, fan_in, scale=1.0):
    return jax.random.normal(key, shape, jnp.float32) * (scale * fan_in ** -0.5)

def _gain(key, shape):
    return 1.0 + 0.05 * jax.random.normal(key, shape, jnp.float32)

def _bias(key, shape, scale=0.02):
    return scale * jax.random.normal(key, shape, jnp.float32)

def setup_inputs(seed: int = 0) -> dict:
    key = jax.random.key(seed)
    ks = iter(jax.random.split(key, 32))
    D = D_MODEL
    x = jax.random.normal(next(ks), (BATCH, SEQ, D), jnp.float32)
    mem = jax.random.normal(next(ks), (BATCH, N_MEM, D), jnp.float32)
    a_w_in = jnp.concatenate([
        _normal(next(ks), (N_EVEN, D, 2 * N_ATTN_HEADS * HEAD_DIM), D),
        _normal(next(ks), (N_EVEN, D, N_ATTN_HEADS * HEAD_DIM), D, BETA),
        _normal(next(ks), (N_EVEN, D, MEM_WIDTH), D),
    ], axis=-1)
    a_w_mem_kv = jnp.concatenate([
        _normal(next(ks), (N_EVEN, D, MEM_WIDTH), D),
        _normal(next(ks), (N_EVEN, D, MEM_WIDTH), D, BETA),
    ], axis=-1)
    a_w_out = _normal(next(ks), (N_EVEN, MIX_WIDTH, D), MIX_WIDTH, BETA)
    a_ln1_g = _gain(next(ks), (N_EVEN, D))
    a_ln1_b = _bias(next(ks), (N_EVEN, D))
    a_ffn_gate = _normal(next(ks), (N_EVEN, D, D_FF), D)
    a_ffn_up = _normal(next(ks), (N_EVEN, D, D_FF), D)
    a_ffn_down = _normal(next(ks), (N_EVEN, D_FF, D), D_FF, BETA)
    a_ln2_g = _gain(next(ks), (N_EVEN, D))
    a_ln2_b = _bias(next(ks), (N_EVEN, D))
    b_w_in = _normal(next(ks), (N_ODD, D, FOURIER_WIDTH + MEM_WIDTH), D)
    b_fourier_g = _gain(next(ks), (N_ODD, N_FOURIER_GROUPS, FOURIER_GROUP_DIM))
    b_w_mem_kv = jnp.concatenate([
        _normal(next(ks), (N_ODD, D, MEM_WIDTH), D),
        _normal(next(ks), (N_ODD, D, MEM_WIDTH), D, BETA),
    ], axis=-1)
    b_w_out = _normal(next(ks), (N_ODD, MIX_WIDTH, D), MIX_WIDTH, BETA)
    b_ln1_g = _gain(next(ks), (N_ODD, D))
    b_ln1_b = _bias(next(ks), (N_ODD, D))
    b_router_w = _normal(next(ks), (N_ODD, D, N_EXPERTS), D)
    b_router_b = _bias(next(ks), (N_ODD, N_EXPERTS), 0.01)
    b_moe_gate = _normal(next(ks), (N_ODD, N_EXPERTS, D, D_FF_EXPERT), D)
    b_moe_up = _normal(next(ks), (N_ODD, N_EXPERTS, D, D_FF_EXPERT), D)
    b_moe_down = _normal(next(ks), (N_ODD, N_EXPERTS, D_FF_EXPERT, D), D_FF_EXPERT, BETA)
    b_ln2_g = _gain(next(ks), (N_ODD, D))
    b_ln2_b = _bias(next(ks), (N_ODD, D))
    return {
        "x": x, "mem": mem,
        "a_w_in": a_w_in, "a_w_mem_kv": a_w_mem_kv, "a_w_out": a_w_out,
        "a_ln1_g": a_ln1_g, "a_ln1_b": a_ln1_b,
        "a_ffn_gate": a_ffn_gate, "a_ffn_up": a_ffn_up, "a_ffn_down": a_ffn_down,
        "a_ln2_g": a_ln2_g, "a_ln2_b": a_ln2_b,
        "b_w_in": b_w_in, "b_fourier_g": b_fourier_g, "b_w_mem_kv": b_w_mem_kv, "b_w_out": b_w_out,
        "b_ln1_g": b_ln1_g, "b_ln1_b": b_ln1_b,
        "b_router_w": b_router_w, "b_router_b": b_router_b,
        "b_moe_gate": b_moe_gate, "b_moe_up": b_moe_up, "b_moe_down": b_moe_down,
        "b_ln2_g": b_ln2_g, "b_ln2_b": b_ln2_b,
    }

def reference(x, mem, a_w_in, a_w_mem_kv, a_w_out, a_ln1_g, a_ln1_b, a_ffn_gate, a_ffn_up,
              a_ffn_down, a_ln2_g, a_ln2_b, b_w_in, b_fourier_g, b_w_mem_kv, b_w_out, b_ln1_g,
              b_ln1_b, b_router_w, b_router_b, b_moe_gate, b_moe_up, b_moe_down, b_ln2_g, b_ln2_b):
    for i in range(DEPTH):
        j = i // 2
        if i % 2 == 0:
            y = _dilated_mixer(x, mem, a_w_in[j], a_w_mem_kv[j], a_w_out[j])
            x = _layer_norm(ALPHA * x + y, a_ln1_g[j], a_ln1_b[j])
            y = _swiglu(x, a_ffn_gate[j], a_ffn_up[j], a_ffn_down[j])
            x = _layer_norm(ALPHA * x + y, a_ln2_g[j], a_ln2_b[j])
        else:
            y = _fourier_mixer(x, mem, b_w_in[j], b_fourier_g[j], b_w_mem_kv[j], b_w_out[j])
            x = _layer_norm(ALPHA * x + y, b_ln1_g[j], b_ln1_b[j])
            y = _moe_swiglu(x, b_router_w[j], b_router_b[j], b_moe_gate[j], b_moe_up[j], b_moe_down[j])
            x = _layer_norm(ALPHA * x + y, b_ln2_g[j], b_ln2_b[j])
    return x


_drawn_inputs = setup_inputs


def setup_inputs(seed=0):
    import zlib

    import numpy as np

    out = dict(_drawn_inputs(seed))
    spreads = {}
    factors = {'a_w_mem_kv': 2.809,
     'b_fourier_g': 4.014,
     'b_w_mem_kv': 2.755,
     'b_router_b': 3.863,
     'b_ln2_b': 2.741}
    for name, (base, spread) in spreads.items():
        noise = np.random.default_rng([zlib.crc32(name.encode()), seed]).standard_normal(out[name].shape)
        drawn = base * np.exp(spread * noise) if base else spread * noise
        out[name] = __import__('jax').numpy.asarray(drawn.astype(out[name].dtype))
    for name, factor in factors.items():
        out[name] = (out[name] * factor).astype(out[name].dtype)
    return out
```

```python
import concourse.bass as bass
from concourse import mybir
from contextlib import ExitStack


def hybrid_encoder(nc, t):
    f32, f32r, i32 = mybir.dt.float32, mybir.dt.float32r, mybir.dt.int32
    ALU, ACT, AX = mybir.AluOpType, mybir.ActivationFunctionType, mybir.AxisListType

    P = 128
    _, S, D = t["x"].shape
    TT = S // P
    KC = D // P
    NM = t["mem"].shape[1]
    HD = D // 8
    NS = 4
    NG = 3
    AW = NS * HD
    FF = t["a_ffn_gate"].shape[2]
    NE, FE = t["b_moe_gate"].shape[1], t["b_moe_gate"].shape[3]
    PW = 512
    UNIT = 2048
    SCALE = float(HD) ** -0.5
    DEPTH = 2
    ALPHA = (2.0 * DEPTH) ** 0.25
    EPS = 1e-5
    NH = NG * NS
    assert (P, TT, KC, NM, AW) == (128, 2, 8, S, PW)

    PANEL = KC * PW // UNIT
    PROJ = t["a_w_in"].shape[2] // PW
    U_MEM_A = 0
    U_MEM_B = U_MEM_A + 2 * PANEL
    U_IN_A = U_MEM_B + 2 * PANEL
    U_OUT_A = U_IN_A + PROJ * PANEL
    U_FFN = U_OUT_A + 2 * PANEL
    FULL = FF // PW
    REST = FF - FULL * PW
    assert KC * REST == UNIT
    U_FFN_DOWN = U_FFN + FULL * 2 * PANEL + 2
    FCH = FF // P
    U_IN_B = U_FFN_DOWN + FCH // 2
    U_OUT_B = U_IN_B + 2 * PANEL
    U_MOE = U_OUT_B + 2 * PANEL
    STEPS = FE // PW
    STEP_U = 6
    EXP_U = STEPS * STEP_U
    PASS_U = NE * EXP_U
    R = 6
    RD = 3
    CAP = P

    ctx = ExitStack()
    with ctx:
        base = (nc.sbuf_base + 31) // 32 * 32
        SLOT = UNIT * 4

        def at(name, shape, dt, off):
            return nc.alloc_sbuf_tensor_at(name, shape, dt, offset=base + off)

        RAW = at("RAW", [P, R, UNIT], f32, 0)
        HI = at("HI", [P, R, UNIT], f32r, R * SLOT)
        EXT = (R + RD) * SLOT
        EXT2 = EXT + RD * SLOT
        LOD = at("LOD", [P, RD, UNIT], f32r, EXT2)
        LOE = at("LOE", [P, RD, UNIT], f32r, EXT2 + RD * SLOT)
        REST0 = EXT2 + 2 * RD * SLOT
        EXTB = EXT2 + RD * SLOT
        QKT = at("QKT", [P, 2 * NH, S], f32, EXT)
        V = at("V", [P, TT, NG * AW], f32, EXTB)
        TAIL = EXTB + TT * NG * AW * 4
        STG = at("STG", [P, 2, TT, PW], f32, TAIL)
        PT = at("PT", [P, NG * TT, S], f32, TAIL)
        MASK = at("MASK", [P, TT, NG, S], f32, TAIL + 6144)
        HTH = at("HTH", [P, FCH, S], f32r, EXT)
        HTL = at("HTL", [P, FCH, S], f32r, EXTB)
        UF = at("UF", [P, TT, PW], f32, EXT)
        DFTP = at("DFTP", [P, TT, 2 * S], f32, EXT + 4096)
        DFTC = at("DFTC", [P, 2, P], f32, EXT + 8192)
        FA = at("FA", [P, 2, 2 * S], f32, EXT + 9216)
        FG = at("FG", [P, AW], f32, EXT + 13312)
        STGB = at("STGB", [P, TT, PW], f32, EXTB)
        PTB = at("PTB", [P, TT, S], f32, EXTB + 4096)

        X = at("X", [P, TT, D], f32, REST0)
        XTH = at("XTH", [P, KC, S], f32r, REST0 + 8192)
        XTL = at("XTL", [P, KC, S], f32r, REST0 + 16384)
        MIXH = at("MIXH", [P, KC, S], f32r, REST0 + 8192)
        MIXL = at("MIXL", [P, KC, S], f32r, REST0 + 16384)
        M0 = REST0 + 24576
        MEMX = at("MEMX", [P, TT, D], f32, RD * 0 + EXT)
        MTH = at("MTH", [P, KC, S], f32r, M0)
        MTL = at("MTL", [P, KC, S], f32r, M0 + 8192)
        PR = at("PR", [P, 2, TT, NG * S], f32, M0)
        LNG = at("LNG", [P, D], f32, M0)
        LNB = at("LNB", [P, D], f32, M0 + 4096)
        SIG = at("SIG", [P, TT, PW], f32, M0 + 8192)
        HB = at("HB", [P, TT, PW], f32, M0 + 12288)
        M1 = M0 + 16384
        QMT = at("QMT", [P, NS, S], f32, M1)
        KMT = [at("KMT0", [P, NS, S], f32, M1 + 4096), at("KMT1", [P, NS, S], f32, M1 + 8192)]
        VM = [at("VM0", [P, TT, PW], f32, M1 + 12288), at("VM1", [P, TT, PW], f32, M1 + 16384)]
        C0 = M1 + 20480
        IDN = at("IDN", [P, P], f32, C0)
        SM = at("SM", [P, 320], f32, C0 + 512)
        XSH = at("XSH", [P, TT, D], f32r, REST0 + 8192)
        XSL = at("XSL", [P, TT, D], f32r, REST0 + 16384)
        XEH = at("XEH", [P, KC, CAP], f32r, M0)
        XEL = at("XEL", [P, KC, CAP], f32r, M0 + 4096)
        ESIG = at("ESIG", [P, PW], f32, M0 + 8192)
        EH = at("EH", [P, PW], f32, M0 + 10240)
        EHTH = at("EHTH", [P, PW // P, CAP], f32r, M0 + 12288)
        EHTL = at("EHTL", [P, PW // P, CAP], f32r, M0 + 14336)
        YH = at("YH", [P, D], f32r, M1)
        YL = at("YL", [P, D], f32r, M1 + 4096)
        CURS = at("CURS", [P, TT, CAP], f32r, M1 + 8192)
        CURT = at("CURT", [P, TT, P], f32r, M1 + 9216)
        IOT = at("IOT", [P, P], f32, M1 + 10240)
        TRI = at("TRI", [P, 2 * P], f32, M1 + 10752)
        RTH = at("RTH", [P, KC, S], f32r, M0)
        RTL = at("RTL", [P, KC, S], f32r, M0 + 8192)
        RW = at("RW", [P, KC, NE], f32, M1)
        RWH = at("RWH", [P, KC, NE], f32r, M1 + 256)
        RWL = at("RWL", [P, KC, NE], f32r, M1 + 512)
        RB = at("RB", [P, NE], f32, M1 + 768)
        RC = at("RC", [P, TT, NE, NE], f32, M1 + 1024)
        RC2 = at("RC2", [P, TT, NE, NE], f32, M1 + 1536)
        RC3 = at("RC3", [P, TT, NE, NE], f32, M1 + 2048)
        LOWM = at("LOWM", [P, NE, NE], f32, M1 + 2560)
        RS = at("RS", [P, 8, TT, NE], f32, M1 + 2816)
        POSC = at("POSC", [P, TT, 2, NE + 1], f32, M1 + 11776)
        CURC = at("CURC", [P, TT, 2], f32, M1 + 11936)
        CNT = at("CNT", [1, 8], f32, M1 + 11968)
        NP_ = at("NP_", [1, 8], i32, M1 + 12000)
        CG = at("CG", [P, 1], f32, M1 + 12064)
        LNG4 = at("LNG4", [P, D], f32, M1 + 12288)
        LNB4 = at("LNB4", [P, D], f32, M1 + 16384)
        MX, NMX, SUM, RSUM = SM[:, 0:2], SM[:, 2:4], SM[:, 4:6], SM[:, 6:8]
        MXB, NMXB, SUMB, RSUMB = SM[:, 8:10], SM[:, 10:12], SM[:, 12:14], SM[:, 14:16]
        BN = SM[:, 16:64].rearrange("p (t s) -> p t s", t=2)
        MV = SM[:, 64:68].rearrange("p (t s) -> p t s", t=2)
        VE, RSTD = SM[:, 68:70], SM[:, 70:72]
        FBN = SM[:, 72:120].rearrange("p (g s) -> p g s", g=8)
        FMV = SM[:, 120:136].rearrange("p (g s) -> p g s", g=8)
        FVE, FRS = SM[:, 136:144], SM[:, 144:152]

        PS = ctx.enter_context(nc.psum_tensor("PS", [P, 8, PW], f32))

        def sem(name):
            return ctx.enter_context(nc.semaphore(name))

        raw_in = [sem(f"raw_in{i}") for i in range(R)]
        hi_done = sem("hi_done")
        lo_done = sem("lo_done")
        used = sem("used")
        x_in, mem_in, idn_in, mask_in = sem("x_in"), sem("mem_in"), sem("idn_in"), sem("mask_in")
        ln_in, b_in, r_in, ln4_in, out_done = sem("ln_in"), sem("b_in"), sem("r_in"), sem("ln4_in"), sem("out_done")
        tp_done = sem("tp_done")
        th_done = sem("th_done")
        tp_free = sem("tp_free")
        pan_free = sem("pan_free")
        sc_done, sc_free, mx_done, ex_done = sem("sc_done"), sem("sc_free"), sem("mx_done"), sem("ex_done")
        pn_done, ptp_done, pt_done = sem("pn_done"), sem("ptp_done"), sem("pt_done")
        o_done, oh_done, ol_done = sem("o_done"), sem("oh_done"), sem("ol_done")
        var_done, sd_done, x_done = sem("var_done"), sem("sd_done"), sem("x_done")
        sig_done, gs_done, h_done = sem("sig_done"), sem("gs_done"), sem("h_done")
        fvar_done, fsd_done, un_done = sem("fvar_done"), sem("fsd_done"), sem("un_done")
        fa_done, fac_done = sem("fa_done"), sem("fac_done")
        xs_done, rw_done, lg_done = sem("xs_done"), sem("rw_done"), sem("lg_done")
        le_done, ex8_done, sel_done, pos_done, route_done = (
            sem("le_done"), sem("ex8_done"), sem("sel_done"), sem("pos_done"), sem("route_done"))
        cur_col, cur_done, ct_done, ctt_done = sem("cur_col"), sem("cur_done"), sem("ct_done"), sem("ctt_done")
        gat_done, xeh_done, xel_done = sem("gat_done"), sem("xeh_done"), sem("xel_done")
        esig_done, egs_done, eh_done = sem("esig_done"), sem("egs_done"), sem("eh_done")
        et_done, eth_done, etl_done = sem("et_done"), sem("eth_done"), sem("etl_done")
        yh_done, yl_done, scat_done, acc_done = sem("yh_done"), sem("yl_done"), sem("scat_done"), sem("acc_done")
        fyh_done, fyl_done, fscat_done = sem("fyh_done"), sem("fyl_done"), sem("fscat_done")
        shift_done = sem("shift_done")
        v_chain = sem("v_chain")
        a_chain = sem("a_chain")

        block = ctx.enter_context(nc.Block())

        def rows(w, k0, k1, c0, cn):
            return w[k0 * P:k1 * P, bass.ds(c0, cn)].rearrange("(c p) n -> p c n", p=P)

        def panel_units(w, c0):
            return [rows(w, 4 * h, 4 * h + 4, c0, PW) for h in range(PANEL)]

        dense_units = []
        for w in (t["a_w_mem_kv"], t["b_w_mem_kv"]):
            for n in range(2):
                dense_units += panel_units(w[0], n * PW)
        for n in range(PROJ):
            dense_units += panel_units(t["a_w_in"][0], n * PW)
        for n in range(2):
            dense_units += panel_units(t["a_w_out"][0], n * PW)
        for n in range(FULL):
            dense_units += panel_units(t["a_ffn_gate"][0], n * PW) + panel_units(t["a_ffn_up"][0], n * PW)
        for w in (t["a_ffn_gate"], t["a_ffn_up"]):
            dense_units.append(rows(w[0], 0, KC, FULL * PW, REST))
        for n in range(FCH // 2):
            dense_units.append(rows(t["a_ffn_down"][0], 2 * n, 2 * n + 2, 0, D))
        for n in range(2):
            dense_units += panel_units(t["b_w_in"][0], n * PW)
        for n in range(2):
            dense_units += panel_units(t["b_w_out"][0], n * PW)
        assert len(dense_units) == U_MOE

        def expert_unit(kind, e, p, h):
            if kind == "down":
                w = t["b_moe_down"][0, e, bass.ds(p * PW + h * 2 * P, 2 * P), :]
                return w.rearrange("(c p) n -> p c n", p=P)
            w = t["b_moe_gate" if kind == "gate" else "b_moe_up"]
            return w[0, e, 4 * h * P:(4 * h + 4) * P, bass.ds(p * PW, PW)].rearrange("(c p) n -> p c n", p=P)

        GATE_UP = [("gate", 0), ("gate", 1), ("up", 0), ("up", 1)]
        DOWN = [("down", 0), ("down", 1)]

        def slot_of(o):
            return (U_MOE + o) % R, (U_MOE + o) // R + 1

        def lo_slot(s):
            return LOD[:, s] if s < RD else LOE[:, s - RD]

        F_MEM, F_X = 0, 4
        F_K = 8
        F_X1 = F_K + 2 * 9
        F_H = F_X1 + 4
        F_X2 = F_H + 2 * (FULL + 1)
        F_QB = F_X2 + 4
        F_X3 = F_QB + 2
        TH = {F_MEM: 0, F_X: 4, F_X1: 8, F_H: 12, F_X2: 12 + 2 * (FULL + 1), F_X3: 16 + 2 * (FULL + 1)}

        def fbank(f):
            return PS[:, 6 + f % 2]

        def fill_view(f, dst):
            c, w = dst.shape[1], dst.shape[2]
            return fbank(f)[:, 0:c * w].rearrange("p (c w) -> p c w", w=w)

        KPAN = {0: (0, KMT[0]), 2: (1, KMT[1])}
        for n in range(6):
            KPAN[4 + n] = (2 + n, QKT[:, NS * n:NS * n + NS])
        KPAN[13] = (8, QMT)
        PAN_OUT_A, PAN_B, PAN_OUT_B = 14, 14, 16

        JOBS = [("slot", h, h, NG) for h in range(NS)] + [("mem0", h, NS + h, 1) for h in range(NS)]
        JOBS += [("mem1", h, NS + h, 1) for h in range(NS)]
        O_FOURIER = 2 * NS

        def o_index(j):
            return j if j < O_FOURIER else j + NS

        def half_bank(half, tt):
            return half * 2 + tt

        @block.sync
        def _(sp):
            sp.dma_start(IDN[:, :], t["c_ident"]).then_inc(idn_in, 16)
            sp.dma_start(MEMX[:, :, :], t["mem"][0].rearrange("(t p) d -> p t d", p=P)).then_inc(mem_in, 16)
            sp.dma_start(X[:, :, :], t["x"][0].rearrange("(t p) d -> p t d", p=P)).then_inc(x_in, 16)
            for u, src in enumerate(dense_units):
                if u >= R:
                    sp.wait_ge(lo_done, u - R + 1)
                c = src.shape[1]
                sp.dma_start(RAW[:, u % R].rearrange("p (c n) -> p c n", c=c), src).then_inc(raw_in[u % R], 16)

            def load(ub, kind, e, p, h, o):
                sp.wait_ge(lo_done, ub + (o - R + 1))
                s, _turn = slot_of(o)
                c = 2 if kind == "down" else 4
                sp.dma_start(RAW[:, s].rearrange("p (c n) -> p c n", c=c),
                             expert_unit(kind, e, p, h)).then_inc(raw_in[s], 16)

            def experts(q):
                with sp.Fori(0, NE) as e:
                    ub = q * PASS_U + e * EXP_U + U_MOE
                    for i, (kind, h) in enumerate(GATE_UP):
                        load(ub, kind, e, 0, h, i)
                    with sp.Fori(1, STEPS) as p:
                        up = ub + (p - 1) * STEP_U
                        for i, (kind, h) in enumerate(GATE_UP):
                            load(up, kind, e, p, h, 4 + i)
                        for i, (kind, h) in enumerate(DOWN):
                            load(up, kind, e, p - 1, h, 8 + i)
                    for i, (kind, h) in enumerate(DOWN):
                        load(ub, kind, e, STEPS - 1, h, EXP_U - 2 + i)

            experts(0)
            sp.wait_ge(route_done, 1)
            n_pass = sp.value_load(NP_[0:1, 0:1], min_val=1, max_val=2)
            with sp.If(n_pass > 1):
                experts(1)
            sp.wait_ge(x_done, 8)
            sp.dma_start(t["out"][0].rearrange("(t p) d -> p t d", p=P), X[:, :, :]).then_inc(out_done, 16)
            sp.wait_ge(out_done, 16)

        @block.gpsimd
        def _(gp):
            gp.wait_ge(tp_free, F_K + 2 * 8)
            gp.dma_start(MASK[:, :, :, :], t["c_mask"]).then_inc(mask_in, 16)
            norms = [("a_ln1_g", "a_ln1_b", ol_done, 2 * NS),
                     ("a_ln2_g", "a_ln2_b", x_done, 2),
                     ("b_ln1_g", "b_ln1_b", ol_done, 4 * NS)]
            for k, (g, b, s, n) in enumerate(norms):
                gp.wait_ge(s, n)
                gp.dma_start(LNG[:, :], t[g][0].partition_broadcast(P)).then_inc(ln_in, 16)
                gp.dma_start(LNB[:, :], t[b][0].partition_broadcast(P)).then_inc(ln_in, 16)
                if k == 1:
                    gp.wait_ge(x_done, 4)
                    gp.dma_start(DFTP[:, :, :], t["c_dftp"]).then_inc(b_in, 16)
                    gp.dma_start(DFTC[:, :, :], t["c_dftc"]).then_inc(b_in, 16)
                    gp.dma_start(FG[:, :], t["b_fourier_g"][0].rearrange("g d -> (g d)").partition_broadcast(P)
                                 ).then_inc(b_in, 16)
            gp.dma_start(RW[:, :, :], t["b_router_w"][0].rearrange("(c p) e -> p c e", p=P)).then_inc(r_in, 16)
            gp.dma_start(RB[:, :], t["b_router_b"][0].partition_broadcast(P)).then_inc(r_in, 16)
            gp.dma_start(LOWM[:, :, :], t["c_low"]).then_inc(r_in, 16)
            gp.dma_start(IOT[:, :], t["c_iota"]).then_inc(r_in, 16)
            gp.dma_start(TRI[:, :], t["c_tri"]).then_inc(r_in, 16)
            gp.dma_start(LNG4[:, :], t["b_ln2_g"][0].partition_broadcast(P)).then_inc(ln4_in, 16)
            gp.dma_start(LNB4[:, :], t["b_ln2_b"][0].partition_broadcast(P)).then_inc(ln4_in, 16)

        @block.scalar
        def _(act):
            def hi(u):
                act.wait_ge(raw_in[u % R], 16 * (u // R + 1))
                if u >= RD:
                    act.wait_ge(used, u - RD + 1)
                nc.scalar.activation(HI[:, u % RD], RAW[:, u % R], ACT.Copy).then_inc(hi_done, 1)

            def hi_fill(f, dst):
                act.wait_ge(tp_done, f + 1)
                nc.scalar.activation(dst, fill_view(f, dst), ACT.Copy).then_inc(th_done, 1)

            def hi_fills(f0, dst):
                for j in range(2 * TT):
                    tt, k = divmod(j, 2)
                    hi_fill(f0 + j, dst[:, 4 * k:4 * k + 4, tt * P:(tt + 1) * P])

            def panel_out(n, dst, lo_bank):
                u = 2 * n if n < PAN_B else U_IN_B + 2 * (n - PAN_B)
                act.wait_ge(used, u + PANEL)
                if n in KPAN and KPAN[n][0] >= 2:
                    act.wait_ge(tp_done, F_K + 2 * (KPAN[n][0] - 1))
                nc.scalar.activation(dst, PS[:, lo_bank:lo_bank + 2], ACT.Copy).then_inc(pan_free, 1)

            def attention(jobs):
                def exps(j):
                    act.wait_ge(mx_done, j + 1)
                    b, w = j % 2, JOBS[j][3] * S
                    nmx, total = (NMX, SUM) if b == 0 else (NMXB, SUMB)
                    for tt in range(TT):
                        nc.scalar.activation(PR[:, b, tt, 0:w], PR[:, b, tt, 0:w], ACT.Exp, bias=nmx[:, tt:tt + 1],
                                             scale=SCALE, accum_out=total[:, tt:tt + 1]).then_inc(ex_done, 1)

                def probs_t(j):
                    act.wait_ge(ptp_done, j + 1)
                    if j > 0:
                        act.wait_ge(o_done, o_index(j - 1) + 1)
                    g = JOBS[j][3]
                    dst = PTB if j >= O_FOURIER else PT
                    nc.scalar.activation(dst[:, 0:g * TT, :].rearrange("p a s -> p (a s)"),
                                         PS[:, 3:6].rearrange("p b n -> p (b n)")[:, 0:g * TT * S],
                                         ACT.Copy).then_inc(pt_done, 1)

                exps(jobs[0])
                for j in jobs:
                    probs_t(j)
                    if j + 1 in jobs:
                        exps(j + 1)
                    mix_hi(o_index(j), JOBS[j][2])

            def mix_hi(i, chunk):
                act.wait_ge(o_done, i + 1)
                nc.scalar.activation(MIXH[:, chunk, :], PS[:, 6 + i % 2, 0:S], ACT.Copy).then_inc(oh_done, 1)

            def deviations(k):
                act.wait_ge(var_done, k + 1)
                nc.scalar.activation(RSTD, VE, ACT.Sqrt).then_inc(sd_done, 1)

            hi_fills(F_MEM, MTH)
            for u in range(RD):
                hi(u)
            hi_fills(F_X, XTH)
            for n in range(PAN_B):
                hi(2 * n + 3)
                hi(2 * n + 4)
                if n in KPAN:
                    panel_out(n, STG[:, KPAN[n][0] % 2], 2 * (n % 2))
                elif n in (1, 3):
                    panel_out(n, VM[n // 2][:, :, :], 2 * (n % 2))
                else:
                    panel_out(n, V[:, :, (n - 10) * PW:(n - 9) * PW], 2 * (n % 2))
            attention(range(0, 2 * NS))
            for u in range(U_OUT_A + RD, U_FFN + RD):
                hi(u)
            deviations(0)
            hi_fills(F_X1, XTH)
            def sigmoids(p, w):
                act.wait_ge(used, U_FFN + 4 * p + (2 if p < FULL else 1))
                if p > 0:
                    act.wait_ge(h_done, p)
                for tt in range(TT):
                    nc.scalar.activation(SIG[:, tt, 0:w], PS[:, tt, 0:w], ACT.Sigmoid).then_inc(sig_done, 1)

            def hidden_hi(p, c):
                for tt in range(TT):
                    hi_fill(F_H + 2 * p + tt, HTH[:, 4 * p:4 * p + c, tt * P:(tt + 1) * P])

            for p in range(FULL):
                for u in range(U_FFN + 4 * p + 3, U_FFN + 4 * p + 5):
                    hi(u)
                sigmoids(p, PW)
                if p > 0:
                    hidden_hi(p - 1, 4)
                for u in range(U_FFN + 4 * p + 5, U_FFN + 4 * p + 7):
                    hi(u)
            hi(U_FFN + 4 * FULL + 3)
            sigmoids(FULL, REST)
            hidden_hi(FULL - 1, 4)
            hi(U_FFN_DOWN + 2)
            hi(U_FFN_DOWN + 3)
            hidden_hi(FULL, 2)
            for u in range(U_FFN_DOWN + 4, U_IN_B + RD):
                hi(u)
            deviations(1)
            hi_fills(F_X2, XTH)
            for u in (U_IN_B + 3, U_IN_B + 4):
                hi(u)
            panel_out(PAN_B, UF[:, :, :], 0)
            hi(U_IN_B + 5)
            act.wait_ge(fvar_done, 1)
            nc.scalar.activation(FRS, FVE, ACT.Sqrt).then_inc(fsd_done, 1)
            hi(U_IN_B + 6)
            panel_out(PAN_B + 1, STGB[:, :, :], 2)
            for g in range(NS):
                act.wait_ge(fa_done, g + 1)
                if g >= 2:
                    act.wait_ge(o_done, O_FOURIER + g - 1)
                nc.scalar.activation(FA[:, g % 2], PS[:, g], ACT.Copy).then_inc(fac_done, 1)
                if g >= 1:
                    mix_hi(O_FOURIER + g - 1, g - 1)
            mix_hi(O_FOURIER + NS - 1, NS - 1)
            attention(range(2 * NS, 3 * NS))
            hi(U_MOE - 1)
            deviations(2)
            act.wait_ge(x_done, 6)
            nc.scalar.activation(XSH[:, :, :], X[:, :, :], ACT.Copy).then_inc(xs_done, 1)
            hi_fills(F_X3, RTH)
            act.wait_ge(r_in, 80)
            nc.scalar.activation(RWH[:, :, :], RW[:, :, :], ACT.Copy).then_inc(rw_done, 1)
            act.wait_ge(le_done, 1)
            nc.scalar.activation(RS[:, 3], RS[:, 3], ACT.Exp).then_inc(ex8_done, 1)

            def hi_expert(ub, turns, o):
                s, turn = slot_of(o)
                act.wait_ge(raw_in[s], (turns + turn) * 16)
                act.wait_ge(used, ub + (o - R + 1))
                nc.scalar.activation(HI[:, s], RAW[:, s], ACT.Copy).then_inc(hi_done, 1)

            def gathered_hi(gb):
                for k in range(2):
                    act.wait_ge(gat_done, gb + k + 1)
                    nc.scalar.activation(XEH[:, 4 * k:4 * k + 4, :].rearrange("p c s -> p (c s)"), PS[:, 5 + k],
                                         ACT.Copy).then_inc(xeh_done, 1)

            def y_hi(done):
                for half in range(2):
                    nc.scalar.activation(YH[:, half * PW:(half + 1) * PW], PS[:, 2 + half], ACT.Copy,
                                         scale=CG[:, 0:1]).then_inc(done, 1)

            def experts(q):
                gathered_hi(q * 36)
                with act.Fori(0, NE) as e:
                    ub = q * PASS_U + e * EXP_U + U_MOE
                    te = q * (PASS_U // R) + e * (EXP_U // R)
                    st = q * NE * STEPS + e * STEPS

                    def sigmoid(u, step, o):
                        act.wait_ge(used, u + (o + 1))
                        nc.scalar.activation(ESIG[:, :], PS[:, 0], ACT.Sigmoid).then_inc(esig_done, 1)

                    def hidden_hi_e(step):
                        act.wait_ge(et_done, step + 1)
                        nc.scalar.activation(EHTH[:, :, :].rearrange("p c s -> p (c s)"), PS[:, 4],
                                             ACT.Copy).then_inc(eth_done, 1)

                    hi_expert(ub, te, 0)
                    hi_expert(ub, te, 1)
                    act.wait_ge(used, ub)
                    y_hi(yh_done)
                    hi_expert(ub, te, 2)
                    hi_expert(ub, te, 3)
                    hi_expert(ub, te, 4)
                    sigmoid(ub, st, 1)
                    for o in (5, 6, 7, 8):
                        hi_expert(ub, te, o)
                    hidden_hi_e(st)
                    sigmoid(ub, st + 1, 5)
                    act.wait_ge(ct_done, q * NE + e + 1)
                    nc.scalar.activation(CURT[:, :, :].rearrange("p t s -> p (t s)"), PS[:, 5, 0:2 * P],
                                         ACT.Copy).then_inc(ctt_done, 1)
                    nc.scalar.activation(CG[:, :], PS[:, 5, 2 * P:2 * P + 1], ACT.Copy).then_inc(ctt_done, 1)
                    hi_expert(ub, te, 9)
                    with act.Fori(2, STEPS) as p:
                        up, tp = ub + (p - 1) * STEP_U, te + (p - 1)
                        for o in (4, 5, 6, 7, 8):
                            hi_expert(up, tp, o)
                        hidden_hi_e(st + p - 1)
                        sigmoid(up, st + p, 5)
                        hi_expert(up, tp, 9)
                    hi_expert(ub, te, EXP_U - 2)
                    hi_expert(ub, te, EXP_U - 1)
                    hidden_hi_e(st + STEPS - 1)
                    gathered_hi(e * 4 + (q * 36 + 4))

            experts(0)
            act.wait_ge(route_done, 1)
            n_pass = act.value_load(NP_[0:1, 0:1], min_val=1, max_val=2)
            with act.If(n_pass > 1):
                experts(1)
            act.wait_ge(used, n_pass * PASS_U + U_MOE)
            act.wait_ge(ctt_done, n_pass * (2 * NE))
            y_hi(fyh_done)
            deviations(3)

        @block.vector
        def _(dve):
            chain = [0]

            def link(ins):
                chain[0] += 1
                ins.then_inc(v_chain, 1)
                dve.wait_ge(v_chain, chain[0])

            def lo(u):
                dve.wait_ge(hi_done, u + 1)
                nc.vector.tensor_tensor(LOD[:, u % RD], RAW[:, u % R], HI[:, u % RD].bitcast(f32),
                                        ALU.subtract).then_inc(lo_done, 1)

            def lo_fills(f0, hi_t, lo_t, k0=0, c=4, n=2 * TT):
                for j in range(n):
                    tt, k = divmod(j, 2) if n == 2 * TT else (j, k0)
                    f = f0 + j
                    s0 = next(b for b in sorted(TH, reverse=True) if b <= f)
                    sl = (slice(None), slice(4 * k, 4 * k + c), slice(tt * P, (tt + 1) * P))
                    dve.wait_ge(th_done, TH[s0] + f - s0 + 1)
                    nc.vector.tensor_tensor(lo_t[sl], fill_view(f, lo_t[sl]), hi_t[sl].bitcast(f32),
                                            ALU.subtract).then_inc(tp_free, 1)

            def transposed_panel(f0, dst):
                for b in range(2):
                    dve.wait_ge(tp_done, f0 + b + 1)
                    d = dst[:, 2 * b:2 * b + 2, :]
                    nc.vector.tensor_copy(d, fill_view(f0 + b, d)).then_inc(tp_free, 1)

            def attention(jobs):
                def scores(j):
                    kind, h, _, g = JOBS[j]
                    b = j % 2
                    flat = PS[:, 0:3].rearrange("p b n -> p (b n)")
                    dve.wait_ge(sc_done, j + 1)
                    if j >= 2:
                        dve.wait_ge(ptp_done, j - 1)
                    if kind == "slot":
                        if j == 0:
                            dve.wait_ge(mask_in, 16)
                        for i in range(NG):
                            slope = 2.0 ** (-(i * NS + h + 1) * 8.0 / NH)
                            ins = nc.vector.scalar_tensor_tensor(
                                out=PR[:, b, :, i * S:(i + 1) * S], in0=MASK[:, :, i, :], scalar=slope / SCALE,
                                in1=flat.rearrange("p (t g s) -> p t g s", t=TT, g=NG)[:, :, i, :],
                                op0=ALU.mult, op1=ALU.add)
                            link(ins) if i < NG - 1 else ins.then_inc(sc_free, 1)
                    else:
                        nc.vector.tensor_copy(PR[:, b, :, 0:S], flat[:, 0:TT * S].rearrange("p (t s) -> p t s", t=TT)
                                              ).then_inc(sc_free, 1)

                def maxima(j):
                    b, w = j % 2, JOBS[j][3] * S
                    mx, nmx = (MX, NMX) if b == 0 else (MXB, NMXB)
                    dve.wait_ge(sc_free, j + 1)
                    link(nc.vector.tensor_reduce(mx, PR[:, b, :, 0:w], AX.X, ALU.max))
                    nc.vector.tensor_scalar(nmx, mx, -SCALE, None, ALU.mult).then_inc(mx_done, 1)

                def normalise(j):
                    b, w = j % 2, JOBS[j][3] * S
                    total, r = (SUM, RSUM) if b == 0 else (SUMB, RSUMB)
                    dve.wait_ge(ex_done, TT * (j + 1))
                    link(nc.vector.reciprocal(r, total))
                    for tt in range(TT):
                        nc.vector.tensor_scalar(PR[:, b, tt, 0:w], PR[:, b, tt, 0:w], r[:, tt:tt + 1], None,
                                                ALU.mult).then_inc(pn_done, 1)

                scores(jobs[0])
                maxima(jobs[0])
                for j in jobs:
                    if j + 1 in jobs:
                        scores(j + 1)
                    normalise(j)
                    if j + 1 in jobs:
                        maxima(j + 1)
                    if j - 1 in jobs:
                        mix_lo(o_index(j - 1), JOBS[j - 1][2])
                mix_lo(o_index(jobs[-1]), JOBS[jobs[-1]][2])

            def mix_lo(i, chunk):
                dve.wait_ge(oh_done, i + 1)
                nc.vector.tensor_tensor(MIXL[:, chunk, :], PS[:, 6 + i % 2, 0:S], MIXH[:, chunk, :].bitcast(f32),
                                        ALU.subtract).then_inc(ol_done, 1)

            def residual(u_half):
                for half in range(2):
                    dve.wait_ge(used, u_half[half])
                    for tt in range(TT):
                        x = X[:, tt, half * PW:(half + 1) * PW]
                        link(nc.vector.scalar_tensor_tensor(out=x, in0=x, scalar=ALPHA,
                                                            in1=PS[:, half_bank(half, tt)],
                                                            op0=ALU.mult, op1=ALU.add))

            def norm(k, gain, bias):
                for tt in range(TT):
                    for half in range(2):
                        link(nc.vector.bn_stats(BN[:, tt, 6 * half:6 * half + 6],
                                                X[:, tt, half * PW:(half + 1) * PW]))
                    link(nc.vector.bn_aggr(MV[:, tt, :], BN[:, tt, 0:12]))
                nc.vector.tensor_scalar(VE, MV[:, :, 1], EPS, None, ALU.add).then_inc(var_done, 1)
                dve.wait_ge(sd_done, k + 1)
                link(nc.vector.reciprocal(RSTD, RSTD))
                dve.wait_ge(*((ln_in, 32 * (k + 1)) if k < 3 else (ln4_in, 32)))
                for tt in range(TT):
                    link(nc.vector.scalar_tensor_tensor(out=X[:, tt, :], in0=X[:, tt, :], scalar=MV[:, tt, 0:1],
                                                        in1=gain[:, :], op0=ALU.subtract, op1=ALU.mult))
                    nc.vector.scalar_tensor_tensor(out=X[:, tt, :], in0=X[:, tt, :], scalar=RSTD[:, tt:tt + 1],
                                                   in1=bias[:, :], op0=ALU.mult, op1=ALU.add).then_inc(x_done, 1)

            lo_fills(F_MEM, MTH, MTL)
            for u in range(RD):
                lo(u)
            lo_fills(F_X, XTH, XTL)
            for n in range(PAN_B):
                if n > 0 and n - 1 in KPAN:
                    lo(2 * n + 3)
                    lo(2 * n + 4)
                    transposed_panel(F_K + 2 * KPAN[n - 1][0], KPAN[n - 1][1])
                else:
                    lo(2 * n + 3)
                    lo(2 * n + 4)
            transposed_panel(F_K + 2 * KPAN[PAN_B - 1][0], KPAN[PAN_B - 1][1])
            attention(range(0, 2 * NS))
            for u in range(U_OUT_A + RD, U_FFN + RD):
                lo(u)
            residual((U_OUT_A + 2, U_OUT_A + 4))
            norm(0, LNG, LNB)
            lo_fills(F_X1, XTH, XTL)

            def gated(p, w):
                dve.wait_ge(sig_done, TT * (p + 1))
                nc.vector.tensor_tensor(SIG[:, :, 0:w], PS[:, 0:2, 0:w], SIG[:, :, 0:w], ALU.mult).then_inc(gs_done, 1)

            def hidden(p, w):
                dve.wait_ge(used, U_FFN + 4 * p + (4 if p < FULL else 2))
                dve.wait_ge(gs_done, p + 1)
                if p > 0:
                    dve.wait_ge(tp_done, F_H + 2 * p)
                nc.vector.tensor_tensor(HB[:, :, 0:w], PS[:, 2:4, 0:w], SIG[:, :, 0:w], ALU.mult).then_inc(h_done, 1)

            def hidden_lo(p, c):
                lo_fills(F_H + 2 * p, HTH, HTL, k0=p, c=c, n=TT)

            for p in range(FULL):
                lo(U_FFN + 4 * p + 3)
                lo(U_FFN + 4 * p + 4)
                gated(p, PW)
                if p > 0:
                    hidden_lo(p - 1, 4)
                lo(U_FFN + 4 * p + 5)
                lo(U_FFN + 4 * p + 6)
                hidden(p, PW)
            lo(U_FFN_DOWN + 1)
            gated(FULL, REST)
            hidden_lo(FULL - 1, 4)
            hidden(FULL, REST)
            lo(U_FFN_DOWN + 2)
            lo(U_FFN_DOWN + 3)
            hidden_lo(FULL, 2)
            for u in range(U_FFN_DOWN + 4, U_IN_B + RD):
                lo(u)
            residual((U_IN_B, U_IN_B))
            norm(1, LNG, LNB)
            lo_fills(F_X2, XTH, XTL)
            lo(U_IN_B + 3)
            lo(U_IN_B + 4)
            uv = UF[:, :, :].rearrange("p t (g c) -> p (t g) c", c=HD)
            dve.wait_ge(pan_free, PAN_B + 1)
            for i in range(TT * NS):
                link(nc.vector.bn_stats(FBN[:, i, :], uv[:, i, :]))
                link(nc.vector.bn_aggr(FMV[:, i, :], FBN[:, i, :]))
            nc.vector.tensor_scalar(FVE, FMV[:, :, 1], EPS, None, ALU.add).then_inc(fvar_done, 1)
            lo(U_IN_B + 5)
            dve.wait_ge(fsd_done, 1)
            link(nc.vector.reciprocal(FRS, FRS))
            for i in range(TT * NS):
                link(nc.vector.tensor_scalar(uv[:, i, :], uv[:, i, :], FMV[:, i, 0:1], FRS[:, i:i + 1],
                                             ALU.subtract, ALU.mult))
            dve.wait_ge(b_in, 48)
            for tt in range(TT):
                nc.vector.tensor_tensor(UF[:, tt, :], UF[:, tt, :], FG[:, :], ALU.mult).then_inc(un_done, 1)
            lo(U_IN_B + 6)
            transposed_panel(F_QB, QMT)
            for g in range(NS):
                mix_lo(O_FOURIER + g, g)
            attention(range(2 * NS, 3 * NS))
            lo(U_MOE - 1)
            residual((U_OUT_B + 2, U_OUT_B + 4))
            norm(2, LNG, LNB)

            dve.wait_ge(xs_done, 1)
            nc.vector.tensor_tensor(XSL[:, :, :], X[:, :, :], XSH[:, :, :].bitcast(f32), ALU.subtract).then_inc(xs_done, 1)
            lo_fills(F_X3, RTH, RTL)
            dve.wait_ge(rw_done, 1)
            nc.vector.tensor_tensor(RWL[:, :, :], RW[:, :, :], RWH[:, :, :].bitcast(f32), ALU.subtract).then_inc(rw_done, 1)
            dve.wait_ge(tp_done, F_X3 + 4)
            dve.wait_ge(xs_done, 2)
            link(nc.vector.tensor_scalar(X[:, :, :], X[:, :, :], ALPHA, None, ALU.mult))
            link(nc.vector.memset(POSC[:, :, 0, :], -1.0))
            link(nc.vector.memset(POSC[:, :, 1, :], 0.0))
            link(nc.vector.memset(CG[:, :], 0.0))
            link(nc.vector.memset(CURT[:, :, :].bitcast(f32), 0.0))
            logit, rank, sel, ex, top = (RS[:, i] for i in (0, 1, 2, 3, 4))
            dve.wait_ge(lg_done, 1)
            link(nc.vector.tensor_tensor(logit, PS[:, 0, 0:TT * NE].rearrange("p (t e) -> p t e", t=TT),
                                         RB[:, :].unsqueeze(1).to_broadcast([P, TT, NE]), ALU.add))
            for tt in range(TT):
                this = logit[:, tt, :].unsqueeze(2).to_broadcast([P, NE, NE])
                other = logit[:, tt, :].unsqueeze(1).to_broadcast([P, NE, NE])
                link(nc.vector.tensor_tensor(RC[:, tt], other, this, ALU.is_gt))
                link(nc.vector.tensor_tensor(RC2[:, tt], other, this, ALU.is_equal))
                link(nc.vector.tensor_tensor(RC3[:, tt], RC2[:, tt], LOWM[:, :, :], ALU.mult))
                link(nc.vector.tensor_tensor(RC[:, tt], RC[:, tt], RC3[:, tt], ALU.add))
            link(nc.vector.tensor_reduce(rank, RC[:, :, :, :], AX.X, ALU.add))
            link(nc.vector.tensor_reduce(top[:, :, 0], logit, AX.X, ALU.max))
            link(nc.vector.tensor_tensor(ex, logit, top[:, :, 0:1].to_broadcast([P, TT, NE]), ALU.subtract))
            nc.vector.tensor_scalar(sel, rank, 1.5, None, ALU.is_lt).then_inc(le_done, 1)
            dve.wait_ge(ex8_done, 1)
            dve.wait_ge(le_done, 1)
            link(nc.vector.tensor_tensor(ex, ex, sel, ALU.mult))
            link(nc.vector.tensor_reduce(top[:, :, 1], ex, AX.X, ALU.add))
            link(nc.vector.reciprocal(top[:, :, 2], top[:, :, 1]))
            link(nc.vector.tensor_tensor(POSC[:, :, 1, 0:NE], ex, top[:, :, 2:3].to_broadcast([P, TT, NE]), ALU.mult))
            dve.wait_ge(pos_done, 1)
            link(nc.vector.scalar_tensor_tensor(out=rank, in0=PS[:, 1, 0:TT * NE].rearrange("p (t e) -> p t e", t=TT),
                                                scalar=1.0, in1=sel, op0=ALU.add, op1=ALU.mult))
            link(nc.vector.tensor_scalar(POSC[:, :, 0, 0:NE], rank, -1.0, None, ALU.add))
            link(nc.vector.tensor_reduce(CNT[0:1, 0:1], PS[0:1, 1, TT * NE:TT * NE + NE], AX.X, ALU.max))
            nc.vector.tensor_scalar(NP_[0:1, 0:1], CNT[0:1, 0:1], CAP + 0.5, 1.0, ALU.is_gt, ALU.add
                                    ).then_inc(route_done, 1)

            def slot_map(e, n):
                nc.vector.tensor_copy(CURC[:, :, :], POSC[:, :, :, bass.ds(e, 1)].rearrange("p t k o -> p t (k o)")
                                      ).then_inc(cur_col, 1)
                dve.wait_ge(cur_col, n + 1)
                for tt in range(TT):
                    nc.vector.tensor_scalar(CURS[:, tt, :], IOT[:, :], CURC[:, tt, 0:1], None,
                                            ALU.is_equal).then_inc(cur_done, 1)

            def lo_expert(ub, o):
                s, _turn = slot_of(o)
                dve.wait_ge(hi_done, ub + (o + 1))
                nc.vector.tensor_tensor(lo_slot(s), RAW[:, s], HI[:, s].bitcast(f32), ALU.subtract).then_inc(lo_done, 1)

            def gathered_lo(gb):
                for k in range(2):
                    dve.wait_ge(gat_done, gb + (k + 3))
                    nc.vector.tensor_copy(XEL[:, 4 * k:4 * k + 4, :].rearrange("p c s -> p (c s)"),
                                          PS[:, 7 if k == 0 else 4]).then_inc(xel_done, 1)

            def y_lo(hi_sem, n, done):
                for half in range(2):
                    cols = slice(half * PW, (half + 1) * PW)
                    dve.wait_ge(hi_sem, n + (half + 1))
                    nc.vector.scalar_tensor_tensor(out=YL[:, cols], in0=PS[:, 2 + half], scalar=CG[:, 0:1],
                                                   in1=YH[:, cols].bitcast(f32), op0=ALU.mult,
                                                   op1=ALU.subtract).then_inc(done, 1)

            def send_back(scat, n, done):
                for i in range(4):
                    tt, half = divmod(i, 2)
                    x = X[:, tt, half * PW:(half + 1) * PW]
                    dve.wait_ge(scat, n + (i + 1))
                    nc.vector.tensor_tensor(x, x, PS[:, 4 + i], ALU.add).then_inc(done, 1)

            def experts(q):
                if q == 1:
                    dve.wait_ge(gat_done, 36)
                    nc.vector.tensor_scalar(POSC[:, :, 0, :], POSC[:, :, 0, :], -float(CAP), None,
                                            ALU.add).then_inc(shift_done, 1)
                    dve.wait_ge(shift_done, 1)
                slot_map(0, q * (NE + 1))
                gathered_lo(q * 36)
                with dve.Fori(0, NE) as e:
                    ub = q * PASS_U + e * EXP_U + U_MOE
                    st = q * NE * STEPS + e * STEPS
                    tn = q * NE + e

                    def gated_e(step):
                        dve.wait_ge(esig_done, step + 1)
                        nc.vector.tensor_tensor(ESIG[:, :], PS[:, 0], ESIG[:, :], ALU.mult).then_inc(egs_done, 1)

                    def hidden_e(u, step, o):
                        dve.wait_ge(used, u + (o + 1))
                        dve.wait_ge(egs_done, step + 1)
                        nc.vector.tensor_tensor(EH[:, :], PS[:, 1], ESIG[:, :], ALU.mult).then_inc(eh_done, 1)

                    def hidden_lo_e(step):
                        dve.wait_ge(eth_done, step + 1)
                        nc.vector.tensor_tensor(EHTL[:, :, :].rearrange("p c s -> p (c s)"), PS[:, 4],
                                                EHTH[:, :, :].rearrange("p c s -> p (c s)").bitcast(f32),
                                                ALU.subtract).then_inc(etl_done, 1)

                    lo_expert(ub, 0)
                    lo_expert(ub, 1)
                    y_lo(yh_done, tn * 2, yl_done)
                    lo_expert(ub, 2)
                    lo_expert(ub, 3)
                    lo_expert(ub, 4)
                    gated_e(st)
                    lo_expert(ub, 5)
                    send_back(scat_done, tn * 4, acc_done)
                    lo_expert(ub, 6)
                    hidden_e(ub, st, 3)
                    lo_expert(ub, 7)
                    lo_expert(ub, 8)
                    hidden_lo_e(st)
                    gated_e(st + 1)
                    dve.wait_ge(ct_done, tn + 1)
                    slot_map(e + 1, tn + (q + 1))
                    lo_expert(ub, 9)
                    with dve.Fori(2, STEPS) as p:
                        up = ub + (p - 1) * STEP_U
                        lo_expert(up, 4)
                        hidden_e(up, st + p - 1, 4 - STEP_U + 3)
                        for o in (5, 6, 7, 8):
                            lo_expert(up, o)
                        hidden_lo_e(st + p - 1)
                        gated_e(st + p)
                        lo_expert(up, 9)
                    lo_expert(ub, EXP_U - 2)
                    hidden_e(ub, st + STEPS - 1, EXP_U - 5)
                    lo_expert(ub, EXP_U - 1)
                    hidden_lo_e(st + STEPS - 1)
                    gathered_lo(e * 4 + (q * 36 + 4))

            experts(0)
            dve.wait_ge(route_done, 1)
            n_pass = dve.value_load(NP_[0:1, 0:1], min_val=1, max_val=2)
            with dve.If(n_pass > 1):
                experts(1)
            y_lo(fyh_done, 0, fyl_done)
            dve.wait_ge(acc_done, n_pass * (4 * NE))
            send_back(fscat_done, 0, v_chain)
            chain[0] += 4
            dve.wait_ge(v_chain, chain[0])
            norm(3, LNG4, LNB4)

        @block.tensor
        def _(pe):
            def three(out, xh, xl, wh, wl, first, last):
                nc.tensor.matmul(out, xh, wh, start=first, stop=False)
                nc.tensor.matmul(out, xh, wl, start=False, stop=False)
                return nc.tensor.matmul(out, xl, wh, start=False, stop=last)

            def fills(f0, src, n=2 * TT):
                for j in range(n):
                    tt, k = divmod(j, 2)
                    fill(f0 + j, [src[:, tt, (4 * k + i) * P:(4 * k + i + 1) * P] for i in range(4)])

            def fill(f, blocks):
                if f >= 2:
                    pe.wait_ge(tp_free, f - 1)
                for i, blk in enumerate(blocks):
                    last = nc.tensor.transpose(fbank(f)[:, i * P:(i + 1) * P], blk, IDN[:, :])
                last.then_inc(tp_done, 1)

            def panel_fills(f0, stg):
                for b in range(2):
                    fill(f0 + b, [stg[:, tt, h * HD:(h + 1) * HD] for h in (2 * b, 2 * b + 1) for tt in range(TT)])

            def unit(u, xh, xl, k0, c, banks, first, last):
                w = UNIT // c
                n = w // len(banks)
                wh = HI[:, u % RD].rearrange("p (c n) -> p c n", c=c)
                wl = LOD[:, u % RD].rearrange("p (c n) -> p c n", c=c)
                pe.wait_ge(lo_done, u + 1)
                for i in range(c):
                    for half in range(len(banks)):
                        for tt in range(TT):
                            tok, col = slice(tt * P, (tt + 1) * P), slice(half * n, (half + 1) * n)
                            ins = three(PS[:, banks[half] + tt, 0:n], xh[:, k0 + i, tok], xl[:, k0 + i, tok],
                                        wh[:, i, col], wl[:, i, col], first and i == 0, last and i == c - 1)
                ins.then_inc(used, 1)

            def panel(u, xh, xl, bank):
                unit(u, xh, xl, 0, 4, (bank,), True, False)
                unit(u + 1, xh, xl, 4, 4, (bank,), False, True)

            def attention(jobs, vals):
                flat = PS[:, 0:3].rearrange("p b n -> p (b n)")
                flat_t = PS[:, 3:6].rearrange("p b n -> p (b n)")

                def scores(j):
                    kind, h, _, g = JOBS[j]
                    if j > 0:
                        pe.wait_ge(sc_free, j)
                    for tt in range(TT):
                        for i in range(g):
                            if kind == "slot":
                                q, k = QKT[:, i * NS + h, :], QKT[:, NH + i * NS + h, :]
                            else:
                                q, k = QMT[:, h, :], KMT[0 if kind == "mem0" else 1][:, h, :]
                            o = (tt * g + i) * S
                            last = nc.tensor.matmul(flat[:, o:o + S], q[:, tt * P:(tt + 1) * P], k, start=True, stop=True)
                    last.then_inc(sc_done, 1)

                def probs_t(j):
                    g = JOBS[j][3]
                    pe.wait_ge(pn_done, TT * (j + 1))
                    if j > 0:
                        pe.wait_ge(pt_done, j)
                    for a in range(g * TT):
                        for tt in range(TT):
                            last = nc.tensor.transpose(flat_t[:, a * S + tt * P:a * S + (tt + 1) * P],
                                                       PR[:, j % 2, tt, a * P:(a + 1) * P], IDN[:, :])
                    last.then_inc(ptp_done, 1)

                def values(j):
                    kind, h, _, g = JOBS[j]
                    i = o_index(j)
                    pe.wait_ge(pt_done, j + 1)
                    if i >= 2:
                        pe.wait_ge(ol_done, i - 1)
                    src = PTB if j >= O_FOURIER else PT
                    for a in range(g * TT):
                        grp, kt = divmod(a, TT)
                        last = nc.tensor.matmul(PS[:, 6 + i % 2, 0:S], vals(kind, kt, grp, h), src[:, a, :],
                                                start=(a == 0), stop=(a == g * TT - 1))
                    last.then_inc(o_done, 1)

                scores(jobs[0])
                for j in jobs:
                    if j + 1 in jobs:
                        scores(j + 1)
                    probs_t(j)
                    values(j)

            def values_of(kind, kt, grp, h):
                if kind == "slot":
                    return V[:, kt, grp * AW + h * HD:grp * AW + (h + 1) * HD]
                return VM[0 if kind == "mem0" else 1][:, kt, h * HD:(h + 1) * HD]

            pe.wait_ge(idn_in, 16)
            pe.wait_ge(mem_in, 16)
            fills(F_MEM, MEMX)
            pe.wait_ge(x_in, 16)
            fills(F_X, X)
            pe.wait_ge(tp_free, F_MEM + 4)
            for n in range(PAN_B):
                if n >= 2:
                    pe.wait_ge(pan_free, n - 1)
                if n == 4:
                    pe.wait_ge(tp_free, F_X + 4)
                panel(2 * n, MTH if n < 4 else XTH, MTL if n < 4 else XTL, 2 * (n % 2))
                if n - 1 in KPAN:
                    k = KPAN[n - 1][0]
                    pe.wait_ge(pan_free, n)
                    panel_fills(F_K + 2 * k, STG[:, k % 2])
            pe.wait_ge(pan_free, PAN_B)
            panel_fills(F_K + 2 * KPAN[PAN_B - 1][0], STG[:, KPAN[PAN_B - 1][0] % 2])
            pe.wait_ge(tp_free, F_K + 2 * 9)
            attention(range(0, 2 * NS), values_of)
            pe.wait_ge(ol_done, 2 * NS)
            for half in range(2):
                panel(U_OUT_A + 2 * half, MIXH, MIXL, half_bank(half, 0))
            for tt in range(TT):
                pe.wait_ge(x_done, tt + 1)
                for k in range(2):
                    fill(F_X1 + 2 * tt + k, [X[:, tt, (4 * k + i) * P:(4 * k + i + 1) * P] for i in range(4)])
            pe.wait_ge(tp_free, F_X1 + 4)

            def hidden_fills(p, c):
                pe.wait_ge(h_done, p + 1)
                for tt in range(TT):
                    fill(F_H + 2 * p + tt, [HB[:, tt, i * P:(i + 1) * P] for i in range(c)])

            for p in range(FULL):
                if p > 0:
                    pe.wait_ge(gs_done, p)
                panel(U_FFN + 4 * p, XTH, XTL, 0)
                if p > 0:
                    hidden_fills(p - 1, 4)
                panel(U_FFN + 4 * p + 2, XTH, XTL, 2)
            pe.wait_ge(gs_done, FULL)
            unit(U_FFN + 4 * FULL, XTH, XTL, 0, KC, (0,), True, True)
            hidden_fills(FULL - 1, 4)
            unit(U_FFN + 4 * FULL + 1, XTH, XTL, 0, KC, (2,), True, True)
            pe.wait_ge(h_done, FULL + 1)
            down = FCH // 2
            for i in range(down):
                if i == 1:
                    hidden_fills(FULL, 2)
                if i == 2 or i == down - 1:
                    pe.wait_ge(tp_free, F_H + 2 * FULL + (2 if i == down - 1 else 0))
                unit(U_FFN_DOWN + i, HTH, HTL, 2 * i, 2, (0, 2), i == 0, i == down - 1)
            for tt in range(TT):
                pe.wait_ge(x_done, 2 + tt + 1)
                for k in range(2):
                    fill(F_X2 + 2 * tt + k, [X[:, tt, (4 * k + i) * P:(4 * k + i + 1) * P] for i in range(4)])
            pe.wait_ge(tp_free, F_X2 + 4)
            panel(U_IN_B, XTH, XTL, 0)
            panel(U_IN_B + 2, XTH, XTL, 2)
            pe.wait_ge(un_done, TT)
            for g in range(NS):
                if g == 2:
                    pe.wait_ge(pan_free, PAN_B + 2)
                for tt in range(TT):
                    last = nc.tensor.matmul(PS[:, g], UF[:, tt, g * HD:(g + 1) * HD], DFTP[:, tt, :],
                                            start=(tt == 0), stop=(tt == TT - 1))
                last.then_inc(fa_done, 1)
            pe.wait_ge(pan_free, PAN_B + 2)
            panel_fills(F_QB, STGB)
            pe.wait_ge(tp_free, F_QB + 2)
            for g in range(NS):
                i = O_FOURIER + g
                pe.wait_ge(fac_done, g + 1)
                if g >= 2:
                    pe.wait_ge(ol_done, i - 1)
                for half in range(2):
                    last = nc.tensor.matmul(PS[:, 6 + i % 2, 0:S], DFTC[:, half, :], FA[:, g % 2, half * S:(half + 1) * S],
                                            start=(half == 0), stop=(half == 1))
                last.then_inc(o_done, 1)
            attention(range(2 * NS, 3 * NS), values_of)
            pe.wait_ge(ol_done, 4 * NS)
            for half in range(2):
                panel(U_OUT_B + 2 * half, MIXH, MIXL, half_bank(half, 0))
            for tt in range(TT):
                pe.wait_ge(x_done, 4 + tt + 1)
                for k in range(2):
                    fill(F_X3 + 2 * tt + k, [X[:, tt, (4 * k + i) * P:(4 * k + i + 1) * P] for i in range(4)])
            pe.wait_ge(tp_free, F_X3 + 4)
            pe.wait_ge(rw_done, 2)
            for tt in range(TT):
                tok = slice(tt * P, (tt + 1) * P)
                for c in range(KC):
                    last = three(PS[:, 0, tt * NE:(tt + 1) * NE], RTH[:, c, tok], RTL[:, c, tok], RWH[:, c, :],
                                 RWL[:, c, :], c == 0, c == KC - 1)
            last.then_inc(lg_done, 1)
            pe.wait_ge(le_done, 1)
            sel = RS[:, 2]
            ones, tri = TRI[:, P:2 * P], TRI[:, 0:P]
            nc.tensor.matmul(PS[:, 1, 0:NE], tri, sel[:, 0, :], start=True, stop=True)
            nc.tensor.matmul(PS[:, 1, NE:2 * NE], ones, sel[:, 0, :], start=True, stop=False)
            nc.tensor.matmul(PS[:, 1, NE:2 * NE], tri, sel[:, 1, :], start=False, stop=True)
            nc.tensor.matmul(PS[0:1, 1, 2 * NE:3 * NE], ones[:, 0:1], sel[:, 0, :], start=True, stop=False)
            nc.tensor.matmul(PS[0:1, 1, 2 * NE:3 * NE], ones[:, 0:1], sel[:, 1, :], start=False,
                             stop=True).then_inc(pos_done, 1)
            pe.wait_ge(route_done, 1)

            def gather(cur, etl):
                pe.wait_ge(cur_done, cur)
                for b, (src, k) in enumerate(((XSH, 0), (XSH, 1), (XSL, 0), (XSL, 1))):
                    bank = (5, 6, 7, 4)[b]
                    if b == 3 and etl is not None:
                        pe.wait_ge(etl_done, etl)
                    for i in range(4):
                        for tt in range(TT):
                            c = 4 * k + i
                            last = nc.tensor.matmul(PS[:, bank, i * P:(i + 1) * P], src[:, tt, c * P:(c + 1) * P],
                                                    CURS[:, tt, :], start=(tt == 0), stop=(tt == TT - 1))
                    last.then_inc(gat_done, 1)

            def scatter(done):
                for i in range(4):
                    tt, half = divmod(i, 2)
                    cols = slice(half * PW, (half + 1) * PW)
                    nc.tensor.matmul(PS[:, 4 + i], CURT[:, tt, :], YH[:, cols], start=True, stop=False)
                    nc.tensor.matmul(PS[:, 4 + i], CURT[:, tt, :], YL[:, cols], start=False, stop=True).then_inc(done, 1)

            def expert_in(ub, o, k0, bank):
                s, _turn = slot_of(o)
                wh = HI[:, s].rearrange("p (c n) -> p c n", c=4)
                wl = lo_slot(s).rearrange("p (c n) -> p c n", c=4)
                pe.wait_ge(lo_done, ub + (o + 1))
                for i in range(4):
                    last = three(PS[:, bank], XEH[:, k0 + i, :], XEL[:, k0 + i, :], wh[:, i, :], wl[:, i, :],
                                 k0 + i == 0, k0 + i == KC - 1)
                last.then_inc(used, 1)

            def expert_down(ub, o, first, last_panel):
                for h in range(2):
                    s, _turn = slot_of(o + h)
                    wh = HI[:, s].rearrange("p (c n) -> p c n", c=2)
                    wl = lo_slot(s).rearrange("p (c n) -> p c n", c=2)
                    pe.wait_ge(lo_done, ub + (o + h + 1))
                    for i in range(2):
                        for half in range(2):
                            cols = slice(half * PW, (half + 1) * PW)
                            last = three(PS[:, 2 + half], EHTH[:, 2 * h + i, :], EHTL[:, 2 * h + i, :],
                                         wh[:, i, cols], wl[:, i, cols], first and h == 0 and i == 0,
                                         last_panel and h == 1 and i == 1)
                    last.then_inc(used, 1)

            def hidden_t(step):
                pe.wait_ge(eh_done, step + 1)
                for i in range(PW // P):
                    last = nc.tensor.transpose(PS[:, 4, i * P:(i + 1) * P], EH[:, i * P:(i + 1) * P], IDN[:, :])
                last.then_inc(et_done, 1)

            def experts(q):
                gather((q * (NE + 1) + 1) * TT, None)
                with pe.Fori(0, NE) as e:
                    ub = q * PASS_U + e * EXP_U + U_MOE
                    st = q * NE * STEPS + e * STEPS
                    tn = q * NE + e
                    gn = e * 2 + (q * 18 + 2)
                    pe.wait_ge(xeh_done, gn)
                    pe.wait_ge(xel_done, gn)
                    expert_in(ub, 0, 0, 0)
                    expert_in(ub, 1, 4, 0)
                    expert_in(ub, 2, 0, 1)
                    expert_in(ub, 3, 4, 1)
                    pe.wait_ge(yl_done, tn * 2 + 2)
                    scatter(scat_done)
                    pe.wait_ge(egs_done, st + 1)
                    expert_in(ub, 4, 0, 0)
                    expert_in(ub, 5, 4, 0)
                    pe.wait_ge(acc_done, tn * 4 + 4)
                    hidden_t(st)
                    pe.wait_ge(cur_done, (tn + (q + 1)) * TT)
                    for tt in range(TT):
                        nc.tensor.transpose(PS[:, 5, tt * P:(tt + 1) * P], CURS[:, tt, :].bitcast(f32), IDN[:, :])
                    for tt in range(TT):
                        last = nc.tensor.matmul(PS[:, 5, TT * P:TT * P + 1], CURS[:, tt, :].bitcast(f32),
                                                CURC[:, tt, 1:2], start=(tt == 0), stop=(tt == TT - 1))
                    last.then_inc(ct_done, 1)
                    expert_in(ub, 6, 0, 1)
                    expert_in(ub, 7, 4, 1)
                    pe.wait_ge(etl_done, st + 1)
                    expert_down(ub, 8, True, False)
                    with pe.Fori(2, STEPS) as p:
                        up = ub + (p - 1) * STEP_U
                        pe.wait_ge(egs_done, st + p)
                        expert_in(up, 4, 0, 0)
                        expert_in(up, 5, 4, 0)
                        hidden_t(st + p - 1)
                        expert_in(up, 6, 0, 1)
                        expert_in(up, 7, 4, 1)
                        pe.wait_ge(etl_done, st + p)
                        expert_down(up, 8, False, False)
                    hidden_t(st + STEPS - 1)
                    gather((tn + (q + 2)) * TT, st + STEPS)
                    expert_down(ub, EXP_U - 2, False, True)

            experts(0)
            n_pass = pe.value_load(NP_[0:1, 0:1], min_val=1, max_val=2)
            with pe.If(n_pass > 1):
                experts(1)
            pe.wait_ge(fyl_done, 2)
            scatter(fscat_done)


def _constants(shapes):
    import numpy as np
    s, p = shapes["x"][1], 128
    hd, tiles = shapes["x"][2] // 8, shapes["x"][1] // 128
    pos = np.arange(s)
    gap = np.abs(pos[:, None] - pos[None, :])
    mask = np.full((p, tiles, 3, s), -1e30, np.float32)
    for g, (window, dilation) in enumerate(((128, 1), (512, 4), (2048, 16))):
        seen = (gap % dilation == 0) & (gap <= window // 2)
        m = np.where(seen, -gap, -1e30).astype(np.float32)
        for tt in range(tiles):
            mask[:, tt, g] = m[tt * p:(tt + 1) * p]
    ang = 2 * np.pi * (np.outer(pos, pos) % s) / s
    both = np.concatenate([np.cos(ang), np.sin(ang)], 1).astype(np.float32)
    ch = np.arange(hd)
    cang = 2 * np.pi * (np.outer(ch, ch) % hd) / hd
    norm = 1.0 / np.sqrt(s * hd)
    dftc = np.stack([np.cos(cang) * norm, -np.sin(cang) * norm], 1).astype(np.float32)
    idx = np.arange(p)
    tri = (idx[:, None] < idx[None, :]).astype(np.float32)
    e = np.arange(8)
    low = np.broadcast_to((e[None, :] < e[:, None]).astype(np.float32), (p, 8, 8))
    return {
        "c_ident": np.eye(p, dtype=np.float32),
        "c_mask": mask,
        "c_dftp": np.ascontiguousarray(both.reshape(tiles, p, 2 * s).transpose(1, 0, 2)),
        "c_dftc": dftc,
        "c_iota": np.ascontiguousarray(np.broadcast_to(idx.astype(np.float32), (p, p))),
        "c_tri": np.concatenate([tri, np.ones((p, p), np.float32)], 1),
        "c_low": np.ascontiguousarray(low),
    }


def kernel(**inputs):
    import numpy as np
    import concourse.bacc as bacc
    from concourse.bass_utils import run_bass_kernel_spmd

    nc = bacc.Bacc("TRN2", target_bir_lowering=False, num_devices=1)
    given = {n: np.ascontiguousarray(a) for n, a in inputs.items()}
    given.update(_constants({n: a.shape for n, a in given.items()}))
    arrays, tensors = {}, {}
    for name, a in given.items():
        arrays[f"in_{name}"] = a
        tensors[name] = nc.dram_tensor(f"in_{name}", a.shape, mybir.dt.from_np(a.dtype), kind="ExternalInput").ap()
    tensors["out"] = nc.dram_tensor("out_0", given["x"].shape, mybir.dt.float32, kind="ExternalOutput").ap()
    hybrid_encoder(nc, tensors)
    r = run_bass_kernel_spmd(nc, [arrays], core_ids=[0])
    return r.results[0]["out_0"]
```

```python
import concourse.bass as bass
from concourse import mybir
from contextlib import ExitStack


def hybrid_encoder(nc, t):
    f32, f32r, i32 = mybir.dt.float32, mybir.dt.float32r, mybir.dt.int32
    ALU, ACT, AX = mybir.AluOpType, mybir.ActivationFunctionType, mybir.AxisListType

    P = 128
    _, S, D = t["x"].shape
    TT = S // P
    KC = D // P
    NM = t["mem"].shape[1]
    HD = D // 8
    NS = 4
    NG = 3
    AW = NS * HD
    FF = t["a_ffn_gate"].shape[2]
    NE, FE = t["b_moe_gate"].shape[1], t["b_moe_gate"].shape[3]
    PW = 512
    UNIT = 2048
    SCALE = float(HD) ** -0.5
    DEPTH = 2
    ALPHA = (2.0 * DEPTH) ** 0.25
    EPS = 1e-5
    NH = NG * NS
    assert (P, TT, KC, NM, AW) == (128, 2, 8, S, PW)

    PANEL = KC * PW // UNIT
    PROJ = t["a_w_in"].shape[2] // PW
    U_MEM_A = 0
    U_MEM_B = U_MEM_A + 2 * PANEL
    U_IN_A = U_MEM_B + 2 * PANEL
    U_OUT_A = U_IN_A + PROJ * PANEL
    U_FFN = U_OUT_A + 2 * PANEL
    FULL = FF // PW
    REST = FF - FULL * PW
    assert KC * REST == UNIT
    U_FFN_DOWN = U_FFN + FULL * 2 * PANEL + 2
    FCH = FF // P
    U_IN_B = U_FFN_DOWN + FCH // 2
    U_OUT_B = U_IN_B + 2 * PANEL
    U_MOE = U_OUT_B + 2 * PANEL
    STEPS = FE // PW
    STEP_U = 6
    EXP_U = STEPS * STEP_U
    PASS_U = NE * EXP_U
    R = 6
    RD = 3
    CAP = P

    ctx = ExitStack()
    with ctx:
        base = (nc.sbuf_base + 31) // 32 * 32
        SLOT = UNIT * 4

        def at(name, shape, dt, off):
            return nc.alloc_sbuf_tensor_at(name, shape, dt, offset=base + off)

        RAW = at("RAW", [P, R, UNIT], f32, 0)
        HI = at("HI", [P, R, UNIT], f32r, R * SLOT)
        EXT = (R + RD) * SLOT
        EXT2 = EXT + RD * SLOT
        LOD = at("LOD", [P, RD, UNIT], f32r, EXT2)
        LOE = at("LOE", [P, RD, UNIT], f32r, EXT2 + RD * SLOT)
        REST0 = EXT2 + 2 * RD * SLOT
        EXTB = EXT2 + RD * SLOT
        QKT = at("QKT", [P, 2 * NH, S], f32, EXT)
        V = at("V", [P, TT, NG * AW], f32, EXTB)
        TAIL = EXTB + TT * NG * AW * 4
        STG = at("STG", [P, 2, TT, PW], f32, TAIL)
        PT = at("PT", [P, NG * TT, S], f32, TAIL)
        MASK = at("MASK", [P, TT, NG, S], f32, TAIL + 6144)
        HTH = at("HTH", [P, FCH, S], f32r, EXT)
        HTL = at("HTL", [P, FCH, S], f32r, EXTB)
        UF = at("UF", [P, TT, PW], f32, EXT)
        DFTP = at("DFTP", [P, TT, 2 * S], f32, EXT + 4096)
        DFTC = at("DFTC", [P, 2, P], f32, EXT + 8192)
        FA = at("FA", [P, 2, 2 * S], f32, EXT + 9216)
        FG = at("FG", [P, AW], f32, EXT + 13312)
        STGB = at("STGB", [P, TT, PW], f32, EXTB)
        PTB = at("PTB", [P, TT, S], f32, EXTB + 4096)

        X = at("X", [P, TT, D], f32, REST0)
        XTH = at("XTH", [P, KC, S], f32r, REST0 + 8192)
        XTL = at("XTL", [P, KC, S], f32r, REST0 + 16384)
        MIXH = at("MIXH", [P, KC, S], f32r, REST0 + 8192)
        MIXL = at("MIXL", [P, KC, S], f32r, REST0 + 16384)
        M0 = REST0 + 24576
        MEMX = at("MEMX", [P, TT, D], f32, RD * 0 + EXT)
        MTH = at("MTH", [P, KC, S], f32r, M0)
        MTL = at("MTL", [P, KC, S], f32r, M0 + 8192)
        PR = at("PR", [P, 2, TT, NG * S], f32, M0)
        LNG = at("LNG", [P, D], f32, M0)
        LNB = at("LNB", [P, D], f32, M0 + 4096)
        SIG = at("SIG", [P, TT, PW], f32, M0 + 8192)
        HB = at("HB", [P, TT, PW], f32, M0 + 12288)
        M1 = M0 + 16384
        QMT = at("QMT", [P, NS, S], f32, M1)
        KMT = [at("KMT0", [P, NS, S], f32, M1 + 4096), at("KMT1", [P, NS, S], f32, M1 + 8192)]
        VM = [at("VM0", [P, TT, PW], f32, M1 + 12288), at("VM1", [P, TT, PW], f32, M1 + 16384)]
        C0 = M1 + 20480
        IDN = at("IDN", [P, P], f32, C0)
        SM = at("SM", [P, 320], f32, C0 + 512)
        XG = at("XG", [P, TT, D], f32, REST0 + 8192)
        XEH = at("XEH", [P, KC, CAP], f32r, M0)
        XEL = at("XEL", [P, KC, CAP], f32r, M0 + 4096)
        ESIG = at("ESIG", [P, PW], f32, M0 + 8192)
        EH = at("EH", [P, PW], f32, M0 + 10240)
        EHTH = at("EHTH", [P, PW // P, CAP], f32r, M0 + 12288)
        EHTL = at("EHTL", [P, PW // P, CAP], f32r, M0 + 14336)
        YH = at("YH", [P, D], f32r, M1)
        YL = at("YL", [P, D], f32r, M1 + 4096)
        CURS = at("CURS", [P, TT, CAP], f32r, M1 + 8192)
        CURT = at("CURT", [P, TT, P], f32r, M1 + 9216)
        IOT = at("IOT", [P, P], f32, M1 + 10240)
        TRI = at("TRI", [P, 2 * P], f32, M1 + 10752)
        RTH = at("RTH", [P, KC, S], f32r, REST0 + 16384)
        RTL = at("RTL", [P, KC, S], f32r, M0 + 8192)
        RW = at("RW", [P, KC, NE], f32, M1)
        RWP = at("RWP", [P, KC, P], f32r, M1 + 4096)
        LT = at("LT", [2 * NE, S], f32, M1 + 8192)
        RB = at("RB", [P, NE], f32, M1 + 768)
        RC = at("RC", [P, TT, NE, NE], f32, M1 + 1024)
        RC2 = at("RC2", [P, TT, NE, NE], f32, M1 + 1536)
        RC3 = at("RC3", [P, TT, NE, NE], f32, M1 + 2048)
        LOWM = at("LOWM", [P, NE, NE], f32, M1 + 2560)
        RS = at("RS", [P, 8, TT, NE], f32, M1 + 2816)
        POSC = at("POSC", [P, TT, 2, NE + 1], f32, M1 + 11776)
        CURC = at("CURC", [P, TT, 2], f32, M1 + 11936)
        CNT = at("CNT", [1, 8], f32, M1 + 11968)
        NP_ = at("NP_", [1, 8], i32, M1 + 12000)
        CG = at("CG", [P, 1], f32, M1 + 12064)
        LNG4 = at("LNG4", [P, D], f32, M1 + 12288)
        LNB4 = at("LNB4", [P, D], f32, M1 + 16384)
        MX, NMX, SUM, RSUM = SM[:, 0:2], SM[:, 2:4], SM[:, 4:6], SM[:, 6:8]
        MXB, NMXB, SUMB, RSUMB = SM[:, 8:10], SM[:, 10:12], SM[:, 12:14], SM[:, 14:16]
        BN = SM[:, 16:64].rearrange("p (t s) -> p t s", t=2)
        MV = SM[:, 64:68].rearrange("p (t s) -> p t s", t=2)
        VE, RSTD = SM[:, 68:70], SM[:, 70:72]
        FBN = SM[:, 72:120].rearrange("p (g s) -> p g s", g=8)
        FMV = SM[:, 120:136].rearrange("p (g s) -> p g s", g=8)
        FVE, FRS = SM[:, 136:144], SM[:, 144:152]

        PS = ctx.enter_context(nc.psum_tensor("PS", [P, 8, PW], f32))

        def sem(name):
            return ctx.enter_context(nc.semaphore(name))

        raw_in = [sem(f"raw_in{i}") for i in range(R)]
        hi_done = sem("hi_done")
        lo_done = sem("lo_done")
        used = sem("used")
        x_in, mem_in, idn_in, mask_in = sem("x_in"), sem("mem_in"), sem("idn_in"), sem("mask_in")
        ln_in, b_in, r_in, ln4_in, out_done = sem("ln_in"), sem("b_in"), sem("r_in"), sem("ln4_in"), sem("out_done")
        tp_done = sem("tp_done")
        th_done = sem("th_done")
        tp_free = sem("tp_free")
        pan_free = sem("pan_free")
        sc_done, sc_free, mx_done, ex_done = sem("sc_done"), sem("sc_free"), sem("mx_done"), sem("ex_done")
        pn_done, ptp_done, pt_done = sem("pn_done"), sem("ptp_done"), sem("pt_done")
        o_done, oh_done, ol_done = sem("o_done"), sem("oh_done"), sem("ol_done")
        var_done, sd_done, x_done = sem("var_done"), sem("sd_done"), sem("x_done")
        sig_done, gs_done, h_done = sem("sig_done"), sem("gs_done"), sem("h_done")
        fvar_done, fsd_done, un_done = sem("fvar_done"), sem("fsd_done"), sem("un_done")
        fa_done, fac_done = sem("fa_done"), sem("fac_done")
        xs_done, rw_done, lg_done = sem("xs_done"), sem("rw_done"), sem("lg_done")
        lt_done, ltt_done = sem("lt_done"), sem("ltt_done")
        le_done, ex8_done, sel_done, pos_done, route_done = (
            sem("le_done"), sem("ex8_done"), sem("sel_done"), sem("pos_done"), sem("route_done"))
        cur_col, cur_done, ct_done, ctt_done = sem("cur_col"), sem("cur_done"), sem("ct_done"), sem("ctt_done")
        gat_done, xeh_done, xel_done = sem("gat_done"), sem("xeh_done"), sem("xel_done")
        esig_done, egs_done, eh_done = sem("esig_done"), sem("egs_done"), sem("eh_done")
        et_done, eth_done, etl_done = sem("et_done"), sem("eth_done"), sem("etl_done")
        yh_done, yl_done, scat_done, acc_done = sem("yh_done"), sem("yl_done"), sem("scat_done"), sem("acc_done")
        fyh_done, fyl_done, fscat_done = sem("fyh_done"), sem("fyl_done"), sem("fscat_done")
        shift_done = sem("shift_done")
        v_chain = sem("v_chain")

        block = ctx.enter_context(nc.Block())

        def rows(w, k0, k1, c0, cn):
            return w[k0 * P:k1 * P, bass.ds(c0, cn)].rearrange("(c p) n -> p c n", p=P)

        def panel_units(w, c0):
            return [rows(w, 4 * h, 4 * h + 4, c0, PW) for h in range(PANEL)]

        dense_units = []
        for w in (t["a_w_mem_kv"], t["b_w_mem_kv"]):
            for n in range(2):
                dense_units += panel_units(w[0], n * PW)
        for n in range(PROJ):
            dense_units += panel_units(t["a_w_in"][0], n * PW)
        for n in range(2):
            dense_units += panel_units(t["a_w_out"][0], n * PW)
        for n in range(FULL):
            dense_units += panel_units(t["a_ffn_gate"][0], n * PW) + panel_units(t["a_ffn_up"][0], n * PW)
        for w in (t["a_ffn_gate"], t["a_ffn_up"]):
            dense_units.append(rows(w[0], 0, KC, FULL * PW, REST))
        for n in range(FCH // 2):
            dense_units.append(rows(t["a_ffn_down"][0], 2 * n, 2 * n + 2, 0, D))
        for n in range(2):
            dense_units += panel_units(t["b_w_in"][0], n * PW)
        for n in range(2):
            dense_units += panel_units(t["b_w_out"][0], n * PW)
        assert len(dense_units) == U_MOE

        def expert_unit(kind, e, p, h):
            if kind == "down":
                w = t["b_moe_down"][0, e, bass.ds(p * PW + h * 2 * P, 2 * P), :]
                return w.rearrange("(c p) n -> p c n", p=P)
            w = t["b_moe_gate" if kind == "gate" else "b_moe_up"]
            return w[0, e, 4 * h * P:(4 * h + 4) * P, bass.ds(p * PW, PW)].rearrange("(c p) n -> p c n", p=P)

        GATE_UP = [("gate", 0), ("gate", 1), ("up", 0), ("up", 1)]
        DOWN = [("down", 0), ("down", 1)]

        def slot_of(o):
            return (U_MOE + o) % R, (U_MOE + o) // R + 1

        def split_slot(o):
            return (o + RD) % R

        def lo_slot(s):
            return LOD[:, s] if s < RD else LOE[:, s - RD]

        F_MEM, F_X = 0, 4
        F_K = 8
        F_X1 = F_K + 2 * 9
        F_H = F_X1 + 4
        F_X2 = F_H + 2 * (FULL + 1)
        F_QB = F_X2 + 4
        F_X3 = F_QB + 2
        TH = {F_MEM: 0, F_X: 4, F_X1: 8, F_H: 12, F_X2: 12 + 2 * (FULL + 1), F_X3: 16 + 2 * (FULL + 1)}

        def fbank(f):
            return PS[:, 4 + f % 4]

        def fill_view(f, dst):
            c, w = dst.shape[1], dst.shape[2]
            return fbank(f)[:, 0:c * w].rearrange("p (c w) -> p c w", w=w)

        KPAN = {0: (0, KMT[0]), 2: (1, KMT[1])}
        for n in range(6):
            KPAN[4 + n] = (2 + n, QKT[:, NS * n:NS * n + NS])
        KPAN[13] = (8, QMT)
        PAN_OUT_A, PAN_B, PAN_OUT_B = 14, 14, 16

        JOBS = [("slot", h, h, NG) for h in range(NS)] + [("mem0", h, NS + h, 1) for h in range(NS)]
        JOBS += [("mem1", h, NS + h, 1) for h in range(NS)]
        O_FOURIER = 2 * NS

        def o_index(j):
            return j if j < O_FOURIER else j + NS

        def half_bank(half, tt):
            return half * 2 + tt

        @block.sync
        def _(sp):
            sp.dma_start(IDN[:, :], t["c_ident"]).then_inc(idn_in, 16)
            sp.dma_start(MEMX[:, :, :], t["mem"][0].rearrange("(t p) d -> p t d", p=P)).then_inc(mem_in, 16)
            sp.dma_start(X[:, :, :], t["x"][0].rearrange("(t p) d -> p t d", p=P)).then_inc(x_in, 16)
            for u, src in enumerate(dense_units):
                if u >= R:
                    sp.wait_ge(lo_done, u - R + 1)
                c = src.shape[1]
                sp.dma_start(RAW[:, u % R].rearrange("p (c n) -> p c n", c=c), src).then_inc(raw_in[u % R], 16)

            def load(ub, kind, e, p, h, o):
                sp.wait_ge(lo_done, ub + (o - R + 1))
                s, _turn = slot_of(o)
                c = 2 if kind == "down" else 4
                sp.dma_start(RAW[:, s].rearrange("p (c n) -> p c n", c=c),
                             expert_unit(kind, e, p, h)).then_inc(raw_in[s], 16)

            def expert(q, e):
                ub = q * PASS_U + e * EXP_U + U_MOE
                for i, (kind, h) in enumerate(GATE_UP):
                    load(ub, kind, e, 0, h, i)
                with sp.Fori(1, STEPS) as p:
                    up = ub + (p - 1) * STEP_U
                    for i, (kind, h) in enumerate(GATE_UP):
                        load(up, kind, e, p, h, 4 + i)
                    for i, (kind, h) in enumerate(DOWN):
                        load(up, kind, e, p - 1, h, 8 + i)
                for i, (kind, h) in enumerate(DOWN):
                    load(ub, kind, e, STEPS - 1, h, EXP_U - 2 + i)

            with sp.Fori(0, NE) as e:
                expert(0, e)
            sp.wait_ge(route_done, 1)
            n_pass = sp.value_load(NP_[0:1, 0:1], min_val=1, max_val=2)
            with sp.If(n_pass > 1):
                with sp.Fori(0, NE) as e:
                    expert(1, e)
            for tt in range(TT):
                sp.wait_ge(x_done, 6 + tt + 1)
                sp.dma_start(t["out"][0, tt * P:(tt + 1) * P, :], X[:, tt, :]).then_inc(out_done, 16)
            sp.wait_ge(out_done, 16 * TT)

        @block.gpsimd
        def _(gp):
            gp.wait_ge(tp_free, F_K + 2 * 8)
            gp.dma_start(MASK[:, :, :, :], t["c_mask"]).then_inc(mask_in, 16)
            norms = [("a_ln1_g", "a_ln1_b", ol_done, 2 * NS),
                     ("a_ln2_g", "a_ln2_b", x_done, 2),
                     ("b_ln1_g", "b_ln1_b", ol_done, 4 * NS)]
            for k, (g, b, s, n) in enumerate(norms):
                gp.wait_ge(s, n)
                gp.dma_start(LNG[:, :], t[g][0].partition_broadcast(P)).then_inc(ln_in, 16)
                gp.dma_start(LNB[:, :], t[b][0].partition_broadcast(P)).then_inc(ln_in, 16)
                if k == 1:
                    gp.wait_ge(x_done, 4)
                    gp.dma_start(DFTP[:, :, :], t["c_dftp"]).then_inc(b_in, 16)
                    gp.dma_start(DFTC[:, :, :], t["c_dftc"]).then_inc(b_in, 16)
                    gp.dma_start(FG[:, :], t["b_fourier_g"][0].rearrange("g d -> (g d)").partition_broadcast(P)
                                 ).then_inc(b_in, 16)
            gp.dma_start(RW[:, :, :], t["b_router_w"][0].rearrange("(c p) e -> p c e", p=P)).then_inc(r_in, 16)
            gp.dma_start(RB[:, :], t["b_router_b"][0].partition_broadcast(P)).then_inc(r_in, 16)
            gp.dma_start(LOWM[:, :, :], t["c_low"]).then_inc(r_in, 16)
            gp.dma_start(IOT[:, :], t["c_iota"]).then_inc(r_in, 16)
            gp.dma_start(TRI[:, :], t["c_tri"]).then_inc(r_in, 16)
            gp.dma_start(LNG4[:, :], t["b_ln2_g"][0].partition_broadcast(P)).then_inc(ln4_in, 16)
            gp.dma_start(LNB4[:, :], t["b_ln2_b"][0].partition_broadcast(P)).then_inc(ln4_in, 16)

        @block.scalar
        def _(act):
            def hi(u):
                act.wait_ge(raw_in[u % R], 16 * (u // R + 1))
                if u >= RD:
                    act.wait_ge(used, u - RD + 1)
                nc.scalar.activation(HI[:, u % RD], RAW[:, u % R], ACT.Copy).then_inc(hi_done, 1)

            def hi_fill(f, dst):
                act.wait_ge(tp_done, f + 1)
                nc.scalar.activation(dst, fill_view(f, dst), ACT.Copy).then_inc(th_done, 1)

            def hi_fills(f0, dst):
                for j in range(2 * TT):
                    tt, k = divmod(j, 2)
                    hi_fill(f0 + j, dst[:, 4 * k:4 * k + 4, tt * P:(tt + 1) * P])

            def panel_out(n, dst, lo_bank):
                u = 2 * n if n < PAN_B else U_IN_B + 2 * (n - PAN_B)
                act.wait_ge(used, u + PANEL)
                if n in KPAN and KPAN[n][0] >= 2:
                    act.wait_ge(tp_done, F_K + 2 * (KPAN[n][0] - 1))
                nc.scalar.activation(dst, PS[:, lo_bank:lo_bank + 2], ACT.Copy).then_inc(pan_free, 1)

            def attention(jobs):
                def exps(j):
                    act.wait_ge(mx_done, j + 1)
                    b, w = j % 2, JOBS[j][3] * S
                    nmx, total = (NMX, SUM) if b == 0 else (NMXB, SUMB)
                    for tt in range(TT):
                        nc.scalar.activation(PR[:, b, tt, 0:w], PR[:, b, tt, 0:w], ACT.Exp, bias=nmx[:, tt:tt + 1],
                                             scale=SCALE, accum_out=total[:, tt:tt + 1]).then_inc(ex_done, 1)

                def probs_t(j):
                    act.wait_ge(ptp_done, j + 1)
                    if j > 0:
                        act.wait_ge(o_done, o_index(j - 1) + 1)
                    g = JOBS[j][3]
                    dst = PTB if j >= O_FOURIER else PT
                    nc.scalar.activation(dst[:, 0:g * TT, :].rearrange("p a s -> p (a s)"),
                                         PS[:, 3:6].rearrange("p b n -> p (b n)")[:, 0:g * TT * S],
                                         ACT.Copy).then_inc(pt_done, 1)

                exps(jobs[0])
                for j in jobs:
                    probs_t(j)
                    if j + 1 in jobs:
                        exps(j + 1)
                    mix_hi(o_index(j), JOBS[j][2])

            def mix_hi(i, chunk):
                act.wait_ge(o_done, i + 1)
                nc.scalar.activation(MIXH[:, chunk, :], PS[:, 6 + i % 2, 0:S], ACT.Copy).then_inc(oh_done, 1)

            def deviations(k):
                act.wait_ge(var_done, k + 1)
                nc.scalar.activation(RSTD, VE, ACT.Sqrt).then_inc(sd_done, 1)

            def hi_first(o):
                s, turn = slot_of(o)
                act.wait_ge(raw_in[s], turn * 16)
                nc.scalar.activation(HI[:, split_slot(o)], RAW[:, s], ACT.Copy).then_inc(hi_done, 1)

            hi_fills(F_MEM, MTH)
            for u in range(RD):
                hi(u)
            hi_fills(F_X, XTH)
            for n in range(PAN_B):
                hi(2 * n + 3)
                hi(2 * n + 4)
                if n in KPAN:
                    panel_out(n, STG[:, KPAN[n][0] % 2], 2 * (n % 2))
                elif n in (1, 3):
                    panel_out(n, VM[n // 2][:, :, :], 2 * (n % 2))
                else:
                    panel_out(n, V[:, :, (n - 10) * PW:(n - 9) * PW], 2 * (n % 2))
            attention(range(0, 2 * NS))
            for u in range(U_OUT_A + RD, U_FFN + RD):
                hi(u)
            deviations(0)
            hi_fills(F_X1, XTH)
            def sigmoids(p, w):
                act.wait_ge(used, U_FFN + 4 * p + (2 if p < FULL else 1))
                if p > 0:
                    act.wait_ge(h_done, p)
                for tt in range(TT):
                    nc.scalar.activation(SIG[:, tt, 0:w], PS[:, tt, 0:w], ACT.Sigmoid).then_inc(sig_done, 1)

            def hidden_hi(p, c):
                for tt in range(TT):
                    hi_fill(F_H + 2 * p + tt, HTH[:, 4 * p:4 * p + c, tt * P:(tt + 1) * P])

            for p in range(FULL):
                for u in range(U_FFN + 4 * p + 3, U_FFN + 4 * p + 5):
                    hi(u)
                sigmoids(p, PW)
                if p > 0:
                    hidden_hi(p - 1, 4)
                for u in range(U_FFN + 4 * p + 5, U_FFN + 4 * p + 7):
                    hi(u)
            hi(U_FFN + 4 * FULL + 3)
            sigmoids(FULL, REST)
            hidden_hi(FULL - 1, 4)
            hi(U_FFN_DOWN + 2)
            hi(U_FFN_DOWN + 3)
            hidden_hi(FULL, 2)
            for u in range(U_FFN_DOWN + 4, U_IN_B + RD):
                hi(u)
            deviations(1)
            hi_fills(F_X2, XTH)
            for u in (U_IN_B + 3, U_IN_B + 4):
                hi(u)
            panel_out(PAN_B, UF[:, :, :], 0)
            hi(U_IN_B + 5)
            act.wait_ge(fvar_done, 1)
            nc.scalar.activation(FRS, FVE, ACT.Sqrt).then_inc(fsd_done, 1)
            hi(U_IN_B + 6)
            panel_out(PAN_B + 1, STGB[:, :, :], 2)
            for g in range(NS):
                act.wait_ge(fa_done, g + 1)
                if g >= 2:
                    act.wait_ge(o_done, O_FOURIER + g - 1)
                nc.scalar.activation(FA[:, g % 2], PS[:, g], ACT.Copy).then_inc(fac_done, 1)
                if g >= 1:
                    mix_hi(O_FOURIER + g - 1, g - 1)
            mix_hi(O_FOURIER + NS - 1, NS - 1)
            attention(range(2 * NS, 3 * NS))
            hi(U_MOE - 1)
            for o in range(RD):
                hi_first(o)
            act.wait_ge(r_in, 80)
            act.wait_ge(rw_done, 1)
            nc.scalar.activation(RWP[:, :, 0:NE], RW[:, :, :], ACT.Copy).then_inc(rw_done, 1)
            act.wait_ge(used, U_MOE)
            hi_first(RD)
            deviations(2)
            hi_first(RD + 1)
            hi_fills(F_X3, RTH)
            hi_first(RD + 2)
            act.wait_ge(x_done, 6)
            nc.scalar.activation(X[:, :, :], XG[:, :, :], ACT.Copy, scale=ALPHA).then_inc(xs_done, 1)
            act.wait_ge(le_done, 1)
            nc.scalar.activation(RS[:, 3], RS[:, 3], ACT.Exp).then_inc(ex8_done, 1)

            def hi_expert(ub, turns, o):
                s, turn = slot_of(o)
                act.wait_ge(raw_in[s], (turns + turn) * 16)
                act.wait_ge(used, ub + (o - R + 1))
                nc.scalar.activation(HI[:, split_slot(o)], RAW[:, s], ACT.Copy).then_inc(hi_done, 1)

            def gathered_hi(gb):
                for k in range(2):
                    act.wait_ge(gat_done, gb + k + 1)
                    nc.scalar.activation(XEH[:, 4 * k:4 * k + 4, :].rearrange("p c s -> p (c s)"), PS[:, 5 + k],
                                         ACT.Copy).then_inc(xeh_done, 1)

            def y_hi(done):
                for half in range(2):
                    nc.scalar.activation(YH[:, half * PW:(half + 1) * PW], PS[:, 2 + half], ACT.Copy,
                                         scale=CG[:, 0:1]).then_inc(done, 1)

            def expert(q, e, back=None):
                ub = q * PASS_U + e * EXP_U + U_MOE
                te = q * (PASS_U // R) + e * (EXP_U // R)
                st = q * NE * STEPS + e * STEPS

                def sigmoid(u, step, o):
                    act.wait_ge(used, u + (o + 1))
                    nc.scalar.activation(ESIG[:, :], PS[:, 0], ACT.Sigmoid).then_inc(esig_done, 1)

                def hidden_hi_e(step):
                    act.wait_ge(et_done, step + 1)
                    nc.scalar.activation(EHTH[:, :, :].rearrange("p c s -> p (c s)"), PS[:, 4],
                                         ACT.Copy).then_inc(eth_done, 1)

                if back is not None:
                    hi_expert(ub, te, 0)
                    hi_expert(ub, te, 1)
                    act.wait_ge(used, ub)
                    y_hi(yh_done)
                    hi_expert(ub, te, 2)
                    hi_expert(ub, te, 3)
                    hi_expert(ub, te, 4)
                sigmoid(ub, st, 1)
                for o in ((6, 7, 8) if back is None else (5, 6, 7, 8)):
                    hi_expert(ub, te, o)
                hidden_hi_e(st)
                sigmoid(ub, st + 1, 5)
                act.wait_ge(ct_done, q * NE + e + 1)
                nc.scalar.activation(CURT[:, :, :].rearrange("p t s -> p (t s)"), PS[:, 5, 0:2 * P],
                                     ACT.Copy).then_inc(ctt_done, 1)
                nc.scalar.activation(CG[:, :], PS[:, 5, 2 * P:2 * P + 1], ACT.Copy).then_inc(ctt_done, 1)
                hi_expert(ub, te, 9)
                with act.Fori(2, STEPS) as p:
                    up, tp = ub + (p - 1) * STEP_U, te + (p - 1)
                    for o in (4, 5, 6, 7, 8):
                        hi_expert(up, tp, o)
                    hidden_hi_e(st + p - 1)
                    sigmoid(up, st + p, 5)
                    hi_expert(up, tp, 9)
                hi_expert(ub, te, EXP_U - 2)
                hi_expert(ub, te, EXP_U - 1)
                hidden_hi_e(st + STEPS - 1)
                gathered_hi(e * 2 + (q * 18 + 2))

            gathered_hi(0)
            expert(0, 0)
            with act.Fori(0, NE - 1) as b:
                expert(0, b + 1, b)
            act.wait_ge(route_done, 1)
            n_pass = act.value_load(NP_[0:1, 0:1], min_val=1, max_val=2)
            with act.If(n_pass > 1):
                gathered_hi(18)
                with act.Fori(0, NE) as e:
                    expert(1, e, e + (NE - 1))
            act.wait_ge(used, n_pass * PASS_U + U_MOE)
            act.wait_ge(ctt_done, n_pass * (2 * NE))
            y_hi(fyh_done)
            deviations(3)

        @block.vector
        def _(dve):
            chain = [0]

            def link(ins):
                mark(ins)
                settle()

            def mark(ins):
                chain[0] += 1
                ins.then_inc(v_chain, 1)

            def settle(n=None):
                dve.wait_ge(v_chain, chain[0] if n is None else n)

            def lo(u):
                dve.wait_ge(hi_done, u + 1)
                nc.vector.tensor_tensor(LOD[:, u % RD], RAW[:, u % R], HI[:, u % RD].bitcast(f32),
                                        ALU.subtract).then_inc(lo_done, 1)

            def lo_fills(f0, hi_t, lo_t, k0=0, c=4, n=2 * TT):
                for j in range(n):
                    tt, k = divmod(j, 2) if n == 2 * TT else (j, k0)
                    f = f0 + j
                    s0 = next(b for b in sorted(TH, reverse=True) if b <= f)
                    sl = (slice(None), slice(4 * k, 4 * k + c), slice(tt * P, (tt + 1) * P))
                    dve.wait_ge(th_done, TH[s0] + f - s0 + 1)
                    nc.vector.tensor_tensor(lo_t[sl], fill_view(f, lo_t[sl]), hi_t[sl].bitcast(f32),
                                            ALU.subtract).then_inc(tp_free, 1)

            def transposed_panel(f0, dst):
                for b in range(2):
                    dve.wait_ge(tp_done, f0 + b + 1)
                    d = dst[:, 2 * b:2 * b + 2, :]
                    nc.vector.tensor_copy(d, fill_view(f0 + b, d)).then_inc(tp_free, 1)

            def attention(jobs):
                def scores(j):
                    kind, h, _, g = JOBS[j]
                    b = j % 2
                    flat = PS[:, 0:3].rearrange("p b n -> p (b n)")
                    dve.wait_ge(sc_done, j + 1)
                    if j >= 2:
                        dve.wait_ge(ptp_done, j - 1)
                    if kind == "slot":
                        if j == 0:
                            dve.wait_ge(mask_in, 16)
                        for i in range(NG):
                            slope = 2.0 ** (-(i * NS + h + 1) * 8.0 / NH)
                            ins = nc.vector.scalar_tensor_tensor(
                                out=PR[:, b, :, i * S:(i + 1) * S], in0=MASK[:, :, i, :], scalar=slope / SCALE,
                                in1=flat.rearrange("p (t g s) -> p t g s", t=TT, g=NG)[:, :, i, :],
                                op0=ALU.mult, op1=ALU.add)
                            link(ins) if i < NG - 1 else ins.then_inc(sc_free, 1)
                    else:
                        nc.vector.tensor_copy(PR[:, b, :, 0:S], flat[:, 0:TT * S].rearrange("p (t s) -> p t s", t=TT)
                                              ).then_inc(sc_free, 1)

                def maxima(j):
                    b, w = j % 2, JOBS[j][3] * S
                    mx, nmx = (MX, NMX) if b == 0 else (MXB, NMXB)
                    dve.wait_ge(sc_free, j + 1)
                    link(nc.vector.tensor_reduce(mx, PR[:, b, :, 0:w], AX.X, ALU.max))
                    nc.vector.tensor_scalar(nmx, mx, -SCALE, None, ALU.mult).then_inc(mx_done, 1)

                def normalise(j):
                    b, w = j % 2, JOBS[j][3] * S
                    total, r = (SUM, RSUM) if b == 0 else (SUMB, RSUMB)
                    dve.wait_ge(ex_done, TT * (j + 1))
                    link(nc.vector.reciprocal(r, total))
                    for tt in range(TT):
                        nc.vector.tensor_scalar(PR[:, b, tt, 0:w], PR[:, b, tt, 0:w], r[:, tt:tt + 1], None,
                                                ALU.mult).then_inc(pn_done, 1)

                scores(jobs[0])
                maxima(jobs[0])
                for j in jobs:
                    if j + 1 in jobs:
                        scores(j + 1)
                    normalise(j)
                    if j + 1 in jobs:
                        maxima(j + 1)
                    if j - 1 in jobs:
                        mix_lo(o_index(j - 1), JOBS[j - 1][2])
                mix_lo(o_index(jobs[-1]), JOBS[jobs[-1]][2])

            def lo_first(o):
                dve.wait_ge(hi_done, U_MOE + o + 1)
                nc.vector.tensor_tensor(lo_slot(split_slot(o)), RAW[:, slot_of(o)[0]], HI[:, split_slot(o)].bitcast(f32),
                                        ALU.subtract).then_inc(lo_done, 1)

            def mix_lo(i, chunk):
                dve.wait_ge(oh_done, i + 1)
                nc.vector.tensor_tensor(MIXL[:, chunk, :], PS[:, 6 + i % 2, 0:S], MIXH[:, chunk, :].bitcast(f32),
                                        ALU.subtract).then_inc(ol_done, 1)

            def stats(tt, half):
                mark(nc.vector.bn_stats(BN[:, tt, 6 * half:6 * half + 6], X[:, tt, half * PW:(half + 1) * PW]))

            def residual(half, units):
                dve.wait_ge(used, units)
                for tt in range(TT):
                    x = X[:, tt, half * PW:(half + 1) * PW]
                    mark(nc.vector.scalar_tensor_tensor(out=x, in0=x, scalar=ALPHA, in1=PS[:, half_bank(half, tt)],
                                                        op0=ALU.mult, op1=ALU.add))
                for tt in range(TT):
                    settle(chain[0] - TT + 1)
                    stats(tt, half)

            def norm(k, gain, bias, dst):
                settle()
                for tt in range(TT):
                    mark(nc.vector.bn_aggr(MV[:, tt, :], BN[:, tt, 0:12]))
                settle()
                nc.vector.tensor_scalar(VE, MV[:, :, 1], EPS, None, ALU.add).then_inc(var_done, 1)
                dve.wait_ge(*((ln_in, 32 * (k + 1)) if k < 3 else (ln4_in, 32)))
                for tt in range(TT):
                    mark(nc.vector.scalar_tensor_tensor(out=X[:, tt, :], in0=X[:, tt, :], scalar=MV[:, tt, 0:1],
                                                        in1=gain[:, :], op0=ALU.subtract, op1=ALU.mult))
                    if tt == 0:
                        dve.wait_ge(sd_done, k + 1)
                        link(nc.vector.reciprocal(RSTD, RSTD))
                for tt in range(TT):
                    settle()
                    nc.vector.scalar_tensor_tensor(out=dst[:, tt, :], in0=X[:, tt, :], scalar=RSTD[:, tt:tt + 1],
                                                   in1=bias[:, :], op0=ALU.mult, op1=ALU.add).then_inc(x_done, 1)

            lo_fills(F_MEM, MTH, MTL)
            for u in range(RD):
                lo(u)
            lo_fills(F_X, XTH, XTL)
            for n in range(PAN_B):
                if n > 0 and n - 1 in KPAN:
                    lo(2 * n + 3)
                    lo(2 * n + 4)
                    transposed_panel(F_K + 2 * KPAN[n - 1][0], KPAN[n - 1][1])
                else:
                    lo(2 * n + 3)
                    lo(2 * n + 4)
            transposed_panel(F_K + 2 * KPAN[PAN_B - 1][0], KPAN[PAN_B - 1][1])
            attention(range(0, 2 * NS))
            lo(U_OUT_A + 3)
            lo(U_OUT_A + 4)
            residual(0, U_OUT_A + 2)
            lo(U_OUT_A + 5)
            residual(1, U_OUT_A + 4)
            norm(0, LNG, LNB, X)
            lo_fills(F_X1, XTH, XTL)

            def gated(p, w):
                dve.wait_ge(sig_done, TT * (p + 1))
                nc.vector.tensor_tensor(SIG[:, :, 0:w], PS[:, 0:2, 0:w], SIG[:, :, 0:w], ALU.mult).then_inc(gs_done, 1)

            def hidden(p, w):
                dve.wait_ge(used, U_FFN + 4 * p + (4 if p < FULL else 2))
                dve.wait_ge(gs_done, p + 1)
                if p > 0:
                    dve.wait_ge(tp_done, F_H + 2 * p)
                nc.vector.tensor_tensor(HB[:, :, 0:w], PS[:, 2:4, 0:w], SIG[:, :, 0:w], ALU.mult).then_inc(h_done, 1)

            def hidden_lo(p, c):
                lo_fills(F_H + 2 * p, HTH, HTL, k0=p, c=c, n=TT)

            lo(U_FFN + 2)
            for p in range(FULL):
                lo(U_FFN + 4 * p + 3)
                lo(U_FFN + 4 * p + 4)
                gated(p, PW)
                if p > 0:
                    hidden_lo(p - 1, 4)
                lo(U_FFN + 4 * p + 5)
                lo(U_FFN + 4 * p + 6)
                hidden(p, PW)
            lo(U_FFN_DOWN + 1)
            gated(FULL, REST)
            hidden_lo(FULL - 1, 4)
            hidden(FULL, REST)
            lo(U_FFN_DOWN + 2)
            lo(U_FFN_DOWN + 3)
            hidden_lo(FULL, 2)
            for u in range(U_FFN_DOWN + 4, U_IN_B + 2):
                lo(u)
            for half in range(2):
                residual(half, U_IN_B)
            norm(1, LNG, LNB, X)
            lo_fills(F_X2, XTH, XTL)
            lo(U_IN_B + 2)
            lo(U_IN_B + 3)
            lo(U_IN_B + 4)
            uv = UF[:, :, :].rearrange("p t (g c) -> p (t g) c", c=HD)
            dve.wait_ge(pan_free, PAN_B + 1)
            for i in range(TT * NS):
                link(nc.vector.bn_stats(FBN[:, i, :], uv[:, i, :]))
                link(nc.vector.bn_aggr(FMV[:, i, :], FBN[:, i, :]))
            nc.vector.tensor_scalar(FVE, FMV[:, :, 1], EPS, None, ALU.add).then_inc(fvar_done, 1)
            lo(U_IN_B + 5)
            dve.wait_ge(fsd_done, 1)
            link(nc.vector.reciprocal(FRS, FRS))
            for i in range(TT * NS):
                link(nc.vector.tensor_scalar(uv[:, i, :], uv[:, i, :], FMV[:, i, 0:1], FRS[:, i:i + 1],
                                             ALU.subtract, ALU.mult))
            dve.wait_ge(b_in, 48)
            for tt in range(TT):
                nc.vector.tensor_tensor(UF[:, tt, :], UF[:, tt, :], FG[:, :], ALU.mult).then_inc(un_done, 1)
            lo(U_IN_B + 6)
            transposed_panel(F_QB, QMT)
            for g in range(NS):
                mix_lo(O_FOURIER + g, g)
            attention(range(2 * NS, 3 * NS))
            lo(U_MOE - 1)
            residual(0, U_OUT_B + 2)
            for o in range(RD):
                lo_first(o)
            nc.vector.memset(RWP[:, :, :].bitcast(f32), 0.0).then_inc(rw_done, 1)
            dve.wait_ge(rw_done, 2)
            nc.vector.tensor_tensor(RWP[:, :, NE:2 * NE], RW[:, :, :], RWP[:, :, 0:NE].bitcast(f32),
                                    ALU.subtract).then_inc(rw_done, 1)
            residual(1, U_OUT_B + 4)
            norm(2, LNG, LNB, XG)

            lo_fills(F_X3, RTH, RTL)
            link(nc.vector.memset(POSC[:, :, 0, :], -1.0))
            nc.vector.memset(POSC[:, :, 1, :], 0.0).then_inc(acc_done, 4)
            dve.wait_ge(acc_done, 4)
            lo_first(RD)
            logit, rank, sel, ex, top = (RS[:, i] for i in (0, 1, 2, 3, 4))
            dve.wait_ge(lg_done, 1)
            nc.vector.tensor_copy(LT[:, :], PS[0:2 * NE, 0, 0:S]).then_inc(lt_done, 1)
            dve.wait_ge(ltt_done, 1)
            parts = PS[:, 1, 0:TT * 2 * NE].rearrange("p (t e) -> p t e", t=TT)
            link(nc.vector.tensor_tensor(logit, parts[:, :, 0:NE], RB[:, :].unsqueeze(1).to_broadcast([P, TT, NE]),
                                         ALU.add))
            link(nc.vector.tensor_tensor(logit, parts[:, :, NE:2 * NE], logit, ALU.add))
            mark(nc.vector.tensor_reduce(top[:, :, 0], logit, AX.X, ALU.max))
            for tt in range(TT):
                this = logit[:, tt, :].unsqueeze(2).to_broadcast([P, NE, NE])
                other = logit[:, tt, :].unsqueeze(1).to_broadcast([P, NE, NE])
                mark(nc.vector.tensor_tensor(RC[:, tt], other, this, ALU.is_gt))
                mark(nc.vector.tensor_tensor(RC2[:, tt], other, this, ALU.is_equal))
            settle()
            mark(nc.vector.tensor_tensor(ex, logit, top[:, :, 0:1].to_broadcast([P, TT, NE]), ALU.subtract))
            for tt in range(TT):
                mark(nc.vector.tensor_tensor(RC3[:, tt], RC2[:, tt], LOWM[:, :, :], ALU.mult))
            settle()
            link(nc.vector.tensor_tensor(RC[:, :, :, :], RC[:, :, :, :], RC3[:, :, :, :], ALU.add))
            link(nc.vector.tensor_reduce(rank, RC[:, :, :, :], AX.X, ALU.add))
            nc.vector.tensor_scalar(sel, rank, 1.5, None, ALU.is_lt).then_inc(le_done, 1)
            lo_first(RD + 1)
            dve.wait_ge(ex8_done, 1)
            dve.wait_ge(le_done, 1)
            link(nc.vector.tensor_tensor(ex, ex, sel, ALU.mult))
            link(nc.vector.tensor_reduce(top[:, :, 1], ex, AX.X, ALU.add))
            link(nc.vector.reciprocal(top[:, :, 2], top[:, :, 1]))
            mark(nc.vector.tensor_tensor(POSC[:, :, 1, 0:NE], ex, top[:, :, 2:3].to_broadcast([P, TT, NE]), ALU.mult))
            dve.wait_ge(pos_done, 1)
            link(nc.vector.scalar_tensor_tensor(out=rank, in0=PS[:, 2, 0:TT * NE].rearrange("p (t e) -> p t e", t=TT),
                                                scalar=1.0, in1=sel, op0=ALU.add, op1=ALU.mult))
            link(nc.vector.tensor_scalar(POSC[:, :, 0, 0:NE], rank, -1.0, None, ALU.add))
            link(nc.vector.tensor_reduce(CNT[0:1, 0:1], PS[0:1, 2, TT * NE:TT * NE + NE], AX.X, ALU.max))
            nc.vector.tensor_scalar(NP_[0:1, 0:1], CNT[0:1, 0:1], CAP + 0.5, 1.0, ALU.is_gt, ALU.add
                                    ).then_inc(route_done, 1)

            def slot_map(e, n):
                nc.vector.tensor_copy(CURC[:, :, :], POSC[:, :, :, bass.ds(e, 1)].rearrange("p t k o -> p t (k o)")
                                      ).then_inc(cur_col, 1)
                dve.wait_ge(cur_col, n + 1)
                for tt in range(TT):
                    nc.vector.tensor_scalar(CURS[:, tt, :], IOT[:, :], CURC[:, tt, 0:1], None,
                                            ALU.is_equal).then_inc(cur_done, 1)

            def lo_expert(ub, o):
                s, _turn = slot_of(o)
                dve.wait_ge(hi_done, ub + (o + 1))
                nc.vector.tensor_tensor(lo_slot(split_slot(o)), RAW[:, s], HI[:, split_slot(o)].bitcast(f32),
                                        ALU.subtract).then_inc(lo_done, 1)

            def gathered_lo(gb):
                for k in range(2):
                    chunks = slice(4 * k, 4 * k + 4)
                    dve.wait_ge(xeh_done, gb + (k + 1))
                    nc.vector.tensor_tensor(XEL[:, chunks, :].rearrange("p c s -> p (c s)"), PS[:, 5 + k],
                                            XEH[:, chunks, :].rearrange("p c s -> p (c s)").bitcast(f32),
                                            ALU.subtract).then_inc(xel_done, 1)

            def y_lo(hi_sem, n, done):
                for half in range(2):
                    cols = slice(half * PW, (half + 1) * PW)
                    dve.wait_ge(hi_sem, n + (half + 1))
                    nc.vector.scalar_tensor_tensor(out=YL[:, cols], in0=PS[:, 2 + half], scalar=CG[:, 0:1],
                                                   in1=YH[:, cols].bitcast(f32), op0=ALU.mult,
                                                   op1=ALU.subtract).then_inc(done, 1)

            def send_back(scat, n, done):
                for i in range(4):
                    tt, half = divmod(i, 2)
                    x = X[:, tt, half * PW:(half + 1) * PW]
                    dve.wait_ge(scat, n + (i + 1))
                    nc.vector.tensor_tensor(x, x, PS[:, 4 + i], ALU.add).then_inc(done, 1)

            def expert(q, e, back=None):
                ub = q * PASS_U + e * EXP_U + U_MOE
                st = q * NE * STEPS + e * STEPS
                tn = q * NE + e

                def gated_e(step):
                    dve.wait_ge(esig_done, step + 1)
                    nc.vector.tensor_tensor(ESIG[:, :], PS[:, 0], ESIG[:, :], ALU.mult).then_inc(egs_done, 1)

                def hidden_e(u, step, o):
                    dve.wait_ge(used, u + (o + 1))
                    dve.wait_ge(egs_done, step + 1)
                    nc.vector.tensor_tensor(EH[:, :], PS[:, 1], ESIG[:, :], ALU.mult).then_inc(eh_done, 1)

                def hidden_lo_e(step):
                    dve.wait_ge(eth_done, step + 1)
                    nc.vector.tensor_tensor(EHTL[:, :, :].rearrange("p c s -> p (c s)"), PS[:, 4],
                                            EHTH[:, :, :].rearrange("p c s -> p (c s)").bitcast(f32),
                                            ALU.subtract).then_inc(etl_done, 1)

                if back is not None:
                    lo_expert(ub, 0)
                    lo_expert(ub, 1)
                    y_lo(yh_done, back * 2, yl_done)
                    lo_expert(ub, 2)
                    lo_expert(ub, 3)
                    lo_expert(ub, 4)
                gated_e(st)
                if back is not None:
                    lo_expert(ub, 5)
                    send_back(scat_done, back * 4, acc_done)
                lo_expert(ub, 6)
                hidden_e(ub, st, 3)
                lo_expert(ub, 7)
                lo_expert(ub, 8)
                hidden_lo_e(st)
                gated_e(st + 1)
                dve.wait_ge(ct_done, tn + 1)
                slot_map(e + 1, tn + (q + 1))
                lo_expert(ub, 9)
                with dve.Fori(2, STEPS) as p:
                    up = ub + (p - 1) * STEP_U
                    lo_expert(up, 4)
                    hidden_e(up, st + p - 1, 4 - STEP_U + 3)
                    for o in (5, 6, 7, 8):
                        lo_expert(up, o)
                    hidden_lo_e(st + p - 1)
                    gated_e(st + p)
                    lo_expert(up, 9)
                lo_expert(ub, EXP_U - 2)
                hidden_e(ub, st + STEPS - 1, EXP_U - 5)
                lo_expert(ub, EXP_U - 1)
                hidden_lo_e(st + STEPS - 1)
                gathered_lo(e * 2 + (q * 18 + 2))

            slot_map(0, 0)
            lo_first(RD + 2)
            gathered_lo(0)
            dve.wait_ge(xs_done, 1)
            expert(0, 0)
            with dve.Fori(0, NE - 1) as b:
                expert(0, b + 1, b)
            dve.wait_ge(route_done, 1)
            n_pass = dve.value_load(NP_[0:1, 0:1], min_val=1, max_val=2)
            with dve.If(n_pass > 1):
                dve.wait_ge(gat_done, 18)
                nc.vector.tensor_scalar(POSC[:, :, 0, :], POSC[:, :, 0, :], -float(CAP), None,
                                        ALU.add).then_inc(shift_done, 1)
                dve.wait_ge(shift_done, 1)
                slot_map(0, NE + 1)
                gathered_lo(18)
                with dve.Fori(0, NE) as e:
                    expert(1, e, e + (NE - 1))
            y_lo(fyh_done, 0, fyl_done)
            dve.wait_ge(acc_done, n_pass * (4 * NE))
            for i in range(4):
                tt, half = divmod(i, 2)
                x = X[:, tt, half * PW:(half + 1) * PW]
                dve.wait_ge(fscat_done, i + 1)
                link(nc.vector.tensor_tensor(x, x, PS[:, 4 + i], ALU.add))
                stats(tt, half)
            norm(3, LNG4, LNB4, X)

        @block.tensor
        def _(pe):
            def three(out, xh, xl, wh, wl, first, last):
                nc.tensor.matmul(out, xh, wh, start=first, stop=False)
                nc.tensor.matmul(out, xh, wl, start=False, stop=False)
                return nc.tensor.matmul(out, xl, wh, start=False, stop=last)

            def fills(f0, src, n=2 * TT):
                for j in range(n):
                    tt, k = divmod(j, 2)
                    fill(f0 + j, [src[:, tt, (4 * k + i) * P:(4 * k + i + 1) * P] for i in range(4)])

            def fill(f, blocks):
                if f >= 4:
                    pe.wait_ge(tp_free, f - 3)
                for i, blk in enumerate(blocks):
                    last = nc.tensor.transpose(fbank(f)[:, i * P:(i + 1) * P], blk, IDN[:, :])
                last.then_inc(tp_done, 1)

            def panel_fills(f0, stg):
                for b in range(2):
                    fill(f0 + b, [stg[:, tt, h * HD:(h + 1) * HD] for h in (2 * b, 2 * b + 1) for tt in range(TT)])

            def unit(u, xh, xl, k0, c, banks, first, last):
                w = UNIT // c
                n = w // len(banks)
                wh = HI[:, u % RD].rearrange("p (c n) -> p c n", c=c)
                wl = LOD[:, u % RD].rearrange("p (c n) -> p c n", c=c)
                pe.wait_ge(lo_done, u + 1)
                for i in range(c):
                    for half in range(len(banks)):
                        for tt in range(TT):
                            tok, col = slice(tt * P, (tt + 1) * P), slice(half * n, (half + 1) * n)
                            ins = three(PS[:, banks[half] + tt, 0:n], xh[:, k0 + i, tok], xl[:, k0 + i, tok],
                                        wh[:, i, col], wl[:, i, col], first and i == 0, last and i == c - 1)
                ins.then_inc(used, 1)

            def first_panel(u, f0, src, n_norm, bank, xh=XTH, xl=XTL):
                for tt in range(TT):
                    pe.wait_ge(x_done, TT * n_norm + tt + 1)
                    for k in range(2):
                        fill(f0 + 2 * tt + k, [src[:, tt, (4 * k + i) * P:(4 * k + i + 1) * P] for i in range(4)])
                if u is None:
                    return
                pe.wait_ge(lo_done, u + PANEL)
                for tt in range(TT):
                    pe.wait_ge(tp_free, f0 + 2 * tt + 2)
                    tok = slice(tt * P, (tt + 1) * P)
                    for c in range(KC):
                        h, i = divmod(c, 4)
                        wh = HI[:, (u + h) % RD].rearrange("p (c n) -> p c n", c=4)[:, i, :]
                        wl = LOD[:, (u + h) % RD].rearrange("p (c n) -> p c n", c=4)[:, i, :]
                        ins = three(PS[:, bank + tt], xh[:, c, tok], xl[:, c, tok], wh, wl, c == 0, c == KC - 1)
                        if tt == TT - 1 and i == 3:
                            ins.then_inc(used, 1)

            def panel(u, xh, xl, bank):
                unit(u, xh, xl, 0, 4, (bank,), True, False)
                unit(u + 1, xh, xl, 4, 4, (bank,), False, True)

            def attention(jobs, vals):
                flat = PS[:, 0:3].rearrange("p b n -> p (b n)")
                flat_t = PS[:, 3:6].rearrange("p b n -> p (b n)")

                def scores(j):
                    kind, h, _, g = JOBS[j]
                    if j > 0:
                        pe.wait_ge(sc_free, j)
                    for tt in range(TT):
                        for i in range(g):
                            if kind == "slot":
                                q, k = QKT[:, i * NS + h, :], QKT[:, NH + i * NS + h, :]
                            else:
                                q, k = QMT[:, h, :], KMT[0 if kind == "mem0" else 1][:, h, :]
                            o = (tt * g + i) * S
                            last = nc.tensor.matmul(flat[:, o:o + S], q[:, tt * P:(tt + 1) * P], k, start=True, stop=True)
                    last.then_inc(sc_done, 1)

                def probs_t(j):
                    g = JOBS[j][3]
                    pe.wait_ge(pn_done, TT * (j + 1))
                    if j > 0:
                        pe.wait_ge(pt_done, j)
                    for a in range(g * TT):
                        for tt in range(TT):
                            last = nc.tensor.transpose(flat_t[:, a * S + tt * P:a * S + (tt + 1) * P],
                                                       PR[:, j % 2, tt, a * P:(a + 1) * P], IDN[:, :])
                    last.then_inc(ptp_done, 1)

                def values(j):
                    kind, h, _, g = JOBS[j]
                    i = o_index(j)
                    pe.wait_ge(pt_done, j + 1)
                    if i >= 2:
                        pe.wait_ge(ol_done, i - 1)
                    src = PTB if j >= O_FOURIER else PT
                    for a in range(g * TT):
                        grp, kt = divmod(a, TT)
                        last = nc.tensor.matmul(PS[:, 6 + i % 2, 0:S], vals(kind, kt, grp, h), src[:, a, :],
                                                start=(a == 0), stop=(a == g * TT - 1))
                    last.then_inc(o_done, 1)

                scores(jobs[0])
                for j in jobs:
                    if j + 1 in jobs:
                        scores(j + 1)
                    probs_t(j)
                    values(j)

            def values_of(kind, kt, grp, h):
                if kind == "slot":
                    return V[:, kt, grp * AW + h * HD:grp * AW + (h + 1) * HD]
                return VM[0 if kind == "mem0" else 1][:, kt, h * HD:(h + 1) * HD]

            pe.wait_ge(idn_in, 16)
            pe.wait_ge(mem_in, 16)
            fills(F_MEM, MEMX)
            pe.wait_ge(x_in, 16)
            fills(F_X, X)
            pe.wait_ge(tp_free, F_MEM + 4)
            for n in range(PAN_B):
                if n >= 2:
                    pe.wait_ge(pan_free, n - 1)
                if n == 4:
                    pe.wait_ge(tp_free, F_X + 4)
                panel(2 * n, MTH if n < 4 else XTH, MTL if n < 4 else XTL, 2 * (n % 2))
                if n - 1 in KPAN:
                    k = KPAN[n - 1][0]
                    pe.wait_ge(pan_free, n)
                    panel_fills(F_K + 2 * k, STG[:, k % 2])
            pe.wait_ge(pan_free, PAN_B)
            panel_fills(F_K + 2 * KPAN[PAN_B - 1][0], STG[:, KPAN[PAN_B - 1][0] % 2])
            pe.wait_ge(tp_free, F_K + 2 * 9)
            attention(range(0, 2 * NS), values_of)
            pe.wait_ge(ol_done, 2 * NS)
            for half in range(2):
                panel(U_OUT_A + 2 * half, MIXH, MIXL, half_bank(half, 0))

            def hidden_fills(p, c):
                pe.wait_ge(h_done, p + 1)
                for tt in range(TT):
                    fill(F_H + 2 * p + tt, [HB[:, tt, i * P:(i + 1) * P] for i in range(c)])

            for p in range(FULL):
                if p > 0:
                    pe.wait_ge(gs_done, p)
                    panel(U_FFN + 4 * p, XTH, XTL, 0)
                else:
                    first_panel(U_FFN, F_X1, X, 0, 0)
                if p > 0:
                    hidden_fills(p - 1, 4)
                panel(U_FFN + 4 * p + 2, XTH, XTL, 2)
            pe.wait_ge(gs_done, FULL)
            unit(U_FFN + 4 * FULL, XTH, XTL, 0, KC, (0,), True, True)
            hidden_fills(FULL - 1, 4)
            unit(U_FFN + 4 * FULL + 1, XTH, XTL, 0, KC, (2,), True, True)
            pe.wait_ge(h_done, FULL + 1)
            down = FCH // 2
            for i in range(down):
                if i == 1:
                    hidden_fills(FULL, 2)
                if i == 2 or i == down - 1:
                    pe.wait_ge(tp_free, F_H + 2 * FULL + (2 if i == down - 1 else 0))
                unit(U_FFN_DOWN + i, HTH, HTL, 2 * i, 2, (0, 2), i == 0, i == down - 1)
            first_panel(U_IN_B, F_X2, X, 1, 0)
            panel(U_IN_B + 2, XTH, XTL, 2)
            pe.wait_ge(un_done, TT)
            for g in range(NS):
                if g == 2:
                    pe.wait_ge(pan_free, PAN_B + 2)
                for tt in range(TT):
                    last = nc.tensor.matmul(PS[:, g], UF[:, tt, g * HD:(g + 1) * HD], DFTP[:, tt, :],
                                            start=(tt == 0), stop=(tt == TT - 1))
                last.then_inc(fa_done, 1)
            pe.wait_ge(pan_free, PAN_B + 2)
            panel_fills(F_QB, STGB)
            pe.wait_ge(tp_free, F_QB + 2)
            for g in range(NS):
                i = O_FOURIER + g
                pe.wait_ge(fac_done, g + 1)
                if g >= 2:
                    pe.wait_ge(ol_done, i - 1)
                for half in range(2):
                    last = nc.tensor.matmul(PS[:, 6 + i % 2, 0:S], DFTC[:, half, :], FA[:, g % 2, half * S:(half + 1) * S],
                                            start=(half == 0), stop=(half == 1))
                last.then_inc(o_done, 1)
            attention(range(2 * NS, 3 * NS), values_of)
            pe.wait_ge(ol_done, 4 * NS)
            for half in range(2):
                panel(U_OUT_B + 2 * half, MIXH, MIXL, half_bank(half, 0))
            first_panel(None, F_X3, XG, 2, None)
            pe.wait_ge(rw_done, 3)
            pe.wait_ge(tp_free, F_X3 + 4)
            for c in range(KC):
                nc.tensor.matmul(PS[:, 0, 0:S], RWP[:, c, :], RTH[:, c, :], start=(c == 0), stop=False)
                last = nc.tensor.matmul(PS[:, 0, 0:S], RWP[:, c, :], RTL[:, c, :], start=False, stop=(c == KC - 1))
            last.then_inc(lg_done, 1)
            pe.wait_ge(lt_done, 1)
            for tt in range(TT):
                last = nc.tensor.transpose(PS[:, 1, tt * 2 * NE:(tt + 1) * 2 * NE], LT[:, tt * P:(tt + 1) * P],
                                           IDN[0:2 * NE, 0:2 * NE])
            last.then_inc(ltt_done, 1)
            pe.wait_ge(le_done, 1)
            sel = RS[:, 2]
            ones, tri = TRI[:, P:2 * P], TRI[:, 0:P]
            nc.tensor.matmul(PS[:, 2, 0:NE], tri, sel[:, 0, :], start=True, stop=True)
            nc.tensor.matmul(PS[:, 2, NE:2 * NE], ones, sel[:, 0, :], start=True, stop=False)
            nc.tensor.matmul(PS[:, 2, NE:2 * NE], tri, sel[:, 1, :], start=False, stop=True)
            nc.tensor.matmul(PS[0:1, 2, 2 * NE:3 * NE], ones[:, 0:1], sel[:, 0, :], start=True, stop=False)
            nc.tensor.matmul(PS[0:1, 2, 2 * NE:3 * NE], ones[:, 0:1], sel[:, 1, :], start=False,
                             stop=True).then_inc(pos_done, 1)
            pe.wait_ge(route_done, 1)

            def gather(cur):
                pe.wait_ge(cur_done, cur)
                for c in range(KC):
                    for tt in range(TT):
                        last = nc.tensor.matmul(PS[:, 5 + c // 4, (c % 4) * P:(c % 4 + 1) * P],
                                                XG[:, tt, c * P:(c + 1) * P], CURS[:, tt, :].bitcast(f32),
                                                start=(tt == 0), stop=(tt == TT - 1))
                    if c % 4 == 3:
                        last.then_inc(gat_done, 1)

            def scatter(done):
                for i in range(4):
                    tt, half = divmod(i, 2)
                    cols = slice(half * PW, (half + 1) * PW)
                    nc.tensor.matmul(PS[:, 4 + i], CURT[:, tt, :], YH[:, cols], start=True, stop=False)
                    nc.tensor.matmul(PS[:, 4 + i], CURT[:, tt, :], YL[:, cols], start=False, stop=True).then_inc(done, 1)

            def expert_in(ub, o, k0, bank):
                s = split_slot(o)
                wh = HI[:, s].rearrange("p (c n) -> p c n", c=4)
                wl = lo_slot(s).rearrange("p (c n) -> p c n", c=4)
                pe.wait_ge(lo_done, ub + (o + 1))
                for i in range(4):
                    last = three(PS[:, bank], XEH[:, k0 + i, :], XEL[:, k0 + i, :], wh[:, i, :], wl[:, i, :],
                                 k0 + i == 0, k0 + i == KC - 1)
                last.then_inc(used, 1)

            def expert_down(ub, o, first, last_panel):
                for h in range(2):
                    s = split_slot(o + h)
                    wh = HI[:, s].rearrange("p (c n) -> p c n", c=2)
                    wl = lo_slot(s).rearrange("p (c n) -> p c n", c=2)
                    pe.wait_ge(lo_done, ub + (o + h + 1))
                    for i in range(2):
                        for half in range(2):
                            cols = slice(half * PW, (half + 1) * PW)
                            last = three(PS[:, 2 + half], EHTH[:, 2 * h + i, :], EHTL[:, 2 * h + i, :],
                                         wh[:, i, cols], wl[:, i, cols], first and h == 0 and i == 0,
                                         last_panel and h == 1 and i == 1)
                    last.then_inc(used, 1)

            def hidden_t(step):
                pe.wait_ge(eh_done, step + 1)
                for i in range(PW // P):
                    last = nc.tensor.transpose(PS[:, 4, i * P:(i + 1) * P], EH[:, i * P:(i + 1) * P], IDN[:, :])
                last.then_inc(et_done, 1)

            def expert(q, e, back=None):
                ub = q * PASS_U + e * EXP_U + U_MOE
                st = q * NE * STEPS + e * STEPS
                tn = q * NE + e
                gn = e * 2 + (q * 18 + 2)
                pe.wait_ge(xeh_done, gn)
                pe.wait_ge(xel_done, gn)
                expert_in(ub, 0, 0, 0)
                expert_in(ub, 1, 4, 0)
                expert_in(ub, 2, 0, 1)
                expert_in(ub, 3, 4, 1)
                if back is not None:
                    pe.wait_ge(yl_done, back * 2 + 2)
                    scatter(scat_done)
                pe.wait_ge(egs_done, st + 1)
                expert_in(ub, 4, 0, 0)
                expert_in(ub, 5, 4, 0)
                if back is not None:
                    pe.wait_ge(acc_done, back * 4 + 8)
                hidden_t(st)
                pe.wait_ge(cur_done, (tn + (q + 1)) * TT)
                for tt in range(TT):
                    nc.tensor.transpose(PS[:, 5, tt * P:(tt + 1) * P], CURS[:, tt, :].bitcast(f32), IDN[:, :])
                for tt in range(TT):
                    last = nc.tensor.matmul(PS[:, 5, TT * P:TT * P + 1], CURS[:, tt, :].bitcast(f32),
                                            CURC[:, tt, 1:2], start=(tt == 0), stop=(tt == TT - 1))
                last.then_inc(ct_done, 1)
                expert_in(ub, 6, 0, 1)
                expert_in(ub, 7, 4, 1)
                pe.wait_ge(etl_done, st + 1)
                expert_down(ub, 8, True, False)
                with pe.Fori(2, STEPS) as p:
                    up = ub + (p - 1) * STEP_U
                    pe.wait_ge(egs_done, st + p)
                    expert_in(up, 4, 0, 0)
                    expert_in(up, 5, 4, 0)
                    hidden_t(st + p - 1)
                    expert_in(up, 6, 0, 1)
                    expert_in(up, 7, 4, 1)
                    pe.wait_ge(etl_done, st + p)
                    expert_down(up, 8, False, False)
                hidden_t(st + STEPS - 1)
                gather((tn + (q + 2)) * TT)
                pe.wait_ge(etl_done, st + STEPS)
                expert_down(ub, EXP_U - 2, False, True)

            gather(TT)
            expert(0, 0)
            with pe.Fori(0, NE - 1) as b:
                expert(0, b + 1, b)
            n_pass = pe.value_load(NP_[0:1, 0:1], min_val=1, max_val=2)
            with pe.If(n_pass > 1):
                pe.wait_ge(xeh_done, 18)
                pe.wait_ge(xel_done, 18)
                gather((NE + 2) * TT)
                with pe.Fori(0, NE) as e:
                    expert(1, e, e + (NE - 1))
            pe.wait_ge(fyl_done, 2)
            scatter(fscat_done)


def _constants(shapes):
    import numpy as np
    s, p = shapes["x"][1], 128
    hd, tiles = shapes["x"][2] // 8, shapes["x"][1] // 128
    pos = np.arange(s)
    gap = np.abs(pos[:, None] - pos[None, :])
    mask = np.full((p, tiles, 3, s), -1e30, np.float32)
    for g, (window, dilation) in enumerate(((128, 1), (512, 4), (2048, 16))):
        seen = (gap % dilation == 0) & (gap <= window // 2)
        m = np.where(seen, -gap, -1e30).astype(np.float32)
        for tt in range(tiles):
            mask[:, tt, g] = m[tt * p:(tt + 1) * p]
    ang = 2 * np.pi * (np.outer(pos, pos) % s) / s
    both = np.concatenate([np.cos(ang), np.sin(ang)], 1).astype(np.float32)
    ch = np.arange(hd)
    cang = 2 * np.pi * (np.outer(ch, ch) % hd) / hd
    norm = 1.0 / np.sqrt(s * hd)
    dftc = np.stack([np.cos(cang) * norm, -np.sin(cang) * norm], 1).astype(np.float32)
    idx = np.arange(p)
    tri = (idx[:, None] < idx[None, :]).astype(np.float32)
    e = np.arange(8)
    low = np.broadcast_to((e[None, :] < e[:, None]).astype(np.float32), (p, 8, 8))
    return {
        "c_ident": np.eye(p, dtype=np.float32),
        "c_mask": mask,
        "c_dftp": np.ascontiguousarray(both.reshape(tiles, p, 2 * s).transpose(1, 0, 2)),
        "c_dftc": dftc,
        "c_iota": np.ascontiguousarray(np.broadcast_to(idx.astype(np.float32), (p, p))),
        "c_tri": np.concatenate([tri, np.ones((p, p), np.float32)], 1),
        "c_low": np.ascontiguousarray(low),
    }


def kernel(**inputs):
    import numpy as np
    import concourse.bacc as bacc
    from concourse.bass_utils import run_bass_kernel_spmd

    nc = bacc.Bacc("TRN2", target_bir_lowering=False, num_devices=1)
    given = {n: np.ascontiguousarray(a) for n, a in inputs.items()}
    given.update(_constants({n: a.shape for n, a in given.items()}))
    arrays, tensors = {}, {}
    for name, a in given.items():
        arrays[f"in_{name}"] = a
        tensors[name] = nc.dram_tensor(f"in_{name}", a.shape, mybir.dt.from_np(a.dtype), kind="ExternalInput").ap()
    tensors["out"] = nc.dram_tensor("out_0", given["x"].shape, mybir.dt.float32, kind="ExternalOutput").ap()
    hybrid_encoder(nc, tensors)
    r = run_bass_kernel_spmd(nc, [arrays], core_ids=[0])
    return r.results[0]["out_0"]
```

```python
import concourse.bass as bass
from concourse import mybir
from contextlib import ExitStack


def hybrid_encoder(nc, t):
    f32, f32r, i32 = mybir.dt.float32, mybir.dt.float32r, mybir.dt.int32
    ALU, ACT, AX = mybir.AluOpType, mybir.ActivationFunctionType, mybir.AxisListType

    P = 128
    _, S, D = t["x"].shape
    TT = S // P
    KC = D // P
    NM = t["mem"].shape[1]
    HD = D // 8
    NS = 4
    NG = 3
    AW = NS * HD
    FF = t["a_ffn_gate"].shape[2]
    NE, FE = t["b_moe_gate"].shape[1], t["b_moe_gate"].shape[3]
    PW = 512
    UNIT = 2048
    SCALE = float(HD) ** -0.5
    DEPTH = 2
    ALPHA = (2.0 * DEPTH) ** 0.25
    EPS = 1e-5
    NH = NG * NS
    assert (P, TT, KC, NM, AW) == (128, 2, 8, S, PW)

    PANEL = KC * PW // UNIT
    PROJ = t["a_w_in"].shape[2] // PW
    U_MEM_A = 0
    U_MEM_B = U_MEM_A + 2 * PANEL
    U_IN_A = U_MEM_B + 2 * PANEL
    U_OUT_A = U_IN_A + PROJ * PANEL
    U_FFN = U_OUT_A + 2 * PANEL
    FULL = FF // PW
    REST = FF - FULL * PW
    assert KC * REST == UNIT
    U_FFN_DOWN = U_FFN + FULL * 2 * PANEL + 2
    FCH = FF // P
    U_IN_B = U_FFN_DOWN + FCH // 2
    U_OUT_B = U_IN_B + 2 * PANEL
    U_MOE = U_OUT_B + 2 * PANEL
    STEPS = FE // PW
    STEP_U = 6
    EXP_U = STEPS * STEP_U
    PASS_U = NE * EXP_U
    R = 6
    RD = 3
    CAP = P

    ctx = ExitStack()
    with ctx:
        base = (nc.sbuf_base + 31) // 32 * 32
        SLOT = UNIT * 4

        def at(name, shape, dt, off):
            return nc.alloc_sbuf_tensor_at(name, shape, dt, offset=base + off)

        RAW = at("RAW", [P, R, UNIT], f32, 0)
        HI = at("HI", [P, R, UNIT], f32r, R * SLOT)
        EXT = (R + RD) * SLOT
        EXT2 = EXT + RD * SLOT
        LOD = at("LOD", [P, RD, UNIT], f32r, EXT2)
        LOE = at("LOE", [P, RD, UNIT], f32r, EXT2 + RD * SLOT)
        REST0 = EXT2 + 2 * RD * SLOT
        EXTB = EXT2 + RD * SLOT
        QKT = at("QKT", [P, 2 * NH, S], f32, EXT)
        V = at("V", [P, TT, NG * AW], f32, EXTB)
        TAIL = EXTB + TT * NG * AW * 4
        STG = at("STG", [P, 2, TT, PW], f32, TAIL)
        PT = at("PT", [P, 8, P], f32, TAIL)
        MASK = at("MASK", [P, TT, PW], f32, TAIL + 8192)
        HTH = at("HTH", [P, FCH, S], f32r, EXT)
        HTL = at("HTL", [P, FCH, S], f32r, EXTB)
        UF = at("UF", [P, TT, PW], f32, EXT)
        DFTP = at("DFTP", [P, TT, 2 * S], f32, EXT + 4096)
        DFTC = at("DFTC", [P, 2, P], f32, EXT + 8192)
        FA = at("FA", [P, NS, 2 * S], f32, EXT + 9216)
        FG = at("FG", [P, AW], f32, EXT + 17408)
        STGB = at("STGB", [P, TT, PW], f32, EXTB + 2 * SLOT)
        PTB = at("PTB", [P, 4, P], f32, EXTB + 2 * SLOT + 4096)

        X = at("X", [P, TT, D], f32, REST0)
        XTH = at("XTH", [P, KC, S], f32r, REST0 + 8192)
        XTL = at("XTL", [P, KC, S], f32r, REST0 + 16384)
        MIXH = at("MIXH", [P, KC, S], f32r, REST0 + 8192)
        MIXL = at("MIXL", [P, KC, S], f32r, REST0 + 16384)
        M0 = REST0 + 24576
        MEMX = at("MEMX", [P, TT, D], f32, EXT)
        MTH = at("MTH", [P, KC, S], f32r, M0)
        MTL = at("MTL", [P, KC, S], f32r, M0 + 8192)
        PR = at("PR", [P, 2, TT, PW], f32, M0)
        LNG = at("LNG", [P, D], f32, M0)
        LNB = at("LNB", [P, D], f32, M0 + 4096)
        SIG = at("SIG", [P, TT, PW], f32, M0 + 8192)
        HB = at("HB", [P, TT, PW], f32, M0 + 12288)
        M1 = M0 + 16384
        QMT = at("QMT", [P, NS, S], f32, M1)
        KMT = [at("KMT0", [P, NS, S], f32, M1 + 4096), at("KMT1", [P, NS, S], f32, M1 + 8192)]
        VM = [at("VM0", [P, TT, PW], f32, M1 + 12288), at("VM1", [P, TT, PW], f32, M1 + 16384)]
        C0 = M1 + 20480
        IDN = at("IDN", [P, P], f32, C0)
        SM = at("SM", [P, 152], f32, C0 + 512)
        C1 = C0 + 512 + 608
        XG = at("XG", [P, TT, D], f32, REST0 + 8192)
        XEH = at("XEH", [P, KC, CAP], f32r, M0)
        XEL = at("XEL", [P, KC, CAP], f32r, M0 + 4096)
        ESIG = at("ESIG", [P, PW], f32, M0 + 8192)
        EH = at("EH", [P, PW], f32, M0 + 10240)
        EHTH = at("EHTH", [P, PW // P, CAP], f32r, M0 + 12288)
        EHTL = at("EHTL", [P, PW // P, CAP], f32r, M0 + 14336)
        YH = at("YH", [P, D], f32r, M1)
        YL = at("YL", [P, D], f32r, M1 + 4096)
        Y = at("Y", [P, D], f32, M1)
        CURS = at("CURS", [P, TT, CAP], f32r, M1 + 8192)
        CURT = at("CURT", [P, TT, P], f32r, M1 + 9216)
        IOT = at("IOT", [P, P], f32, C1)
        TRI = at("TRI", [P, 2 * P], f32, C1 + 512)
        RTH = at("RTH", [P, KC, S], f32r, REST0 + 16384)
        RTL = at("RTL", [P, KC, S], f32r, M0 + 8192)
        RW = at("RW", [P, KC, NE], f32, C1 + 1536)
        RWP = at("RWP", [P, KC, P], f32r, M1 + 4096)
        LT = at("LT", [2 * NE, S], f32, M1 + 8192)
        RB = at("RB", [P, NE], f32, C1 + 1792)
        RC = at("RC", [P, TT, NE, NE], f32, M1 + 1024)
        RC2 = at("RC2", [P, TT, NE, NE], f32, M1 + 1536)
        RC3 = at("RC3", [P, TT, NE, NE], f32, M1 + 2048)
        LOWM = at("LOWM", [P, NE, NE], f32, C1 + 1824)
        RS = at("RS", [P, 8, TT, NE], f32, M1 + 2816)
        POSC = at("POSC", [P, TT, 2, NE + 1], f32, M1 + 11776)
        CURC = at("CURC", [P, TT, 2], f32, M1 + 11936)
        CNT = at("CNT", [1, 8], f32, M1 + 11968)
        NP_ = at("NP_", [1, 8], i32, M1 + 12000)
        CG = at("CG", [P, 1], f32, M1 + 12064)
        EARLY = [at("EARLY0", [P, UNIT], f32, M1 + 12288), at("EARLY1", [P, UNIT], f32, REST0 + 16384)]
        LNG4 = at("LNG4", [P, D], f32, REST0 + 16384)
        LNB4 = at("LNB4", [P, D], f32, REST0 + 20480)
        MX, NMX, SUM, RSUM = SM[:, 0:2], SM[:, 2:4], SM[:, 4:6], SM[:, 6:8]
        MXB, NMXB, SUMB, RSUMB = SM[:, 8:10], SM[:, 10:12], SM[:, 12:14], SM[:, 14:16]
        BN = SM[:, 16:64].rearrange("p (t s) -> p t s", t=2)
        MV = SM[:, 64:68].rearrange("p (t s) -> p t s", t=2)
        VE, RSTD = SM[:, 68:70], SM[:, 70:72]
        FBN = SM[:, 72:120].rearrange("p (g s) -> p g s", g=8)
        FMV = SM[:, 120:136].rearrange("p (g s) -> p g s", g=8)
        FVE, FRS = SM[:, 136:144], SM[:, 144:152]

        PS = ctx.enter_context(nc.psum_tensor("PS", [P, 8, PW], f32))

        def sem(name):
            return ctx.enter_context(nc.semaphore(name))

        raw_in = [sem(f"raw_in{i}") for i in range(R)]
        early_in = [sem("early_in0"), sem("early_in1")]
        hi_done = sem("hi_done")
        lo_done = sem("lo_done")
        used = sem("used")
        mem_in = [sem("mem_in0"), sem("mem_in1")]
        x_in, idn_in, mask_in = sem("x_in"), sem("idn_in"), sem("mask_in")
        ln_in, b_in, r_in, ln4_in, out_done = sem("ln_in"), sem("b_in"), sem("r_in"), sem("ln4_in"), sem("out_done")
        tp_done = sem("tp_done")
        th_done = sem("th_done")
        tp_free = sem("tp_free")
        pan_free = sem("pan_free")
        sc_done, sc_free, mx_done, ex_done = sem("sc_done"), sem("sc_free"), sem("mx_done"), sem("ex_done")
        pn_done, ptp_done, pt_done = sem("pn_done"), sem("ptp_done"), sem("pt_done")
        o_done, oh_done, ol_done = sem("o_done"), sem("oh_done"), sem("ol_done")
        sum_done = sem("sum_done")
        var_done, sd_done, x_done = sem("var_done"), sem("sd_done"), sem("x_done")
        sig_done, gs_done, h_done = sem("sig_done"), sem("gs_done"), sem("h_done")
        fvar_done, fsd_done, un_done = sem("fvar_done"), sem("fsd_done"), sem("un_done")
        fa_done, fac_done = sem("fa_done"), sem("fac_done")
        xs_done, rw_done, lg_done = sem("xs_done"), sem("rw_done"), sem("lg_done")
        lt_done, ltt_done = sem("lt_done"), sem("ltt_done")
        le_done, ex8_done, pos_done, route_done = sem("le_done"), sem("ex8_done"), sem("pos_done"), sem("route_done")
        cur_col, cur_done, ct_done, ctt_done = sem("cur_col"), sem("cur_done"), sem("ct_done"), sem("ctt_done")
        gat_done, xeh_done, xel_done = sem("gat_done"), sem("xeh_done"), sem("xel_done")
        esig_done, egs_done, eh_done = sem("esig_done"), sem("egs_done"), sem("eh_done")
        et_done, eth_done, etl_done = sem("et_done"), sem("eth_done"), sem("etl_done")
        yh_done, yl_done, scat_done, acc_done = sem("yh_done"), sem("yl_done"), sem("scat_done"), sem("acc_done")
        fy_done, fscat_done = sem("fy_done"), sem("fscat_done")
        shift_done = sem("shift_done")
        v_chain = sem("v_chain")

        block = ctx.enter_context(nc.Block())

        def rows(w, k0, k1, c0, cn):
            return w[k0 * P:k1 * P, bass.ds(c0, cn)].rearrange("(c p) n -> p c n", p=P)

        def panel_units(w, c0):
            return [rows(w, 4 * h, 4 * h + 4, c0, PW) for h in range(PANEL)]

        def out_units(w):
            return [rows(w, 4 * h, 4 * h + 4, n * PW, PW) for h in range(2) for n in range(2)]

        dense_units = []
        for w in (t["a_w_mem_kv"], t["b_w_mem_kv"]):
            for n in range(2):
                dense_units += panel_units(w[0], n * PW)
        for n in range(PROJ):
            dense_units += panel_units(t["a_w_in"][0], n * PW)
        dense_units += out_units(t["a_w_out"][0])
        for n in range(FULL):
            dense_units += panel_units(t["a_ffn_gate"][0], n * PW) + panel_units(t["a_ffn_up"][0], n * PW)
        for w in (t["a_ffn_gate"], t["a_ffn_up"]):
            dense_units.append(rows(w[0], 0, KC, FULL * PW, REST))
        for n in range(FCH // 2):
            dense_units.append(rows(t["a_ffn_down"][0], 2 * n, 2 * n + 2, 0, D))
        for n in range(2):
            dense_units += panel_units(t["b_w_in"][0], n * PW)
        dense_units += out_units(t["b_w_out"][0])
        assert len(dense_units) == U_MOE

        def expert_unit(kind, e, p, h):
            if kind == "down":
                w = t["b_moe_down"][0, e, bass.ds(p * PW + h * 2 * P, 2 * P), :]
                return w.rearrange("(c p) n -> p c n", p=P)
            w = t["b_moe_gate" if kind == "gate" else "b_moe_up"]
            return w[0, e, 4 * h * P:(4 * h + 4) * P, bass.ds(p * PW, PW)].rearrange("(c p) n -> p c n", p=P)

        GATE_UP = [("gate", 0), ("gate", 1), ("up", 0), ("up", 1)]
        DOWN = [("down", 0), ("down", 1)]

        def slot_of(o):
            return (U_MOE + o) % R, (U_MOE + o) // R + 1

        EARLY_E = 1
        EARLY_U = EXP_U - 2
        GATHERS = 2 * NE

        def split_slot(o):
            return (o + RD) % R

        def lo_slot(s):
            return LOD[:, s] if s < RD else LOE[:, s - RD]

        F_MEM, F_X = 0, 4
        F_K = 8
        F_X1 = F_K + 2 * 9
        F_H = F_X1 + 4
        F_X2 = F_H + 2 * (FULL + 1)
        F_QB = F_X2 + 4
        F_X3 = F_QB + 2
        TH = {F_MEM: 0, F_X: 4, F_X1: 8, F_H: 12, F_X2: 12 + 2 * (FULL + 1), F_X3: 16 + 2 * (FULL + 1)}

        def fbank(f):
            return PS[:, 4 + f % 4]

        def fill_view(f, dst):
            c, w = dst.shape[1], dst.shape[2]
            return fbank(f)[:, 0:c * w].rearrange("p (c w) -> p c w", w=w)

        KPAN = {0: (0, KMT[0]), 2: (1, KMT[1])}
        for n in range(6):
            KPAN[4 + n] = (2 + n, QKT[:, NS * n:NS * n + NS])
        KPAN[13] = (8, QMT)
        PAN_B = PROJ + 4

        JOBS = [("slot", h, h) for h in range(NS)] + [("mem0", h, NS + h) for h in range(NS)]
        JOBS += [("mem1", h, NS + h) for h in range(NS)]
        JOBS_A, JOBS_B = range(0, 2 * NS), range(2 * NS, 3 * NS)

        def width(j):
            return PW if JOBS[j][0] == "slot" else S

        def blocks(j):
            out = [(tt, kt * P) for kt in range(TT) for tt in range(TT)]
            if JOBS[j][0] == "slot":
                out += [(tt, grp * P) for grp in (2, 3) for tt in range(TT)]
            return out

        def score_bank(j, tt):
            if j in JOBS_A:
                return PS[:, 2 * (j % 2) + tt, 0:width(j)]
            return PS[:, 4 + j % 2, tt * S:(tt + 1) * S]

        def scores_of(j):
            if j in JOBS_A:
                return PS[:, 2 * (j % 2):2 * (j % 2) + 2, 0:width(j)]
            return PS[:, 4 + j % 2].rearrange("p (t s) -> p t s", t=TT)

        def prob_blocks(j):
            if j in JOBS_A:
                return PS[:, 4:6].rearrange("p b n -> p (b n)")[:, 0:len(blocks(j)) * P]
            return PS[:, 6]

        def prob_sbuf(j):
            return (PT if j in JOBS_A else PTB)[:, 0:len(blocks(j)), :].rearrange("p b n -> p (b n)")

        O_FOURIER = 2 * NS

        def o_index(j):
            return j if j < O_FOURIER else j + NS

        def out_bank(i):
            if i < O_FOURIER:
                return PS[:, 6 + i % 2, 0:S]
            if i < O_FOURIER + NS:
                return PS[:, i - O_FOURIER, 0:S]
            return PS[:, 7, 0:S]

        def half_bank(half, tt):
            return half * 2 + tt

        @block.sync
        def _(sp):
            sp.dma_start(IDN[:, :], t["c_ident"]).then_inc(idn_in, 16)
            for u, src in enumerate(dense_units):
                if u == 1:
                    for tt in range(TT):
                        sp.dma_start(MEMX[:, tt, :], t["mem"][0].rearrange("(p t) d -> p t d", t=TT)[:, tt, :]
                                     ).then_inc(mem_in[tt], 16)
                elif u == 2:
                    sp.dma_start(X[:, :, :], t["x"][0].rearrange("(p t) d -> p t d", t=TT)).then_inc(x_in, 16)
                if u >= R:
                    sp.wait_ge(lo_done, u - R + 1)
                c = src.shape[1]
                sp.dma_start(RAW[:, u % R].rearrange("p (c n) -> p c n", c=c), src).then_inc(raw_in[u % R], 16)

            def load(ub, kind, e, p, h, o):
                sp.wait_ge(lo_done, ub + (o - R + 1))
                s, _turn = slot_of(o)
                c = 2 if kind == "down" else 4
                sp.dma_start(RAW[:, s].rearrange("p (c n) -> p c n", c=c),
                             expert_unit(kind, e, p, h)).then_inc(raw_in[s], 16)

            def early(h):
                src = expert_unit("down", EARLY_E, STEPS - 1, h)
                sp.dma_start(EARLY[h][:, :].rearrange("p (c n) -> p c n", c=2), src).then_inc(early_in[h], 16)

            def expert(q, e, starts_stream=False, tail_early=False):
                ub = q * PASS_U + e * EXP_U + U_MOE
                for i, (kind, h) in enumerate(GATE_UP):
                    load(ub, kind, e, 0, h, i)

                def panel(p, prev, up, early_buffers=False):
                    for i, (kind, h) in enumerate(GATE_UP):
                        load(up, kind, e, p, h, 4 + i)
                    load(up, "down", e, prev, 0, 8)
                    if early_buffers:
                        sp.wait_ge(o_done, 4 * NS)
                        early(0)
                    load(up, "down", e, prev, 1, 9)
                    if early_buffers:
                        sp.wait_ge(lg_done, 1)
                        early(1)

                first = 1
                if starts_stream:
                    panel(1, 0, ub, True)
                    first = 2
                with sp.Fori(first, STEPS) as p:
                    panel(p, p - 1, ub + (p - 1) * STEP_U)
                if not tail_early:
                    for i, (kind, h) in enumerate(DOWN):
                        load(ub, kind, e, STEPS - 1, h, EARLY_U + i)

            expert(0, 0, starts_stream=True)
            expert(0, EARLY_E, tail_early=True)
            with sp.Fori(EARLY_E + 1, NE) as e:
                expert(0, e)
            sp.wait_ge(route_done, 1)
            n_pass = sp.value_load(NP_[0:1, 0:1], min_val=1, max_val=2)
            with sp.If(n_pass > 1):
                with sp.Fori(0, NE) as e:
                    expert(1, e)
            sp.wait_ge(lo_done, U_MOE + (EARLY_E + 1) * EXP_U)
            sp.dma_start(LNG4[:, :], t["b_ln2_g"][0].partition_broadcast(P)).then_inc(ln4_in, 16)
            sp.dma_start(LNB4[:, :], t["b_ln2_b"][0].partition_broadcast(P)).then_inc(ln4_in, 16)
            for tt in range(TT):
                sp.wait_ge(x_done, 6 + tt + 1)
                sp.dma_start(t["out"][0].rearrange("(p t) d -> p t d", t=TT)[:, tt, :],
                             X[:, tt, :]).then_inc(out_done, 16)
            sp.wait_ge(out_done, 16 * TT)

        @block.gpsimd
        def _(gp):
            gp.wait_ge(used, 4)
            gp.dma_start(MASK[:, :, :], t["c_mask"]).then_inc(mask_in, 16)
            norms = [("a_ln1_g", "a_ln1_b", ol_done, 2 * NS),
                     ("a_ln2_g", "a_ln2_b", x_done, 2),
                     ("b_ln1_g", "b_ln1_b", ol_done, 4 * NS)]
            for k, (g, b, s, n) in enumerate(norms):
                gp.wait_ge(s, n)
                gp.dma_start(LNG[:, :], t[g][0].partition_broadcast(P)).then_inc(ln_in, 16)
                gp.dma_start(LNB[:, :], t[b][0].partition_broadcast(P)).then_inc(ln_in, 16)
                if k == 0:
                    gp.dma_start(RW[:, :, :], t["b_router_w"][0].rearrange("(c p) e -> p c e", p=P)).then_inc(r_in, 16)
                    gp.dma_start(RB[:, :], t["b_router_b"][0].partition_broadcast(P)).then_inc(r_in, 16)
                    gp.dma_start(LOWM[:, :, :], t["c_low"]).then_inc(r_in, 16)
                    gp.dma_start(IOT[:, :], t["c_iota"]).then_inc(r_in, 16)
                    gp.dma_start(TRI[:, :], t["c_tri"]).then_inc(r_in, 16)
                if k == 1:
                    gp.wait_ge(x_done, 4)
                    gp.dma_start(DFTP[:, :, :], t["c_dftp"]).then_inc(b_in, 16)
                    gp.dma_start(DFTC[:, :, :], t["c_dftc"]).then_inc(b_in, 16)
                    gp.dma_start(FG[:, :], t["b_fourier_g"][0].rearrange("g d -> (g d)").partition_broadcast(P)
                                 ).then_inc(b_in, 16)

        @block.scalar
        def _(act):
            def hi(u):
                act.wait_ge(raw_in[u % R], 16 * (u // R + 1))
                if u >= RD:
                    act.wait_ge(used, u - RD + 1)
                nc.scalar.activation(HI[:, u % RD], RAW[:, u % R], ACT.Copy).then_inc(hi_done, 1)

            def hi_fill(f, dst):
                act.wait_ge(tp_done, f + 1)
                nc.scalar.activation(dst, fill_view(f, dst), ACT.Copy).then_inc(th_done, 1)

            def hi_fills(f0, dst, js=range(2 * TT)):
                for j in js:
                    tt, k = divmod(j, 2)
                    hi_fill(f0 + j, dst[:, 4 * k:4 * k + 4, tt * P:(tt + 1) * P])

            def panel_out(n, dst, lo_bank):
                u = 2 * n if n < PAN_B else U_IN_B + 2 * (n - PAN_B)
                act.wait_ge(used, u + PANEL)
                if n in KPAN and KPAN[n][0] >= 2:
                    act.wait_ge(tp_done, F_K + 2 * (KPAN[n][0] - 1))
                nc.scalar.activation(dst, PS[:, lo_bank:lo_bank + 2], ACT.Copy).then_inc(pan_free, 1)

            def exps(j):
                act.wait_ge(mx_done, j + 1)
                b, w = j % 2, width(j)
                nmx, total = (NMX, SUM) if b == 0 else (NMXB, SUMB)
                for tt in range(TT):
                    nc.scalar.activation(PR[:, b, tt, 0:w], PR[:, b, tt, 0:w], ACT.Exp, bias=nmx[:, tt:tt + 1],
                                         scale=SCALE, accum_out=total[:, tt:tt + 1]).then_inc(ex_done, 1)

            def probs_t(j):
                act.wait_ge(ptp_done, j + 1)
                if j > 0:
                    act.wait_ge(o_done, o_index(j - 1) + 1)
                nc.scalar.activation(prob_sbuf(j), prob_blocks(j), ACT.Copy).then_inc(pt_done, 1)

            def job_hi(j):
                mix_hi(o_index(j), JOBS[j][2])

            def mix_hi(i, chunk):
                act.wait_ge(o_done, i + 1)
                nc.scalar.activation(MIXH[:, chunk, :], out_bank(i), ACT.Copy).then_inc(oh_done, 1)

            def deviation(k, tt):
                act.wait_ge(var_done, TT * k + tt + 1)
                nc.scalar.activation(RSTD[:, tt:tt + 1], VE[:, tt:tt + 1], ACT.Sqrt).then_inc(sd_done, 1)

            def hi_first(o):
                s, turn = slot_of(o)
                act.wait_ge(raw_in[s], turn * 16)
                nc.scalar.activation(HI[:, split_slot(o)], RAW[:, s], ACT.Copy).then_inc(hi_done, 1)

            hi(0)
            hi_fills(F_MEM, MTH)
            hi(1)
            hi(2)
            for n in range(PAN_B):
                hi(2 * n + 3)
                if n == PAN_B - 1:
                    exps(0)
                else:
                    hi(2 * n + 4)
                if n == 0:
                    hi_fills(F_X, XTH)
                if n in KPAN:
                    panel_out(n, STG[:, KPAN[n][0] % 2], 2 * (n % 2))
                elif n in (1, 3):
                    panel_out(n, VM[n // 2][:, :, :], 2 * (n % 2))
                else:
                    panel_out(n, V[:, :, (n - 10) * PW:(n - 9) * PW], 2 * (n % 2))
            hi(U_OUT_A + 2)
            for j in JOBS_A:
                probs_t(j)
                if j + 1 in JOBS_A:
                    exps(j + 1)
                job_hi(j)
                if j == JOBS_A[-2]:
                    hi(U_OUT_A + 3)
            hi(U_OUT_A + 4)
            deviation(0, 0)
            hi(U_OUT_A + 5)
            hi_fills(F_X1, XTH, range(0, 2))
            deviation(0, 1)
            hi(U_OUT_A + 6)
            hi_fills(F_X1, XTH, range(2, 4))
            def sigmoids(p, w):
                act.wait_ge(used, U_FFN + 4 * p + (2 if p < FULL else 1))
                if p > 0:
                    act.wait_ge(h_done, p)
                for tt in range(TT):
                    nc.scalar.activation(SIG[:, tt, 0:w], PS[:, tt, 0:w], ACT.Sigmoid).then_inc(sig_done, 1)

            def hidden_hi(p, c):
                for tt in range(TT):
                    hi_fill(F_H + 2 * p + tt, HTH[:, 4 * p:4 * p + c, tt * P:(tt + 1) * P])

            for p in range(FULL):
                for u in range(U_FFN + 4 * p + 3, U_FFN + 4 * p + 5):
                    hi(u)
                sigmoids(p, PW)
                if p > 0:
                    hidden_hi(p - 1, 4)
                for u in range(U_FFN + 4 * p + 5, U_FFN + 4 * p + 7):
                    hi(u)
            hi(U_FFN + 4 * FULL + 3)
            sigmoids(FULL, REST)
            hidden_hi(FULL - 1, 4)
            hi(U_FFN_DOWN + 2)
            hi(U_FFN_DOWN + 3)
            hidden_hi(FULL, 2)
            for u in range(U_FFN_DOWN + 4, U_IN_B + 1):
                hi(u)
            deviation(1, 0)
            hi(U_IN_B + 1)
            hi_fills(F_X2, XTH, range(0, 2))
            deviation(1, 1)
            hi(U_IN_B + 2)
            hi_fills(F_X2, XTH, range(2, 4))
            act.wait_ge(r_in, 80)
            act.wait_ge(rw_done, 1)
            nc.scalar.activation(RWP[:, :, 0:NE], RW[:, :, :], ACT.Copy).then_inc(rw_done, 1)
            hi(U_IN_B + 3)
            panel_out(PAN_B, UF[:, :, :], 0)
            hi(U_IN_B + 4)
            act.wait_ge(fvar_done, 1)
            nc.scalar.activation(FRS, FVE, ACT.Sqrt).then_inc(fsd_done, 1)
            hi(U_IN_B + 5)
            hi(U_IN_B + 6)
            panel_out(PAN_B + 1, STGB[:, :, :], 2)
            for g in range(NS):
                act.wait_ge(fa_done, g + 1)
                nc.scalar.activation(FA[:, g], PS[:, g], ACT.Copy).then_inc(fac_done, 1)
            b0 = JOBS_B[0]
            exps(b0)
            for g in range(NS):
                mix_hi(O_FOURIER + g, g)
            for j in JOBS_B:
                probs_t(j)
                if j + 1 in JOBS_B:
                    exps(j + 1)
                if j == b0 + 2:
                    hi_first(0)
                job_hi(j)
                if j == b0 + 1:
                    hi(U_MOE - 1)
            hi_first(1)
            hi_first(2)
            deviation(2, 0)
            act.wait_ge(used, U_MOE)
            hi_fills(F_X3, RTH, range(0, 2))
            deviation(2, 1)
            hi_fills(F_X3, RTH, range(2, 4))
            for o in (3, 4, 5):
                hi_first(o)
            act.wait_ge(le_done, 1)
            nc.scalar.activation(RS[:, 3], RS[:, 3], ACT.Exp).then_inc(ex8_done, 1)
            act.wait_ge(x_done, 6)
            nc.scalar.activation(X[:, :, :], XG[:, :, :], ACT.Copy, scale=ALPHA).then_inc(xs_done, 1)

            def hi_expert(ub, turns, o, all_turns=False):
                s, turn = slot_of(o)
                if not all_turns and o % R >= EARLY_U % R:
                    turn -= 1
                act.wait_ge(raw_in[s], (turns + turn) * 16)
                act.wait_ge(used, ub + (o - R + 1))
                nc.scalar.activation(HI[:, split_slot(o)], RAW[:, s], ACT.Copy).then_inc(hi_done, 1)

            def hi_early(h):
                act.wait_ge(early_in[h], 16)
                act.wait_ge(used, U_MOE + EARLY_E * EXP_U + EARLY_U + (h - R + 1))
                nc.scalar.activation(HI[:, split_slot(EARLY_U + h)], EARLY[h][:, :], ACT.Copy).then_inc(hi_done, 1)

            def gathered_hi(gb):
                for k in range(2):
                    act.wait_ge(gat_done, gb + k + 1)
                    nc.scalar.activation(XEH[:, 4 * k:4 * k + 4, :].rearrange("p c s -> p (c s)"), PS[:, 5 + k],
                                         ACT.Copy).then_inc(xeh_done, 1)

            def y_hi():
                for half in range(2):
                    nc.scalar.activation(YH[:, half * PW:(half + 1) * PW], PS[:, 2 + half], ACT.Copy,
                                         scale=CG[:, 0:1]).then_inc(yh_done, 1)

            def expert(q, e, back=None, all_turns=False, early=False, last_one=False):
                ub = q * PASS_U + e * EXP_U + U_MOE
                te = q * (PASS_U // R) + e * (EXP_U // R)
                st = q * NE * STEPS + e * STEPS

                def sigmoid(u, step, o):
                    act.wait_ge(used, u + (o + 1))
                    nc.scalar.activation(ESIG[:, :], PS[:, 0], ACT.Sigmoid).then_inc(esig_done, 1)

                def hidden_hi_e(step):
                    act.wait_ge(et_done, step + 1)
                    nc.scalar.activation(EHTH[:, :, :].rearrange("p c s -> p (c s)"), PS[:, 4],
                                         ACT.Copy).then_inc(eth_done, 1)

                if back is not None:
                    hi_expert(ub, te, 0, all_turns)
                    hi_expert(ub, te, 1, all_turns)
                    act.wait_ge(used, ub)
                    y_hi()
                    hi_expert(ub, te, 2, all_turns)
                    hi_expert(ub, te, 3, all_turns)
                    hi_expert(ub, te, 4, all_turns)
                if back is None:
                    hi_expert(ub, te, 6, all_turns)
                sigmoid(ub, st, 1)
                for o in ((7, 8) if back is None else (5, 6, 7, 8)):
                    hi_expert(ub, te, o, all_turns)
                hidden_hi_e(st)
                sigmoid(ub, st + 1, 5)
                act.wait_ge(ct_done, q * NE + e + 1)
                nc.scalar.activation(CURT[:, :, :].rearrange("p t s -> p (t s)"), PS[:, 5, 0:2 * P],
                                     ACT.Copy).then_inc(ctt_done, 1)
                nc.scalar.activation(CG[:, :], PS[:, 5, 2 * P:2 * P + 1], ACT.Copy).then_inc(ctt_done, 1)
                hi_expert(ub, te, 9, all_turns)
                with act.Fori(2, STEPS) as p:
                    up, tp = ub + (p - 1) * STEP_U, te + (p - 1)
                    for o in (4, 5, 6, 7, 8):
                        hi_expert(up, tp, o, all_turns)
                    hidden_hi_e(st + p - 1)
                    sigmoid(up, st + p, 5)
                    hi_expert(up, tp, 9, all_turns)
                for h in range(2):
                    if early:
                        hi_early(h)
                    else:
                        hi_expert(ub, te, EARLY_U + h, all_turns)
                hidden_hi_e(st + STEPS - 1)
                if not last_one:
                    gathered_hi(e * 2 + (q * GATHERS + 2))

            gathered_hi(0)
            expert(0, 0, all_turns=True)
            expert(0, EARLY_E, EARLY_E - 1, all_turns=True, early=True)
            with act.Fori(EARLY_E, NE - 2) as b:
                expert(0, b + 1, b)
            expert(0, NE - 1, NE - 2, last_one=True)
            act.wait_ge(route_done, 1)
            n_pass = act.value_load(NP_[0:1, 0:1], min_val=1, max_val=2)
            with act.If(n_pass > 1):
                gathered_hi(GATHERS)
                with act.Fori(0, NE) as e:
                    expert(1, e, e + (NE - 1))
            act.wait_ge(used, n_pass * PASS_U + U_MOE)
            act.wait_ge(ctt_done, n_pass * (2 * NE))
            for half in range(2):
                nc.scalar.activation(Y[:, half * PW:(half + 1) * PW], PS[:, 2 + half], ACT.Copy,
                                     scale=CG[:, 0:1]).then_inc(fy_done, 1)
            for tt in range(TT):
                deviation(3, tt)

        @block.vector
        def _(dve):
            chain = [0]

            def link(ins):
                mark(ins)
                settle()

            def mark(ins):
                chain[0] += 1
                ins.then_inc(v_chain, 1)

            def settle(n=None):
                dve.wait_ge(v_chain, chain[0] if n is None else n)

            def lo(u):
                dve.wait_ge(hi_done, u + 1)
                nc.vector.tensor_tensor(LOD[:, u % RD], RAW[:, u % R], HI[:, u % RD].bitcast(f32),
                                        ALU.subtract).then_inc(lo_done, 1)

            def lo_fills(f0, hi_t, lo_t, k0=0, c=4, n=2 * TT, js=None):
                for j in (range(n) if js is None else js):
                    tt, k = divmod(j, 2) if n == 2 * TT else (j, k0)
                    f = f0 + j
                    s0 = next(b for b in sorted(TH, reverse=True) if b <= f)
                    sl = (slice(None), slice(4 * k, 4 * k + c), slice(tt * P, (tt + 1) * P))
                    dve.wait_ge(th_done, TH[s0] + f - s0 + 1)
                    nc.vector.tensor_tensor(lo_t[sl], fill_view(f, lo_t[sl]), hi_t[sl].bitcast(f32),
                                            ALU.subtract).then_inc(tp_free, 1)

            def transposed_panel(f0, dst):
                for b in range(2):
                    dve.wait_ge(tp_done, f0 + b + 1)
                    d = dst[:, 2 * b:2 * b + 2, :]
                    nc.vector.tensor_copy(d, fill_view(f0 + b, d)).then_inc(tp_free, 1)

            def scores(j):
                kind, h, _ = JOBS[j]
                dst = PR[:, j % 2, :, 0:width(j)]
                dve.wait_ge(sc_done, j + 1)
                if j >= 2:
                    dve.wait_ge(ptp_done, j - 1)
                if kind == "slot":
                    if j == 0:
                        dve.wait_ge(mask_in, 16)
                    nc.vector.scalar_tensor_tensor(out=dst, in0=MASK[:, :, :], in1=scores_of(j),
                                                   scalar=2.0 ** (-(h + 1) * 8.0 / NH) / SCALE,
                                                   op0=ALU.mult, op1=ALU.add).then_inc(sc_free, 1)
                else:
                    nc.vector.tensor_copy(dst, scores_of(j)).then_inc(sc_free, 1)

            def maxima(j):
                mx, nmx = (MX, NMX) if j % 2 == 0 else (MXB, NMXB)
                dve.wait_ge(sc_free, j + 1)
                link(nc.vector.tensor_reduce(mx, PR[:, j % 2, :, 0:width(j)], AX.X, ALU.max))
                nc.vector.tensor_scalar(nmx, mx, -SCALE, None, ALU.mult).then_inc(mx_done, 1)

            def normalise(j):
                b, w = j % 2, width(j)
                total, r = (SUM, RSUM) if b == 0 else (SUMB, RSUMB)
                dve.wait_ge(ex_done, TT * (j + 1))
                link(nc.vector.reciprocal(r, total))
                for tt in range(TT):
                    nc.vector.tensor_scalar(PR[:, b, tt, 0:w], PR[:, b, tt, 0:w], r[:, tt:tt + 1], None,
                                            ALU.mult).then_inc(pn_done, 1)

            def job_lo(j):
                mix_lo(o_index(j), JOBS[j][2])

            def mix_lo(i, chunk):
                dve.wait_ge(oh_done, i + 1)
                nc.vector.tensor_tensor(MIXL[:, chunk, :], out_bank(i), MIXH[:, chunk, :].bitcast(f32),
                                        ALU.subtract).then_inc(ol_done, 1)

            def lo_first(o):
                dve.wait_ge(hi_done, U_MOE + o + 1)
                nc.vector.tensor_tensor(lo_slot(split_slot(o)), RAW[:, slot_of(o)[0]],
                                        HI[:, split_slot(o)].bitcast(f32), ALU.subtract).then_inc(lo_done, 1)

            def residual(k, tt, units):
                dve.wait_ge(*((sum_done, k + 1) if tt == 0 else (used, units)))
                for half in range(2):
                    x = X[:, tt, half * PW:(half + 1) * PW]
                    mark(nc.vector.scalar_tensor_tensor(out=x, in0=x, scalar=ALPHA, in1=PS[:, half_bank(half, tt)],
                                                        op0=ALU.mult, op1=ALU.add))

            def norm(k, tt, gain, bias, halves, dst):
                for half in range(2):
                    if k < 3:
                        settle(chain[0] - 1)
                    else:
                        dve.wait_ge(fscat_done, 2 * tt + half + 1)
                    mark(nc.vector.bn_stats(BN[:, tt, 6 * half:6 * half + 6], halves[half]))
                settle()
                link(nc.vector.bn_aggr(MV[:, tt, :], BN[:, tt, 0:12]))
                nc.vector.tensor_scalar(VE[:, tt:tt + 1], MV[:, tt, 1:2], EPS, None, ALU.add).then_inc(var_done, 1)
                dve.wait_ge(*((ln_in, 32 * (k + 1)) if k < 3 else (ln4_in, 32)))
                for half in range(2):
                    cols = slice(half * PW, (half + 1) * PW)
                    if k < 3 and half == 1:
                        continue
                    if k < 3:
                        cols, src = slice(0, D), X[:, tt, :]
                    else:
                        src = halves[half]
                    mark(nc.vector.scalar_tensor_tensor(out=X[:, tt, cols], in0=src, scalar=MV[:, tt, 0:1],
                                                        in1=gain[:, cols], op0=ALU.subtract, op1=ALU.mult))
                dve.wait_ge(sd_done, TT * k + tt + 1)
                link(nc.vector.reciprocal(RSTD[:, tt:tt + 1], RSTD[:, tt:tt + 1]))
                nc.vector.scalar_tensor_tensor(out=dst[:, tt, :], in0=X[:, tt, :], scalar=RSTD[:, tt:tt + 1],
                                               in1=bias[:, :], op0=ALU.mult, op1=ALU.add).then_inc(x_done, 1)

            def x_halves(tt):
                return [X[:, tt, half * PW:(half + 1) * PW] for half in range(2)]

            lo(0)
            lo_fills(F_MEM, MTH, MTL)
            lo(1)
            lo(2)
            for n in range(PAN_B):
                if n == PAN_B - 1:
                    scores(0)
                    maxima(0)
                    lo(2 * n + 3)
                else:
                    lo(2 * n + 3)
                    lo(2 * n + 4)
                if n == 0:
                    lo_fills(F_X, XTH, XTL)
                elif n - 1 in KPAN:
                    transposed_panel(F_K + 2 * KPAN[n - 1][0], KPAN[n - 1][1])
            normalise(0)
            transposed_panel(F_K + 2 * KPAN[PAN_B - 1][0], KPAN[PAN_B - 1][1])
            scores(1)
            maxima(1)
            for j in JOBS_A:
                if j + 1 in JOBS_A:
                    normalise(j + 1)
                if j + 2 in JOBS_A:
                    scores(j + 2)
                    maxima(j + 2)
                if j == 0:
                    lo(U_OUT_A + 2)
                elif j == JOBS_A[-1]:
                    lo(U_OUT_A + 3)
                job_lo(j)
            lo(U_OUT_A + 4)
            residual(0, 0, None)
            norm(0, 0, LNG, LNB, x_halves(0), X)
            residual(0, 1, U_OUT_A + 4)
            lo_fills(F_X1, XTH, XTL, js=range(0, 2))
            lo(U_OUT_A + 5)
            norm(0, 1, LNG, LNB, x_halves(1), X)
            lo_fills(F_X1, XTH, XTL, js=range(2, 4))

            def gated(p, w):
                dve.wait_ge(sig_done, TT * (p + 1))
                nc.vector.tensor_tensor(SIG[:, :, 0:w], PS[:, 0:2, 0:w], SIG[:, :, 0:w], ALU.mult).then_inc(gs_done, 1)

            def hidden(p, w):
                dve.wait_ge(used, U_FFN + 4 * p + (4 if p < FULL else 2))
                dve.wait_ge(gs_done, p + 1)
                if p > 0:
                    dve.wait_ge(tp_done, F_H + 2 * p)
                nc.vector.tensor_tensor(HB[:, :, 0:w], PS[:, 2:4, 0:w], SIG[:, :, 0:w], ALU.mult).then_inc(h_done, 1)

            def hidden_lo(p, c):
                lo_fills(F_H + 2 * p, HTH, HTL, k0=p, c=c, n=TT)

            lo(U_FFN + 2)
            for p in range(FULL):
                lo(U_FFN + 4 * p + 3)
                lo(U_FFN + 4 * p + 4)
                gated(p, PW)
                if p > 0:
                    hidden_lo(p - 1, 4)
                lo(U_FFN + 4 * p + 5)
                lo(U_FFN + 4 * p + 6)
                hidden(p, PW)
            lo(U_FFN_DOWN + 1)
            gated(FULL, REST)
            hidden_lo(FULL - 1, 4)
            hidden(FULL, REST)
            lo(U_FFN_DOWN + 2)
            lo(U_FFN_DOWN + 3)
            hidden_lo(FULL, 2)
            for u in range(U_FFN_DOWN + 4, U_IN_B + 1):
                lo(u)
            residual(1, 0, None)
            norm(1, 0, LNG, LNB, x_halves(0), X)
            residual(1, 1, U_IN_B)
            lo_fills(F_X2, XTH, XTL, js=range(0, 2))
            lo(U_IN_B + 1)
            norm(1, 1, LNG, LNB, x_halves(1), X)
            lo_fills(F_X2, XTH, XTL, js=range(2, 4))
            lo(U_IN_B + 2)
            nc.vector.memset(RWP[:, :, :].bitcast(f32), 0.0).then_inc(rw_done, 1)
            dve.wait_ge(rw_done, 2)
            nc.vector.tensor_tensor(RWP[:, :, NE:2 * NE], RW[:, :, :], RWP[:, :, 0:NE].bitcast(f32),
                                    ALU.subtract).then_inc(rw_done, 1)
            lo(U_IN_B + 3)
            uv = UF[:, :, :].rearrange("p t (g c) -> p (t g) c", c=HD)
            dve.wait_ge(pan_free, PAN_B + 1)
            for i in range(TT * NS):
                mark(nc.vector.bn_stats(FBN[:, i, :], uv[:, i, :]))
            settle()
            for i in range(TT * NS):
                mark(nc.vector.bn_aggr(FMV[:, i, :], FBN[:, i, :]))
            settle()
            nc.vector.tensor_scalar(FVE, FMV[:, :, 1], EPS, None, ALU.add).then_inc(fvar_done, 1)
            dve.wait_ge(fsd_done, 1)
            link(nc.vector.reciprocal(FRS, FRS))
            for i in range(TT * NS):
                mark(nc.vector.tensor_scalar(uv[:, i, :], uv[:, i, :], FMV[:, i, 0:1], FRS[:, i:i + 1],
                                             ALU.subtract, ALU.mult))
            dve.wait_ge(b_in, 48)
            settle()
            for tt in range(TT):
                nc.vector.tensor_tensor(UF[:, tt, :], UF[:, tt, :], FG[:, :], ALU.mult).then_inc(un_done, 1)
            for u in range(U_IN_B + 4, U_OUT_B + RD):
                lo(u)
            transposed_panel(F_QB, QMT)
            b0 = JOBS_B[0]
            scores(b0)
            maxima(b0)
            scores(b0 + 1)
            normalise(b0)
            maxima(b0 + 1)
            for g in range(NS):
                mix_lo(O_FOURIER + g, g)
            for j in JOBS_B:
                if j + 1 in JOBS_B:
                    normalise(j + 1)
                if j + 2 in JOBS_B:
                    scores(j + 2)
                    maxima(j + 2)
                if j == b0 + 2:
                    lo(U_MOE - 1)
                    lo_first(0)
                job_lo(j)
            lo_first(1)
            lo_first(2)
            residual(2, 0, None)
            norm(2, 0, LNG, LNB, x_halves(0), XG)
            residual(2, 1, U_MOE)
            norm(2, 1, LNG, LNB, x_halves(1), XG)

            lo_fills(F_X3, RTH, RTL)
            link(nc.vector.memset(POSC[:, :, 0, :], -1.0))
            nc.vector.memset(POSC[:, :, 1, :], 0.0).then_inc(acc_done, 4)
            dve.wait_ge(acc_done, 4)
            lo_first(3)
            logit, rank, sel, ex, top = (RS[:, i] for i in (0, 1, 2, 3, 4))
            dve.wait_ge(lg_done, 1)
            nc.vector.tensor_copy(LT[:, :], PS[0:2 * NE, 0, 0:S]).then_inc(lt_done, 1)
            dve.wait_ge(ltt_done, 1)
            parts = PS[:, 1, 0:TT * 2 * NE].rearrange("p (t e) -> p t e", t=TT)
            link(nc.vector.tensor_tensor(logit, parts[:, :, 0:NE], RB[:, :].unsqueeze(1).to_broadcast([P, TT, NE]),
                                         ALU.add))
            link(nc.vector.tensor_tensor(logit, parts[:, :, NE:2 * NE], logit, ALU.add))
            mark(nc.vector.tensor_reduce(top[:, :, 0], logit, AX.X, ALU.max))
            for tt in range(TT):
                this = logit[:, tt, :].unsqueeze(2).to_broadcast([P, NE, NE])
                other = logit[:, tt, :].unsqueeze(1).to_broadcast([P, NE, NE])
                mark(nc.vector.tensor_tensor(RC[:, tt], other, this, ALU.is_gt))
                mark(nc.vector.tensor_tensor(RC2[:, tt], other, this, ALU.is_equal))
            settle()
            mark(nc.vector.tensor_tensor(ex, logit, top[:, :, 0:1].to_broadcast([P, TT, NE]), ALU.subtract))
            for tt in range(TT):
                mark(nc.vector.tensor_tensor(RC3[:, tt], RC2[:, tt], LOWM[:, :, :], ALU.mult))
            settle()
            link(nc.vector.tensor_tensor(RC[:, :, :, :], RC[:, :, :, :], RC3[:, :, :, :], ALU.add))
            link(nc.vector.tensor_reduce(rank, RC[:, :, :, :], AX.X, ALU.add))
            nc.vector.tensor_scalar(sel, rank, 1.5, None, ALU.is_lt).then_inc(le_done, 1)
            dve.wait_ge(ex8_done, 1)
            dve.wait_ge(le_done, 1)
            link(nc.vector.tensor_tensor(ex, ex, sel, ALU.mult))
            link(nc.vector.tensor_reduce(top[:, :, 1], ex, AX.X, ALU.add))
            link(nc.vector.reciprocal(top[:, :, 2], top[:, :, 1]))
            mark(nc.vector.tensor_tensor(POSC[:, :, 1, 0:NE], ex, top[:, :, 2:3].to_broadcast([P, TT, NE]), ALU.mult))
            dve.wait_ge(pos_done, 1)
            link(nc.vector.scalar_tensor_tensor(out=rank, in0=PS[:, 2, 0:TT * NE].rearrange("p (t e) -> p t e", t=TT),
                                                scalar=1.0, in1=sel, op0=ALU.add, op1=ALU.mult))
            link(nc.vector.tensor_scalar(POSC[:, :, 0, 0:NE], rank, -1.0, None, ALU.add))
            link(nc.vector.tensor_reduce(CNT[0:1, 0:1], PS[0:1, 2, TT * NE:TT * NE + NE], AX.X, ALU.max))
            nc.vector.tensor_scalar(NP_[0:1, 0:1], CNT[0:1, 0:1], CAP + 0.5, 1.0, ALU.is_gt, ALU.add
                                    ).then_inc(route_done, 1)

            def slot_map(e, n):
                nc.vector.tensor_copy(CURC[:, :, :], POSC[:, :, :, bass.ds(e, 1)].rearrange("p t k o -> p t (k o)")
                                      ).then_inc(cur_col, 1)
                dve.wait_ge(cur_col, n + 1)
                for tt in range(TT):
                    nc.vector.tensor_scalar(CURS[:, tt, :], IOT[:, :], CURC[:, tt, 0:1], None,
                                            ALU.is_equal).then_inc(cur_done, 1)

            def lo_expert(ub, o):
                s, _turn = slot_of(o)
                dve.wait_ge(hi_done, ub + (o + 1))
                nc.vector.tensor_tensor(lo_slot(split_slot(o)), RAW[:, s], HI[:, split_slot(o)].bitcast(f32),
                                        ALU.subtract).then_inc(lo_done, 1)

            def lo_early(h):
                dve.wait_ge(hi_done, U_MOE + EARLY_E * EXP_U + EARLY_U + h + 1)
                s = split_slot(EARLY_U + h)
                nc.vector.tensor_tensor(lo_slot(s), EARLY[h][:, :], HI[:, s].bitcast(f32),
                                        ALU.subtract).then_inc(lo_done, 1)

            def gathered_lo(gb):
                for k in range(2):
                    chunks = slice(4 * k, 4 * k + 4)
                    dve.wait_ge(xeh_done, gb + (k + 1))
                    nc.vector.tensor_tensor(XEL[:, chunks, :].rearrange("p c s -> p (c s)"), PS[:, 5 + k],
                                            XEH[:, chunks, :].rearrange("p c s -> p (c s)").bitcast(f32),
                                            ALU.subtract).then_inc(xel_done, 1)

            def y_lo(n):
                for half in range(2):
                    cols = slice(half * PW, (half + 1) * PW)
                    dve.wait_ge(yh_done, n + (half + 1))
                    nc.vector.scalar_tensor_tensor(out=YL[:, cols], in0=PS[:, 2 + half], scalar=CG[:, 0:1],
                                                   in1=YH[:, cols].bitcast(f32), op0=ALU.mult,
                                                   op1=ALU.subtract).then_inc(yl_done, 1)

            def send_back(n):
                for i in range(4):
                    tt, half = divmod(i, 2)
                    x = X[:, tt, half * PW:(half + 1) * PW]
                    dve.wait_ge(scat_done, n + (i + 1))
                    nc.vector.tensor_tensor(x, x, PS[:, 4 + i], ALU.add).then_inc(acc_done, 1)

            def expert(q, e, back=None, early=False, last_one=False):
                ub = q * PASS_U + e * EXP_U + U_MOE
                st = q * NE * STEPS + e * STEPS
                tn = q * NE + e

                def gated_e(step):
                    dve.wait_ge(esig_done, step + 1)
                    nc.vector.tensor_tensor(ESIG[:, :], PS[:, 0], ESIG[:, :], ALU.mult).then_inc(egs_done, 1)

                def hidden_e(u, step, o):
                    dve.wait_ge(used, u + (o + 1))
                    dve.wait_ge(egs_done, step + 1)
                    nc.vector.tensor_tensor(EH[:, :], PS[:, 1], ESIG[:, :], ALU.mult).then_inc(eh_done, 1)

                def hidden_lo_e(step):
                    dve.wait_ge(eth_done, step + 1)
                    nc.vector.tensor_tensor(EHTL[:, :, :].rearrange("p c s -> p (c s)"), PS[:, 4],
                                            EHTH[:, :, :].rearrange("p c s -> p (c s)").bitcast(f32),
                                            ALU.subtract).then_inc(etl_done, 1)

                if back is not None:
                    lo_expert(ub, 0)
                    lo_expert(ub, 1)
                    y_lo(back * 2)
                    lo_expert(ub, 2)
                    lo_expert(ub, 3)
                    lo_expert(ub, 4)
                if back is None:
                    lo_expert(ub, 6)
                    gated_e(st)
                else:
                    gated_e(st)
                    lo_expert(ub, 5)
                    send_back(back * 4)
                    lo_expert(ub, 6)
                hidden_e(ub, st, 3)
                lo_expert(ub, 7)
                lo_expert(ub, 8)
                hidden_lo_e(st)
                gated_e(st + 1)
                dve.wait_ge(ct_done, tn + 1)
                slot_map(e + 1, tn + (q + 1))
                lo_expert(ub, 9)
                with dve.Fori(2, STEPS) as p:
                    up = ub + (p - 1) * STEP_U
                    lo_expert(up, 4)
                    hidden_e(up, st + p - 1, 4 - STEP_U + 3)
                    for o in (5, 6, 7, 8):
                        lo_expert(up, o)
                    hidden_lo_e(st + p - 1)
                    gated_e(st + p)
                    lo_expert(up, 9)
                if early:
                    lo_early(0)
                else:
                    lo_expert(ub, EARLY_U)
                hidden_e(ub, st + STEPS - 1, EXP_U - 5)
                if last_one:
                    hidden_lo_e(st + STEPS - 1)
                if early:
                    lo_early(1)
                else:
                    lo_expert(ub, EARLY_U + 1)
                if not last_one:
                    hidden_lo_e(st + STEPS - 1)
                if not last_one:
                    gathered_lo(e * 2 + (q * GATHERS + 2))

            slot_map(0, 0)
            lo_first(4)
            gathered_lo(0)
            lo_first(5)
            dve.wait_ge(xs_done, 1)
            expert(0, 0)
            expert(0, EARLY_E, EARLY_E - 1, early=True)
            with dve.Fori(EARLY_E, NE - 2) as b:
                expert(0, b + 1, b)
            expert(0, NE - 1, NE - 2, last_one=True)
            dve.wait_ge(route_done, 1)
            n_pass = dve.value_load(NP_[0:1, 0:1], min_val=1, max_val=2)
            with dve.If(n_pass > 1):
                dve.wait_ge(gat_done, GATHERS)
                nc.vector.tensor_scalar(POSC[:, :, 0, :], POSC[:, :, 0, :], -float(CAP), None,
                                        ALU.add).then_inc(shift_done, 1)
                dve.wait_ge(shift_done, 1)
                slot_map(0, NE + 1)
                gathered_lo(GATHERS)
                with dve.Fori(0, NE) as e:
                    expert(1, e, e + (NE - 1))
            for tt in range(TT):
                norm(3, tt, LNG4, LNB4, [PS[:, 4 + 2 * tt + half] for half in range(2)], X)

        @block.tensor
        def _(pe):
            def three(out, xh, xl, wh, wl, first, last):
                nc.tensor.matmul(out, xh, wh, start=first, stop=False)
                nc.tensor.matmul(out, xh, wl, start=False, stop=False)
                return nc.tensor.matmul(out, xl, wh, start=False, stop=last)

            def fills(f0, src, n=2 * TT):
                for j in range(n):
                    tt, k = divmod(j, 2)
                    fill(f0 + j, [src[:, tt, (4 * k + i) * P:(4 * k + i + 1) * P] for i in range(4)])

            def fill(f, blocks):
                if f >= 4:
                    pe.wait_ge(tp_free, f - 3)
                for i, blk in enumerate(blocks):
                    last = nc.tensor.transpose(fbank(f)[:, i * P:(i + 1) * P], blk, IDN[:, :])
                last.then_inc(tp_done, 1)

            def panel_fills(f0, stg):
                for b in range(2):
                    fill(f0 + b, [stg[:, tt, h * HD:(h + 1) * HD] for h in (2 * b, 2 * b + 1) for tt in range(TT)])

            def unit(u, xh, xl, k0, c, banks, first, last):
                w = UNIT // c
                n = w // len(banks)
                wh = HI[:, u % RD].rearrange("p (c n) -> p c n", c=c)
                wl = LOD[:, u % RD].rearrange("p (c n) -> p c n", c=c)
                pe.wait_ge(lo_done, u + 1)
                for i in range(c):
                    for half in range(len(banks)):
                        for tt in range(TT):
                            tok, col = slice(tt * P, (tt + 1) * P), slice(half * n, (half + 1) * n)
                            ins = three(PS[:, banks[half] + tt, 0:n], xh[:, k0 + i, tok], xl[:, k0 + i, tok],
                                        wh[:, i, col], wl[:, i, col], first and i == 0, last and i == c - 1)
                ins.then_inc(used, 1)

            def tile_fills(f0, src, n_norm, tt):
                pe.wait_ge(x_done, TT * n_norm + tt + 1)
                for k in range(2):
                    fill(f0 + 2 * tt + k, [src[:, tt, (4 * k + i) * P:(4 * k + i + 1) * P] for i in range(4)])

            def first_panel(u, f0, n_norm, bank):
                for tt in range(TT):
                    tile_fills(f0, X, n_norm, tt)
                    tok = slice(tt * P, (tt + 1) * P)
                    for c in range(KC):
                        h, i = divmod(c, 4)
                        if i == 0:
                            pe.wait_ge(tp_free, f0 + 2 * tt + h + 1)
                        if tt == 0 and i == 0:
                            pe.wait_ge(lo_done, u + h + 1)
                        wh = HI[:, (u + h) % RD].rearrange("p (c n) -> p c n", c=4)[:, i, :]
                        wl = LOD[:, (u + h) % RD].rearrange("p (c n) -> p c n", c=4)[:, i, :]
                        ins = three(PS[:, bank + tt], XTH[:, c, tok], XTL[:, c, tok], wh, wl, c == 0, c == KC - 1)
                        if tt == TT - 1 and i == 3:
                            ins.then_inc(used, 1)

            def last_pair(u, xh, xl, k0s, c, banks):
                w = UNIT // c
                pe.wait_ge(lo_done, u + 2)
                for tt in range(TT):
                    tok = slice(tt * P, (tt + 1) * P)
                    for h in range(2):
                        n = w // len(banks[h])
                        wh = HI[:, (u + h) % RD].rearrange("p (c n) -> p c n", c=c)
                        wl = LOD[:, (u + h) % RD].rearrange("p (c n) -> p c n", c=c)
                        for i in range(c):
                            for half, bank in enumerate(banks[h]):
                                last = i == c - 1 and (h == 1 or banks[0] != banks[1])
                                ins = three(PS[:, bank + tt, 0:n], xh[:, k0s[h] + i, tok], xl[:, k0s[h] + i, tok],
                                            wh[:, i, half * n:(half + 1) * n], wl[:, i, half * n:(half + 1) * n],
                                            False, last)
                        if tt == TT - 1:
                            ins.then_inc(used, 1)
                    if tt == 0:
                        ins.then_inc(sum_done, 1)

            def panel(u, xh, xl, bank):
                unit(u, xh, xl, 0, 4, (bank,), True, False)
                unit(u + 1, xh, xl, 4, 4, (bank,), False, True)

            def scores(j):
                kind, h, _ = JOBS[j]
                if j >= 2:
                    pe.wait_ge(sc_free, j - 1)
                for tt in range(TT):
                    out, tok = score_bank(j, tt), slice(tt * P, (tt + 1) * P)
                    if kind == "slot":
                        nc.tensor.matmul(out[:, 0:S], QKT[:, h, tok], QKT[:, NH + h, :], start=True, stop=True)
                        for grp in (1, 2):
                            last = nc.tensor.matmul(out[:, (grp + 1) * P:(grp + 2) * P], QKT[:, grp * NS + h, tok],
                                                    QKT[:, NH + grp * NS + h, tok], start=True, stop=True)
                    else:
                        last = nc.tensor.matmul(out, QMT[:, h, tok], KMT[0 if kind == "mem0" else 1][:, h, :],
                                                start=True, stop=True)
                last.then_inc(sc_done, 1)

            def probs_t(j):
                pe.wait_ge(pn_done, TT * (j + 1))
                if j > 0:
                    pe.wait_ge(pt_done, j)
                for b, (tt, col) in enumerate(blocks(j)):
                    last = nc.tensor.transpose(prob_blocks(j)[:, b * P:(b + 1) * P], PR[:, j % 2, tt, col:col + P],
                                               IDN[:, :])
                last.then_inc(ptp_done, 1)

            def values(j):
                kind, h, _ = JOBS[j]
                i = o_index(j)
                pe.wait_ge(pt_done, j + 1)
                if j in JOBS_A and j >= 2:
                    pe.wait_ge(ol_done, i - 1)
                elif j in JOBS_B and j > JOBS_B[0]:
                    pe.wait_ge(ol_done, i)
                out, probs, cols = out_bank(i), prob_sbuf(j), slice(h * HD, (h + 1) * HD)
                for kt in range(TT):
                    v = V[:, kt, cols] if kind == "slot" else VM[0 if kind == "mem0" else 1][:, kt, cols]
                    last = nc.tensor.matmul(out, v, probs[:, kt * S:(kt + 1) * S], start=(kt == 0),
                                            stop=(kind != "slot" and kt == TT - 1))
                if kind == "slot":
                    for grp in (1, 2):
                        for tt in range(TT):
                            b = 2 * (grp + 1) + tt
                            v = V[:, tt, grp * AW + h * HD:grp * AW + (h + 1) * HD]
                            last = nc.tensor.matmul(out[:, tt * P:(tt + 1) * P], v, probs[:, b * P:(b + 1) * P],
                                                    start=False, stop=(grp == 2 and tt == TT - 1))
                last.then_inc(o_done, 1)

            def out_unit(u0, k):
                unit(u0 + k, MIXH, MIXL, 4 * (k // 2), 4, (2 * (k % 2),), k < 2, k >= 2)

            pe.wait_ge(idn_in, 16)
            for tt in range(TT):
                pe.wait_ge(mem_in[tt], 16)
                for k in range(2):
                    fill(F_MEM + 2 * tt + k, [MEMX[:, tt, (4 * k + i) * P:(4 * k + i + 1) * P] for i in range(4)])
            for n in range(PAN_B):
                if n >= 2:
                    pe.wait_ge(pan_free, n - 1)
                if n == 4:
                    pe.wait_ge(tp_free, F_X + 4)
                if n == 0:
                    pe.wait_ge(lo_done, 1)
                    for tt in range(TT):
                        pe.wait_ge(tp_free, F_MEM + 2 * tt + 1)
                        tok = slice(tt * P, (tt + 1) * P)
                        for i in range(4):
                            last = three(PS[:, tt], MTH[:, i, tok], MTL[:, i, tok], HI[:, 0, i * PW:(i + 1) * PW],
                                         LOD[:, 0, i * PW:(i + 1) * PW], i == 0, False)
                    last.then_inc(used, 1)
                    pe.wait_ge(tp_free, F_MEM + 4)
                    unit(1, MTH, MTL, 4, 4, (0,), False, True)
                elif n < PAN_B - 1:
                    panel(2 * n, MTH if n < 4 else XTH, MTL if n < 4 else XTL, 2 * (n % 2))
                else:
                    unit(2 * n, XTH, XTL, 0, 4, (2,), True, False)
                    pe.wait_ge(tp_free, F_K + 2 * 8)
                    pe.wait_ge(pan_free, n)
                    scores(0)
                    unit(2 * n + 1, XTH, XTL, 4, 4, (2,), False, True)
                if n == 0:
                    pe.wait_ge(x_in, 16)
                    fills(F_X, X)
                if n - 1 in KPAN:
                    k = KPAN[n - 1][0]
                    pe.wait_ge(pan_free, n)
                    panel_fills(F_K + 2 * k, STG[:, k % 2])
            pe.wait_ge(pan_free, PAN_B)
            panel_fills(F_K + 2 * KPAN[PAN_B - 1][0], STG[:, KPAN[PAN_B - 1][0] % 2])
            scores(1)
            pe.wait_ge(tp_free, F_K + 2 * 9)
            for j in JOBS_A:
                probs_t(j)
                if j == JOBS_A[-2]:
                    pe.wait_ge(ol_done, NS)
                    pe.wait_ge(sc_free, 2 * NS)
                    out_unit(U_OUT_A, 0)
                elif j == JOBS_A[-1]:
                    out_unit(U_OUT_A, 1)
                if j + 2 in JOBS_A:
                    scores(j + 2)
                values(j)
            pe.wait_ge(ol_done, 2 * NS)
            last_pair(U_OUT_A + 2, MIXH, MIXL, (4, 4), 4, ((0,), (2,)))

            def hidden_fills(p, c):
                pe.wait_ge(h_done, p + 1)
                for tt in range(TT):
                    fill(F_H + 2 * p + tt, [HB[:, tt, i * P:(i + 1) * P] for i in range(c)])

            for p in range(FULL):
                if p > 0:
                    pe.wait_ge(gs_done, p)
                    panel(U_FFN + 4 * p, XTH, XTL, 0)
                else:
                    first_panel(U_FFN, F_X1, 0, 0)
                if p > 0:
                    hidden_fills(p - 1, 4)
                panel(U_FFN + 4 * p + 2, XTH, XTL, 2)
            pe.wait_ge(gs_done, FULL)
            unit(U_FFN + 4 * FULL, XTH, XTL, 0, KC, (0,), True, True)
            hidden_fills(FULL - 1, 4)
            unit(U_FFN + 4 * FULL + 1, XTH, XTL, 0, KC, (2,), True, True)
            pe.wait_ge(h_done, FULL + 1)
            down = FCH // 2
            for i in range(down - 2):
                if i == 1:
                    hidden_fills(FULL, 2)
                if i == 2:
                    pe.wait_ge(tp_free, F_H + 2 * FULL)
                unit(U_FFN_DOWN + i, HTH, HTL, 2 * i, 2, (0, 2), i == 0, False)
            pe.wait_ge(tp_free, F_H + 2 * FULL + 2)
            last_pair(U_IN_B - 2, HTH, HTL, (FCH - 4, FCH - 2), 2, ((0, 2), (0, 2)))
            first_panel(U_IN_B, F_X2, 1, 0)
            panel(U_IN_B + 2, XTH, XTL, 2)
            pe.wait_ge(un_done, TT)
            for g in range(NS):
                if g == 2:
                    pe.wait_ge(pan_free, PAN_B + 2)
                    panel_fills(F_QB, STGB)
                for tt in range(TT):
                    last = nc.tensor.matmul(PS[:, g], UF[:, tt, g * HD:(g + 1) * HD], DFTP[:, tt, :],
                                            start=(tt == 0), stop=(tt == TT - 1))
                last.then_inc(fa_done, 1)
            pe.wait_ge(tp_free, F_QB + 2)
            b0 = JOBS_B[0]
            scores(b0)
            scores(b0 + 1)
            for g in range(NS):
                pe.wait_ge(fac_done, g + 1)
                for half in range(2):
                    last = nc.tensor.matmul(out_bank(O_FOURIER + g), DFTC[:, half, :],
                                            FA[:, g, half * S:(half + 1) * S], start=(half == 0), stop=(half == 1))
                last.then_inc(o_done, 1)
            for j in JOBS_B:
                if j == b0 + 1:
                    pe.wait_ge(ol_done, O_FOURIER + NS)
                    out_unit(U_OUT_B, 0)
                probs_t(j)
                if j == b0 + 2:
                    out_unit(U_OUT_B, 1)
                if j + 2 in JOBS_B:
                    scores(j + 2)
                values(j)
            pe.wait_ge(ol_done, 4 * NS)
            last_pair(U_OUT_B + 2, MIXH, MIXL, (4, 4), 4, ((0,), (2,)))
            for tt in range(TT):
                tile_fills(F_X3, XG, 2, tt)
            pe.wait_ge(rw_done, 3)
            pe.wait_ge(tp_free, F_X3 + 4)
            for c in range(KC):
                nc.tensor.matmul(PS[:, 0, 0:S], RWP[:, c, :], RTH[:, c, :], start=(c == 0), stop=False)
                last = nc.tensor.matmul(PS[:, 0, 0:S], RWP[:, c, :], RTL[:, c, :], start=False, stop=(c == KC - 1))
            last.then_inc(lg_done, 1)
            pe.wait_ge(lt_done, 1)
            for tt in range(TT):
                last = nc.tensor.transpose(PS[:, 1, tt * 2 * NE:(tt + 1) * 2 * NE], LT[:, tt * P:(tt + 1) * P],
                                           IDN[0:2 * NE, 0:2 * NE])
            last.then_inc(ltt_done, 1)
            pe.wait_ge(le_done, 1)
            sel = RS[:, 2]
            ones, tri = TRI[:, P:2 * P], TRI[:, 0:P]
            nc.tensor.matmul(PS[:, 2, 0:NE], tri, sel[:, 0, :], start=True, stop=True)
            nc.tensor.matmul(PS[:, 2, NE:2 * NE], ones, sel[:, 0, :], start=True, stop=False)
            nc.tensor.matmul(PS[:, 2, NE:2 * NE], tri, sel[:, 1, :], start=False, stop=True)
            nc.tensor.matmul(PS[0:1, 2, 2 * NE:3 * NE], ones[:, 0:1], sel[:, 0, :], start=True, stop=False)
            nc.tensor.matmul(PS[0:1, 2, 2 * NE:3 * NE], ones[:, 0:1], sel[:, 1, :], start=False,
                             stop=True).then_inc(pos_done, 1)
            pe.wait_ge(route_done, 1)

            def gather(cur):
                pe.wait_ge(cur_done, cur)
                for c in range(KC):
                    for tt in range(TT):
                        last = nc.tensor.matmul(PS[:, 5 + c // 4, (c % 4) * P:(c % 4 + 1) * P],
                                                XG[:, tt, c * P:(c + 1) * P], CURS[:, tt, :].bitcast(f32),
                                                start=(tt == 0), stop=(tt == TT - 1))
                    if c % 4 == 3:
                        last.then_inc(gat_done, 1)

            def scatter():
                for i in range(4):
                    tt, half = divmod(i, 2)
                    cols = slice(half * PW, (half + 1) * PW)
                    nc.tensor.matmul(PS[:, 4 + i], CURT[:, tt, :], YH[:, cols], start=True, stop=False)
                    nc.tensor.matmul(PS[:, 4 + i], CURT[:, tt, :], YL[:, cols], start=False, stop=True
                                     ).then_inc(scat_done, 1)

            def expert_in(ub, o, k0, bank):
                s = split_slot(o)
                wh = HI[:, s].rearrange("p (c n) -> p c n", c=4)
                wl = lo_slot(s).rearrange("p (c n) -> p c n", c=4)
                pe.wait_ge(lo_done, ub + (o + 1))
                for i in range(4):
                    last = three(PS[:, bank], XEH[:, k0 + i, :], XEL[:, k0 + i, :], wh[:, i, :], wl[:, i, :],
                                 k0 + i == 0, k0 + i == KC - 1)
                last.then_inc(used, 1)

            def expert_down(ub, o, first, last_panel):
                for h in range(2):
                    s = split_slot(o + h)
                    wh = HI[:, s].rearrange("p (c n) -> p c n", c=2)
                    wl = lo_slot(s).rearrange("p (c n) -> p c n", c=2)
                    pe.wait_ge(lo_done, ub + (o + h + 1))
                    for i in range(2):
                        for half in range(2):
                            cols = slice(half * PW, (half + 1) * PW)
                            last = three(PS[:, 2 + half], EHTH[:, 2 * h + i, :], EHTL[:, 2 * h + i, :],
                                         wh[:, i, cols], wl[:, i, cols], first and h == 0 and i == 0,
                                         last_panel and h == 1 and i == 1)
                    last.then_inc(used, 1)

            def hidden_t(step):
                pe.wait_ge(eh_done, step + 1)
                for i in range(PW // P):
                    last = nc.tensor.transpose(PS[:, 4, i * P:(i + 1) * P], EH[:, i * P:(i + 1) * P], IDN[:, :])
                last.then_inc(et_done, 1)

            def expert(q, e, back=None, last_one=False):
                ub = q * PASS_U + e * EXP_U + U_MOE
                st = q * NE * STEPS + e * STEPS
                tn = q * NE + e
                gn = e * 2 + (q * GATHERS + 1)
                pe.wait_ge(xel_done, gn)
                expert_in(ub, 0, 0, 0)
                pe.wait_ge(xel_done, gn + 1)
                expert_in(ub, 1, 4, 0)
                expert_in(ub, 2, 0, 1)
                expert_in(ub, 3, 4, 1)
                if back is not None:
                    pe.wait_ge(yl_done, back * 2 + 2)
                    scatter()
                pe.wait_ge(egs_done, st + 1)
                expert_in(ub, 4, 0, 0)
                expert_in(ub, 5, 4, 0)
                if back is not None:
                    pe.wait_ge(acc_done, back * 4 + 8)
                hidden_t(st)
                pe.wait_ge(cur_done, (tn + (q + 1)) * TT)
                for tt in range(TT):
                    nc.tensor.transpose(PS[:, 5, tt * P:(tt + 1) * P], CURS[:, tt, :].bitcast(f32), IDN[:, :])
                for tt in range(TT):
                    last = nc.tensor.matmul(PS[:, 5, TT * P:TT * P + 1], CURS[:, tt, :].bitcast(f32),
                                            CURC[:, tt, 1:2], start=(tt == 0), stop=(tt == TT - 1))
                last.then_inc(ct_done, 1)
                expert_in(ub, 6, 0, 1)
                expert_in(ub, 7, 4, 1)
                pe.wait_ge(etl_done, st + 1)
                expert_down(ub, 8, True, False)
                with pe.Fori(2, STEPS) as p:
                    up = ub + (p - 1) * STEP_U
                    pe.wait_ge(egs_done, st + p)
                    expert_in(up, 4, 0, 0)
                    expert_in(up, 5, 4, 0)
                    hidden_t(st + p - 1)
                    expert_in(up, 6, 0, 1)
                    expert_in(up, 7, 4, 1)
                    pe.wait_ge(etl_done, st + p)
                    expert_down(up, 8, False, False)
                hidden_t(st + STEPS - 1)
                if not last_one:
                    gather((tn + (q + 2)) * TT)
                pe.wait_ge(etl_done, st + STEPS)
                expert_down(ub, EXP_U - 2, False, True)

            gather(TT)
            expert(0, 0)
            with pe.Fori(0, NE - 2) as b:
                expert(0, b + 1, b)
            expert(0, NE - 1, NE - 2, last_one=True)
            n_pass = pe.value_load(NP_[0:1, 0:1], min_val=1, max_val=2)
            with pe.If(n_pass > 1):
                pe.wait_ge(xeh_done, GATHERS)
                pe.wait_ge(xel_done, GATHERS)
                gather((NE + 2) * TT)
                with pe.Fori(0, NE) as e:
                    expert(1, e, e + (NE - 1))
                pe.wait_ge(xel_done, 2 * GATHERS + 2)
            pe.wait_ge(acc_done, n_pass * (4 * NE))
            for i in range(4):
                tt, half = divmod(i, 2)
                cols = slice(half * PW, (half + 1) * PW)
                nc.tensor.matmul(PS[:, 4 + i], IDN[:, :], X[:, tt, cols], start=True, stop=False)
                if tt == 0:
                    pe.wait_ge(fy_done, half + 1)
                nc.tensor.matmul(PS[:, 4 + i], CURT[:, tt, :].bitcast(f32), Y[:, cols], start=False,
                                 stop=True).then_inc(fscat_done, 1)


def _constants(shapes):
    import numpy as np
    s, p = shapes["x"][1], 128
    hd, tiles = shapes["x"][2] // 8, shapes["x"][1] // 128
    pos = np.arange(s)
    gap = np.abs(pos[:, None] - pos[None, :])
    order = pos.reshape(p, tiles).T
    mask = np.full((p, tiles, 4 * p), -1e30, np.float32)
    for g, (window, dilation) in enumerate(((128, 1), (512, 4), (2048, 16))):
        seen = (gap % dilation == 0) & (gap <= window // 2)
        m = np.where(seen, -gap * 2.0 ** (-8.0 * g / 3), -1e30)
        for tt in range(tiles):
            keys = order.reshape(-1) if g == 0 else order[tt]
            first = 0 if g == 0 else (g + 1) * p
            mask[:, tt, first:first + len(keys)] = m[np.ix_(order[tt], keys)]
    ang = 2 * np.pi * (np.outer(pos, pos) % s) / s
    ang = ang[np.ix_(order.reshape(-1), order.reshape(-1))]
    both = np.concatenate([np.cos(ang), np.sin(ang)], 1).astype(np.float32)
    ch = np.arange(hd)
    cang = 2 * np.pi * (np.outer(ch, ch) % hd) / hd
    norm = 1.0 / np.sqrt(s * hd)
    dftc = np.stack([np.cos(cang) * norm, -np.sin(cang) * norm], 1).astype(np.float32)
    idx = np.arange(p)
    tri = (idx[:, None] < idx[None, :]).astype(np.float32)
    e = np.arange(8)
    low = np.broadcast_to((e[None, :] < e[:, None]).astype(np.float32), (p, 8, 8))
    return {
        "c_ident": np.eye(p, dtype=np.float32),
        "c_mask": mask,
        "c_dftp": np.ascontiguousarray(both.reshape(tiles, p, 2 * s).transpose(1, 0, 2)),
        "c_dftc": dftc,
        "c_iota": np.ascontiguousarray(np.broadcast_to(idx.astype(np.float32), (p, p))),
        "c_tri": np.concatenate([tri, np.ones((p, p), np.float32)], 1),
        "c_low": np.ascontiguousarray(low),
    }


def kernel(**inputs):
    import numpy as np
    import concourse.bacc as bacc
    from concourse.bass_utils import run_bass_kernel_spmd

    nc = bacc.Bacc("TRN2", target_bir_lowering=False, num_devices=1)
    given = {n: np.ascontiguousarray(a) for n, a in inputs.items()}
    given.update(_constants({n: a.shape for n, a in given.items()}))
    arrays, tensors = {}, {}
    for name, a in given.items():
        arrays[f"in_{name}"] = a
        tensors[name] = nc.dram_tensor(f"in_{name}", a.shape, mybir.dt.from_np(a.dtype), kind="ExternalInput").ap()
    tensors["out"] = nc.dram_tensor("out_0", given["x"].shape, mybir.dt.float32, kind="ExternalOutput").ap()
    hybrid_encoder(nc, tensors)
    r = run_bass_kernel_spmd(nc, [arrays], core_ids=[0])
    return r.results[0]["out_0"]
```
